# Optimizing a Trainium2 kernel written in Bass

```python
import math
import jax
import jax.numpy as jnp
from jax import lax
import numpy as np
import jax, jax.numpy as jnp

D_MODEL = 1024
BATCH = 1
SEQ = 512
DEPTH = 1

GLA_HEADS = 4
GLA_DK = 128
GLA_DV = 256
GLA_GATE_RANK = 16
GLA_TAU = 16.0
GLA_CHUNK = 64
NSA_HEADS = 8
NSA_GROUPS = 2
NSA_REP = NSA_HEADS // NSA_GROUPS
NSA_DH = 64
NSA_CMP_LEN = 32
NSA_CMP_STRIDE = 16
NSA_SLC_LEN = 64
NSA_N_SEL = 16
NSA_WINDOW = 512
NSA_Q_BLOCK = 128
D_FF = 2816
RMS_EPS = 1e-6
NEG = -1e30

GLA_QK_W = GLA_HEADS * GLA_DK
GLA_V_W = GLA_HEADS * GLA_DV
NSA_Q_W = NSA_HEADS * NSA_DH
NSA_KV_W = NSA_GROUPS * NSA_DH
NSA_GATE_W = NSA_HEADS * 3
IN_SPLITS = (GLA_QK_W, GLA_QK_W, GLA_V_W, GLA_V_W, GLA_GATE_RANK,
             NSA_Q_W, NSA_KV_W, NSA_KV_W, NSA_KV_W, NSA_KV_W, NSA_KV_W, NSA_KV_W,
             NSA_GATE_W, D_MODEL, D_MODEL)
IN_WIDTH = 4 * GLA_QK_W // 2 + 2 * GLA_V_W + GLA_GATE_RANK + NSA_Q_W + 6 * NSA_KV_W + NSA_GATE_W + 2 * D_MODEL


def rms_norm(x, g):
    xf = x.astype(jnp.float32)
    y = xf * lax.rsqrt(jnp.mean(xf * xf, axis=-1, keepdims=True) + RMS_EPS)
    return (y * g.astype(jnp.float32)).astype(x.dtype)

def masked_softmax(s, mask):
    s = jnp.where(mask, s, NEG)
    p = jax.nn.softmax(s, axis=-1)
    return jnp.where(mask, p, 0.0)

def gla_mixer(q, k, v, r, a_lr, w_alpha2, b_alpha, norm_g):
    B, S = q.shape[0], q.shape[1]
    C = GLA_CHUNK
    nc = S // C

    def heads(t, d):
        return t.reshape(B, nc, C, GLA_HEADS, d).transpose(0, 3, 1, 2, 4).astype(jnp.float32)

    qh = heads(q, GLA_DK) * (GLA_DK ** -0.5)
    kh = heads(k, GLA_DK)
    vh = heads(v, GLA_DV)
    log_a = jax.nn.log_sigmoid((a_lr @ w_alpha2 + b_alpha).astype(jnp.float32)) / GLA_TAU
    b = jnp.cumsum(heads(log_a, GLA_DK), axis=3)
    b_last = b[:, :, :, -1:, :]
    qe = qh * jnp.exp(b)
    ke = kh * jnp.exp(-b)
    kd = kh * jnp.exp(b_last - b)
    causal = jnp.tril(jnp.ones((C, C), dtype=bool))
    attn = jnp.where(causal, jnp.einsum('bhncd,bhnsd->bhncs', qe, ke), 0.0)
    o = jnp.einsum('bhncs,bhnse->bhnce', attn, vh)
    upd = jnp.einsum('bhncd,bhnce->nbhde', kd, vh)
    decay = jnp.exp(b_last[:, :, :, 0, :]).transpose(2, 0, 1, 3)

    def step(state, inp):
        dec, u = inp
        return dec[..., None] * state + u, state

    init = jnp.zeros((B, GLA_HEADS, GLA_DK, GLA_DV), jnp.float32)
    _, s_prev = lax.scan(step, init, (decay, upd))
    o = o + jnp.einsum('bhncd,nbhde->bhnce', qe, s_prev)
    o = o * lax.rsqrt(jnp.mean(o * o, axis=-1, keepdims=True) + RMS_EPS) * norm_g.astype(jnp.float32)
    o = o.reshape(B, GLA_HEADS, S, GLA_DV).transpose(0, 2, 1, 3).reshape(B, S, GLA_V_W)
    return (o * jax.nn.silu(r.astype(jnp.float32))).astype(r.dtype)

def nsa_mixer(q, k_c, v_c, k_s, v_s, k_w, v_w, gate_logits, pe_k, w1_k, w2_k, pe_v, w1_v, w2_v):
    B, S = q.shape[0], q.shape[1]
    G, R, DH = NSA_GROUPS, NSA_REP, NSA_DH
    L, ST, SL, QB, W = NSA_CMP_LEN, NSA_CMP_STRIDE, NSA_SLC_LEN, NSA_Q_BLOCK, NSA_WINDOW
    qh = q.reshape(B, S, G, R, DH).transpose(0, 2, 3, 1, 4).astype(jnp.float32) * (DH ** -0.5)

    def kv_heads(t):
        return t.reshape(B, S, G, DH).transpose(0, 2, 1, 3).astype(jnp.float32)

    gates = jax.nn.sigmoid(gate_logits.astype(jnp.float32)).reshape(B, S, G, R, 3).transpose(0, 2, 3, 1, 4)
    h_idx = jnp.arange(NSA_HEADS, dtype=jnp.float32)
    slopes = jnp.exp2(-8.0 * (h_idx + 1.0) / NSA_HEADS).reshape(1, G, R, 1, 1)

    n_cmp = (S - L) // ST + 1
    starts_c = ST * jnp.arange(n_cmp)
    idx_c = starts_c[:, None] + jnp.arange(L)[None, :]

    def compress(t, pe, w1, w2):
        blocks = t[:, :, idx_c] + pe
        flat = blocks.reshape(B, G, n_cmp, L * DH)
        return jax.nn.silu(flat @ w1) @ w2

    kc = compress(kv_heads(k_c), pe_k, w1_k, w2_k).astype(jnp.float32)
    vc = compress(kv_heads(v_c), pe_v, w1_v, w2_v).astype(jnp.float32)
    end_c = starts_c + L - 1

    n_slc = S // SL
    n_sel = min(NSA_N_SEL, n_slc)
    starts_s = SL * jnp.arange(n_slc)
    ov = jnp.clip(jnp.minimum(starts_c[:, None] + L, starts_s[None, :] + SL)
                  - jnp.maximum(starts_c[:, None], starts_s[None, :]), 0, None).astype(jnp.float32) / L
    ks_blocks = kv_heads(k_s).reshape(B, G, n_slc, SL, DH)
    vs_blocks = kv_heads(v_s).reshape(B, G, n_slc, SL, DH)
    gather = jax.vmap(jax.vmap(lambda blk, ix: blk[ix]))

    kw_pad = jnp.pad(kv_heads(k_w), ((0, 0), (0, 0), (W, 0), (0, 0)))
    vw_pad = jnp.pad(kv_heads(v_w), ((0, 0), (0, 0), (W, 0), (0, 0)))

    nq = S // QB
    q_blocks = qh.reshape(B, G, R, nq, QB, DH).transpose(3, 0, 1, 2, 4, 5)
    g_blocks = gates.reshape(B, G, R, nq, QB, 3).transpose(3, 0, 1, 2, 4, 5)
    jb = jnp.arange(n_slc)
    r_w = jnp.arange(W + QB)

    def attend_block(args):
        i, qb, gb = args
        q0 = i * QB
        t = q0 + jnp.arange(QB)
        tf = t.astype(jnp.float32)
        dist_c = tf[:, None] - end_c[None, :].astype(jnp.float32)
        s_c = jnp.einsum('bgrqd,bgnd->bgrqn', qb, kc) - slopes * dist_c
        p_c = masked_softmax(s_c, end_c[None, :] <= t[:, None])
        o_c = jnp.einsum('bgrqn,bgnd->bgrqd', p_c, vc)
        imp = jnp.einsum('bgrqn,nj->bgqj', p_c, ov)
        cur = t // SL
        forced = (jb[None, :] == 0) | (jb[None, :] == cur[:, None]) | (jb[None, :] == cur[:, None] - 1)
        score = jnp.where(jb[None, :] > cur[:, None], NEG, jnp.where(forced, -NEG, imp))
        _, sel = lax.top_k(score, n_sel)
        ks = gather(ks_blocks, sel).reshape(B, G, QB, n_sel * SL, DH)
        vs = gather(vs_blocks, sel).reshape(B, G, QB, n_sel * SL, DH)
        pos_s = (sel[..., None] * SL + jnp.arange(SL)).reshape(B, G, QB, n_sel * SL)
        dist_s = (tf[None, None, :, None] - pos_s.astype(jnp.float32))[:, :, None]
        s_s = jnp.einsum('bgrqd,bgqkd->bgrqk', qb, ks) - slopes * dist_s
        p_s = masked_softmax(s_s, (pos_s <= t[None, None, :, None])[:, :, None])
        o_s = jnp.einsum('bgrqk,bgqkd->bgrqd', p_s, vs)
        kw = lax.dynamic_slice_in_dim(kw_pad, q0, W + QB, axis=2)
        vw = lax.dynamic_slice_in_dim(vw_pad, q0, W + QB, axis=2)
        pos_w = q0 - W + r_w
        dist_w = t[:, None] - pos_w[None, :]
        mask_w = (pos_w[None, :] >= 0) & (dist_w >= 0) & (dist_w < W)
        s_w = jnp.einsum('bgrqd,bgkd->bgrqk', qb, kw) - slopes * dist_w.astype(jnp.float32)
        p_w = masked_softmax(s_w, mask_w)
        o_w = jnp.einsum('bgrqk,bgkd->bgrqd', p_w, vw)
        return gb[..., 0:1] * o_c + gb[..., 1:2] * o_s + gb[..., 2:3] * o_w

    o = lax.map(attend_block, (jnp.arange(nq), q_blocks, g_blocks))
    return o.transpose(1, 0, 4, 2, 3, 5).reshape(B, S, NSA_Q_W).astype(q.dtype)

def first_inputs(seed: int = 0) -> dict:
    key = jax.random.key(seed)
    ks = jax.random.split(key, 24)
    f32 = jnp.float32

    def normal(k, shape, fan_in):
        return jax.random.normal(k, shape, f32) * (fan_in ** -0.5)

    def gain(k, shape):
        return 1.0 + 0.1 * jax.random.normal(k, shape, f32)

    Ld = DEPTH
    return {
        'x': jax.random.normal(ks[0], (BATCH, SEQ, D_MODEL), f32),
        'norm_mix_pre': gain(ks[1], (Ld, D_MODEL)),
        'norm_mix_post': gain(ks[2], (Ld, D_MODEL)),
        'norm_ffn_pre': gain(ks[3], (Ld, D_MODEL)),
        'norm_ffn_post': gain(ks[4], (Ld, D_MODEL)),
        'w_in': normal(ks[5], (Ld, D_MODEL, IN_WIDTH), D_MODEL),
        'gla_w_alpha2': normal(ks[6], (Ld, GLA_GATE_RANK, GLA_QK_W), GLA_GATE_RANK),
        'gla_b_alpha': 0.1 * jax.random.normal(ks[7], (Ld, GLA_QK_W), f32),
        'gla_norm_g': gain(ks[8], (Ld, GLA_DV)),
        'nsa_cmp_pe_k': 0.1 * jax.random.normal(ks[9], (Ld, NSA_CMP_LEN, NSA_DH), f32),
        'nsa_cmp_w1_k': normal(ks[10], (Ld, NSA_CMP_LEN * NSA_DH, NSA_DH), NSA_CMP_LEN * NSA_DH),
        'nsa_cmp_w2_k': normal(ks[11], (Ld, NSA_DH, NSA_DH), NSA_DH),
        'nsa_cmp_pe_v': 0.1 * jax.random.normal(ks[12], (Ld, NSA_CMP_LEN, NSA_DH), f32),
        'nsa_cmp_w1_v': normal(ks[13], (Ld, NSA_CMP_LEN * NSA_DH, NSA_DH), NSA_CMP_LEN * NSA_DH),
        'nsa_cmp_w2_v': normal(ks[14], (Ld, NSA_DH, NSA_DH), NSA_DH),
        'w_proj_gla': normal(ks[15], (Ld, GLA_V_W, D_MODEL), GLA_V_W),
        'w_proj_nsa': normal(ks[16], (Ld, NSA_Q_W, D_MODEL), NSA_Q_W),
        'w_out': normal(ks[17], (Ld, D_MODEL, D_MODEL), D_MODEL),
        'w_ffn_gate': normal(ks[18], (Ld, D_MODEL, D_FF), D_MODEL),
        'w_ffn_up': normal(ks[19], (Ld, D_MODEL, D_FF), D_MODEL),
        'w_ffn_down': normal(ks[20], (Ld, D_FF, D_MODEL), D_FF),
    }

def first_block(x, norm_mix_pre, norm_mix_post, norm_ffn_pre, norm_ffn_post, w_in,
              gla_w_alpha2, gla_b_alpha, gla_norm_g,
              nsa_cmp_pe_k, nsa_cmp_w1_k, nsa_cmp_w2_k, nsa_cmp_pe_v, nsa_cmp_w1_v, nsa_cmp_w2_v,
              w_proj_gla, w_proj_nsa, w_out, w_ffn_gate, w_ffn_up, w_ffn_down):
    split_points = [int(c) for c in np.cumsum(IN_SPLITS)[:-1]]
    for l in range(DEPTH):
        h = rms_norm(x, norm_mix_pre[l])
        proj = h @ w_in[l]
        (g_q, g_k, g_v, g_r, g_a, n_q, n_kc, n_vc, n_ks, n_vs, n_kw, n_vw,
         n_gate, merge_gla, merge_nsa) = jnp.split(proj, split_points, axis=-1)
        o_gla = gla_mixer(g_q, g_k, g_v, g_r, g_a, gla_w_alpha2[l], gla_b_alpha[l], gla_norm_g[l])
        o_nsa = nsa_mixer(n_q, n_kc, n_vc, n_ks, n_vs, n_kw, n_vw, n_gate,
                          nsa_cmp_pe_k[l], nsa_cmp_w1_k[l], nsa_cmp_w2_k[l],
                          nsa_cmp_pe_v[l], nsa_cmp_w1_v[l], nsa_cmp_w2_v[l])
        mixed = (jax.nn.sigmoid(merge_gla) * (o_gla @ w_proj_gla[l])
                 + jax.nn.sigmoid(merge_nsa) * (o_nsa @ w_proj_nsa[l]))
        x = x + rms_norm(mixed @ w_out[l], norm_mix_post[l])
        h = rms_norm(x, norm_ffn_pre[l])
        f = (jax.nn.silu(h @ w_ffn_gate[l]) * (h @ w_ffn_up[l])) @ w_ffn_down[l]
        x = x + rms_norm(f, norm_ffn_post[l])
    return x


CHUNK = 64
MIX_WIDTH = D_MODEL
CONV_A_WIDTH = D_MODEL // 4
CONV_A_K = 3
CONV_B_WIDTH = D_MODEL // 4
CONV_B_K = 31
SB_HEAD_DIM = 64
SB_HEADS = (MIX_WIDTH - CONV_A_WIDTH - CONV_B_WIDTH) // SB_HEAD_DIM
SB_WIDTH = SB_HEADS * SB_HEAD_DIM
SB_BLOCK = 128
D_FF_2 = 4 * D_MODEL
IN_COLS = 3 * CONV_A_WIDTH + 2 * CONV_B_WIDTH + 3 * SB_WIDTH
LN_EPS = 1e-5


def _rmsnorm(x, g):
    xf = x.astype(jnp.float32)
    y = xf * lax.rsqrt(jnp.mean(xf * xf, axis=-1, keepdims=True) + RMS_EPS)
    return (y * g.astype(jnp.float32)).astype(x.dtype)

def _layernorm(x, g, b):
    xf = x.astype(jnp.float32)
    mu = jnp.mean(xf, axis=-1, keepdims=True)
    var = jnp.mean(jnp.square(xf - mu), axis=-1, keepdims=True)
    y = (xf - mu) * lax.rsqrt(var + LN_EPS)
    return (y * g.astype(jnp.float32) + b.astype(jnp.float32)).astype(x.dtype)

def _causal_dwconv(x, w):
    k, c = w.shape
    return lax.conv_general_dilated(
        x, w[:, None, :].astype(x.dtype),
        window_strides=(1,), padding=((k - 1, 0),),
        dimension_numbers=("NWC", "WIO", "NWC"),
        feature_group_count=c)

def _stick_breaking(q, k, v):
    t_len = q.shape[2]
    scale = 1.0 / math.sqrt(q.shape[-1])
    outs = []
    for q0 in range(0, t_len, SB_BLOCK):
        kv_len = q0 + SB_BLOCK
        qb = q[:, :, q0:kv_len]
        kb = k[:, :, :kv_len]
        vb = v[:, :, :kv_len]
        z = jnp.einsum("bhqd,bhkd->bhqk", qb, kb).astype(jnp.float32) * scale
        t_idx = q0 + jnp.arange(SB_BLOCK)[:, None]
        s_idx = jnp.arange(kv_len)[None, :]
        mask = s_idx < t_idx
        log_beta = jax.nn.log_sigmoid(z)
        log_1m = jnp.where(mask, log_beta - z, 0.0)
        suffix = lax.cumsum(log_1m, axis=3, reverse=True) - log_1m
        a = jnp.where(mask, jnp.exp(log_beta + suffix), 0.0)
        outs.append(jnp.einsum("bhqk,bhkd->bhqd", a.astype(v.dtype), vb))
    return jnp.concatenate(outs, axis=2)

def _layer(x, g_attn, w_in, w_conv_a, w_conv_b, b_conv_b, ln_b_g, ln_b_b, w_out,
           g_ffn, w_ff1, w_ff2):
    bsz, t_len, _ = x.shape
    h = _rmsnorm(x, g_attn)
    p = h @ w_in
    o0 = 0
    def take(n):
        nonlocal o0
        s = p[..., o0:o0 + n]
        o0 += n
        return s
    a_b = take(CONV_A_WIDTH)
    a_c = take(CONV_A_WIDTH)
    a_h = take(CONV_A_WIDTH)
    b_glu = take(2 * CONV_B_WIDTH)
    q = take(SB_WIDTH)
    k = take(SB_WIDTH)
    v = take(SB_WIDTH)

    y_a = a_b * _causal_dwconv(a_c * a_h, w_conv_a)

    g = b_glu[..., :CONV_B_WIDTH] * jax.nn.sigmoid(b_glu[..., CONV_B_WIDTH:])
    g = _causal_dwconv(g, w_conv_b) + b_conv_b
    y_b = jax.nn.silu(_layernorm(g, ln_b_g, ln_b_b))

    def heads(t):
        return t.reshape(bsz, t_len, SB_HEADS, SB_HEAD_DIM).transpose(0, 2, 1, 3)
    o = _stick_breaking(heads(q), heads(k), heads(v))
    y_c = o.transpose(0, 2, 1, 3).reshape(bsz, t_len, SB_WIDTH)

    x = x + jnp.concatenate([y_a, y_b, y_c], axis=-1) @ w_out

    h2 = _rmsnorm(x, g_ffn)
    x = x + jnp.square(jax.nn.relu(h2 @ w_ff1)) @ w_ff2
    return x

def second_inputs(seed: int = 0) -> dict:
    key = jax.random.key(seed)
    ks = jax.random.split(key, 14)
    f32 = jnp.float32
    def nrm(k, shape, scale):
        return jax.random.normal(k, shape, f32) * scale
    return {
        "x": nrm(ks[0], (BATCH, SEQ, D_MODEL), 1.0),
        "g_attn": 1.0 + nrm(ks[1], (DEPTH, D_MODEL), 0.02),
        "w_in": nrm(ks[2], (DEPTH, D_MODEL, IN_COLS), D_MODEL ** -0.5),
        "w_conv_a": nrm(ks[3], (DEPTH, CONV_A_K, CONV_A_WIDTH), CONV_A_K ** -0.5),
        "w_conv_b": nrm(ks[4], (DEPTH, CONV_B_K, CONV_B_WIDTH), CONV_B_K ** -0.5),
        "b_conv_b": nrm(ks[5], (DEPTH, CONV_B_WIDTH), 0.02),
        "ln_b_g": 1.0 + nrm(ks[6], (DEPTH, CONV_B_WIDTH), 0.02),
        "ln_b_b": nrm(ks[7], (DEPTH, CONV_B_WIDTH), 0.02),
        "w_out": nrm(ks[8], (DEPTH, MIX_WIDTH, D_MODEL), MIX_WIDTH ** -0.5),
        "g_ffn": 1.0 + nrm(ks[9], (DEPTH, D_MODEL), 0.02),
        "w_ff1": nrm(ks[10], (DEPTH, D_MODEL, D_FF_2), D_MODEL ** -0.5),
        "w_ff2": nrm(ks[11], (DEPTH, D_FF_2, D_MODEL), D_FF_2 ** -0.5),
        "g_final": 1.0 + nrm(ks[12], (D_MODEL,), 0.02),
    }

def second_block(x, g_attn, w_in, w_conv_a, w_conv_b, b_conv_b, ln_b_g, ln_b_b, w_out,
              g_ffn, w_ff1, w_ff2, g_final):
    for l in range(DEPTH):
        x = _layer(x, g_attn[l], w_in[l], w_conv_a[l], w_conv_b[l], b_conv_b[l],
                   ln_b_g[l], ln_b_b[l], w_out[l], g_ffn[l], w_ff1[l], w_ff2[l])
    return _rmsnorm(x, g_final)


def setup_inputs(seed=0):
    out = dict(first_inputs(seed))
    for name, value in second_inputs(seed + 1).items():
        if name != "x":
            out[name + "_2"] = value
    return out


def reference(
    x, norm_mix_pre, norm_mix_post, norm_ffn_pre, norm_ffn_post, w_in, gla_w_alpha2,
    gla_b_alpha, gla_norm_g, nsa_cmp_pe_k, nsa_cmp_w1_k, nsa_cmp_w2_k, nsa_cmp_pe_v,
    nsa_cmp_w1_v, nsa_cmp_w2_v, w_proj_gla, w_proj_nsa, w_out, w_ffn_gate, w_ffn_up, w_ffn_down,
    g_attn_2, w_in_2, w_conv_a_2, w_conv_b_2, b_conv_b_2, ln_b_g_2, ln_b_b_2, w_out_2, g_ffn_2,
    w_ff1_2, w_ff2_2, g_final_2,
):
    x = first_block(
        x, norm_mix_pre, norm_mix_post, norm_ffn_pre, norm_ffn_post, w_in, gla_w_alpha2,
        gla_b_alpha, gla_norm_g, nsa_cmp_pe_k, nsa_cmp_w1_k, nsa_cmp_w2_k, nsa_cmp_pe_v,
        nsa_cmp_w1_v, nsa_cmp_w2_v, w_proj_gla, w_proj_nsa, w_out, w_ffn_gate, w_ffn_up,
        w_ffn_down,
    )
    return second_block(
        x, g_attn_2, w_in_2, w_conv_a_2, w_conv_b_2, b_conv_b_2, ln_b_g_2, ln_b_b_2, w_out_2,
        g_ffn_2, w_ff1_2, w_ff2_2, g_final_2,
    )


_drawn_inputs = setup_inputs


def setup_inputs(seed=0):
    import zlib

    import numpy as np

    out = dict(_drawn_inputs(seed))
    spreads = {}
    factors = {'nsa_cmp_pe_k': 8.0,
     'g_attn_2': 4.689,
     'b_conv_b_2': 64.0,
     'ln_b_g_2': 64.0,
     'ln_b_b_2': 64.0,
     'g_ffn_2': 24.55,
     'g_final_2': 8.075}
    for name, (base, spread) in spreads.items():
        noise = np.random.default_rng([zlib.crc32(name.encode()), seed]).standard_normal(out[name].shape)
        drawn = base * np.exp(spread * noise) if base else spread * noise
        out[name] = jnp.asarray(drawn.astype(out[name].dtype))
    for name, factor in factors.items():
        out[name] = (out[name] * factor).astype(out[name].dtype)
    return out
```

```python
from contextlib import ExitStack

import numpy as np

import concourse.bass as bass
from concourse import mybir

F32 = mybir.dt.float32
F32R = mybir.dt.float32r
U32 = mybir.dt.uint32
ALU = mybir.AluOpType
ACT = mybir.ActivationFunctionType
AXX = mybir.AxisListType.X

P = 128
S = 512
D = 1024
TT = S // P
KD = D // P
RMS_EPS = 1e-6
LN_EPS = 1e-5
NEG = -1e30

GLA_H, DK, DV, RANK, TAU, CHUNK = 4, 128, 256, 16, 16.0, 64
NCH = S // CHUNK
NH, NG, DH = 8, 2, 64
REP = NH // NG
CL, CS = 32, 16
NCMP = (S - CL) // CS + 1
D_FF, D_FF2 = 2816, 4096
CW, KA, KB = 256, 3, 31
SLOPES = 2.0 ** (-8.0 * (np.arange(NH) + 1) / NH)
SBH = 8

FILLS = [(1, 3, 5, 7), (1, 3, 5), (1, 3, 5), (0, 2)]
FILL_EVERY = 6

EARLY = 4
GATE_EVERY = 12

FILL2_EVERY = 4

_w = dict(gq=512, gk=512, gv=1024, gr=1024, ga=16, nq=512, kc=128, vc=128, ks=128, vs=128, kw=128,
          vw=128, gate=24, mg=1024, mn=1024)
OFF1 = dict(zip(_w, np.cumsum([0] + list(_w.values()))[:-1].tolist()))
_w2 = dict(ab=256, ac=256, ah=256, glu=512, q=512, k=512, v=512)
OFF2 = dict(zip(_w2, np.cumsum([0] + list(_w2.values()))[:-1].tolist()))

CH = 2048
HALF = CH // 2


def cols(start, n):
    return list(range(start, start + n))


def groups_of(n, sizes):
    out, at = [], 0
    for s in sizes:
        out.append((at, s))
        at += s
    assert at == n
    return out


NSA_ROWS = sum((cols(DH * j, DH) + cols(DH * (REP + j), DH) for j in range(REP)), [])
FFN1_GROUPS = groups_of(D_FF // P, [6, 6, 5, 5])
FFN2_GROUPS = groups_of(D_FF2 // P, [6, 6, 5, 5, 5, 5])


def plan():
    out = []

    def by_column(layer, w, c, nk=KD):
        n = CH // nk
        for a in range(0, len(c), n):
            out.append((layer, w, 0, nk, c[a:a + n]))

    def by_row(layer, w, c, row0, nk):
        for a in range(0, nk, 4):
            out.append((layer, w, row0 + a * P, min(4, nk - a), c))

    o = OFF1
    by_column("gla a", "w_in", cols(o["ga"], 16))
    for n in range(2):
        by_row("gla v", "w_in", cols(o["gv"] + 512 * n, 512), 0, KD)

    def gla_qk(h):
        by_column(f"gla qk {h}", "w_in", cols(o["gq"] + DK * h, DK) + cols(o["gk"] + DK * h, DK))

    nq = [sum((cols(o["nq"] + DH * j, DH) + cols(o["nq"] + DH * (REP + j), DH) for j in pair), [])
          for pair in ((0, 1), (2, 3))]
    gla_qk(0)
    by_row("nsa v gate", "w_in", cols(o["vs"], P) + cols(o["vw"], P) + cols(o["gate"], 24), 0, KD)
    gla_qk(1)
    by_column("nsa kc vc", "w_in", cols(o["kc"], P) + cols(o["vc"], P))
    gla_qk(2)
    by_column("gla r", "w_in", cols(o["gr"], 2 * P))
    gla_qk(3)
    by_column("gla r", "w_in", cols(o["gr"] + 2 * P, D - 4 * P))
    by_column("nsa q", "w_in", nq[0])
    by_column("nsa q", "w_in", nq[1])
    by_column("nsa ks kw", "w_in", cols(o["ks"], P) + cols(o["kw"], P))
    by_column("gla r", "w_in", cols(o["gr"] + D - 2 * P, 2 * P))
    by_column("merge gates", "w_in", cols(o["mg"], P * EARLY))
    for j in range(0, KD, 2):
        if j >= EARLY:
            by_column("merge gates", "w_in", cols(o["mg"] + P * j, 2 * P))
        by_column("proj gla", "w_proj_gla", cols(P * j, 2 * P))
        by_column("merge gates", "w_in", cols(o["mn"] + P * j, 2 * P))
        by_column("proj nsa", "w_proj_nsa", cols(P * j, 2 * P), 4)
    for n in range(2):
        by_row("out", "w_out", cols(512 * n, 512), 0, KD)

    def ffn(tag, groups, ups, down):
        for g in range(len(groups) + 1):
            if g < len(groups):
                t0, nt = groups[g]
                if len(ups) == 2:
                    for t in range(t0, t0 + nt):
                        for u in ups:
                            by_column(f"up {tag}", u, cols(P * t, P))
                else:
                    by_column(f"up {tag}", ups[0], cols(P * t0, P * nt))
            if g:
                t0, nt = groups[g - 1]
                for n in range(2):
                    by_row(f"down {tag}", down, cols(512 * n, 512), P * t0, nt)

    ffn(1, FFN1_GROUPS, ["w_ffn_gate", "w_ffn_up"], "w_ffn_down")
    o = OFF2
    by_column("glu 2", "w_in_2", cols(o["glu"], 512))
    by_row("v 2", "w_in_2", cols(o["v"], 512), 0, KD)

    def qk2(f):
        by_column("qk 2", "w_in_2", cols(o["q"] + P * f, P) + cols(o["k"] + P * f, P))

    for f in range(3):
        qk2(f)
    by_column("ac ah 2", "w_in_2", cols(o["ac"], 512))
    qk2(3)
    by_column("ab 2", "w_in_2", cols(o["ab"], 256))
    for n in range(2):
        by_row("out 2", "w_out_2", cols(512 * n, 512), 0, KD)
    ffn(2, FFN2_GROUPS, ["w_ff1_2"], "w_ff2_2")
    return out


_vec = [("norm_mix_pre", 8), ("norm_ffn_pre", 8), ("g_attn_2", 8), ("g_ffn_2", 8), ("gla_b_alpha", 4),
        ("gla_norm_g", 2), ("b_conv_b_2", 2), ("ln_b_g_2", 2), ("ln_b_b_2", 2)]
VEC, NVEC = {}, 0
for _name, _n in _vec:
    VEC[_name] = (NVEC, _n)
    NVEC += _n
_con = [("ident", P), ("gla_mask", P), ("upper", P), ("block", P), ("before", P), ("ones", P),
        ("eps", 2), ("dist", S), ("cmp_dist", TT * NCMP), ("cmp_mask", TT * 32),
        ("q_scale", REP), ("slopes", NH), ("minus_slopes", NH)]
CON, NCON = {}, 0
for _name, _n in _con:
    CON[_name] = (NCON, _n)
    NCON += _n


def constants():
    p, c = np.arange(P)[:, None], np.arange(P)[None, :]
    out = np.zeros((P, NCON), np.float32)

    def put(name, a):
        o, n = CON[name]
        out[:, o:o + n] = np.broadcast_to(a, (P, n))

    put("ident", p == c)
    put("gla_mask", (p <= c) & (p // CHUNK == c // CHUNK))
    put("upper", -1.0 * (p >= c))
    put("block", np.where(p < c, 0.0, NEG))
    put("before", p < c)
    put("ones", 1.0)
    put("eps", np.array([RMS_EPS, LN_EPS]))
    key = np.arange(S)[None, :] - (S - P)
    put("dist", np.where(key <= p, key - p, NEG))
    t = p + P * np.arange(TT)[None, :]
    end = CS * np.arange(NCMP) + CL - 1
    seen = end[None, None, :] <= t[:, :, None]
    put("cmp_dist", np.where(seen, end[None, None, :] - t[:, :, None], NEG).reshape(P, -1))
    m = np.zeros((P, TT, 32))
    m[:, :, :NCMP] = seen
    put("cmp_mask", m.reshape(P, -1))
    head = np.where(p < DH, 0, REP) + np.arange(REP)[None, :]
    put("q_scale", DH ** -0.5 / SLOPES[head])
    put("slopes", SLOPES)
    put("minus_slopes", -SLOPES)
    return out


class Lane:

    def __init__(self, engine, sem):
        self.engine, self.sem, self.count, self.queue, self.waited = engine, sem, 0, [], {}

    def wait(self, *marks):
        for lane, value in marks:
            if self.waited.get(id(lane), 0) < value:
                self.waited[id(lane)] = value
                self.queue.append((self.engine.wait_ge, (lane.sem, value), {}, None))

    def run(self, what, *args, after=(), **named):
        self.wait(*after)
        self.queue.append((what, args, named, None))

    def do(self, what, *args, after=(), **named):
        self.wait(*after)
        self.count += 1
        self.queue.append((what, args, named, (self.sem, 1)))
        return self, self.count

    def write(self):
        for what, args, named, signal in self.queue:
            instruction = what(*args, **named)
            if signal:
                instruction.then_inc(*signal)


class Loads:

    def __init__(self, sem):
        self.sem, self.count = sem, 0

    def start(self, lane, out, in_, after=()):
        lane.wait(*after)
        self.count += 16
        lane.queue.append((lane.engine.dma_start, (out, in_), {}, (self.sem, 16)))
        return self, self.count


class Rotating:

    def __init__(self, bufs):
        self.bufs, self.at, self.readers = bufs, -1, [[] for _ in bufs]

    def take(self):
        self.at = (self.at + 1) % len(self.bufs)
        marks, self.readers[self.at] = self.readers[self.at], []
        return self.bufs[self.at], marks, self.readers[self.at]


def program(nc, T, wstream, vectors, consts, out):
    outer = ExitStack()
    with outer:
        def sb(name, shape, dt=F32, ctx=outer):
            return ctx.enter_context(nc.sbuf_tensor(name, [P] + shape, dt))

        def sem(name):
            return outer.enter_context(nc.semaphore(name))

        pe = Lane(nc.tensor, sem("pe_done"))
        act = Lane(nc.scalar, sem("act_done"))
        dve = Lane(nc.vector, sem("dve_done"))
        pool = Lane(nc.gpsimd, sem("pool_done"))
        sp = Lane(nc.sync, sem("sp_done"))
        banks = [outer.enter_context(nc.psum_tensor(f"bank{i}", [P, 512], F32)) for i in range(8)]
        linear_banks = Rotating(banks[0:2])
        core_banks = Rotating(banks[2:8])

        con = sb("con", [NCON])
        vec = sb("vec", [NVEC])

        def C(name):
            o, n = CON[name]
            return con[:, o:o + n]

        def V(name, j):
            return vec[:, VEC[name][0] + j:VEC[name][0] + j + 1]

        eps_rms, eps_ln = C("eps")[:, 0:1], C("eps")[:, 1:2]
        ident = C("ident")
        ident_r, upper_r, ones_r, block_r = (sb(n, [P], F32R) for n in ("ident_r", "upper_r", "ones_r", "block_r"))
        got_con = Loads(sem("got_con")).start(sp, con[:, :], consts)
        got_vec = Loads(sem("got_vec")).start(sp, vec[:, :], vectors)

        def exp_ln_tables():
            act.run(nc.scalar.preload_act_table_set, "natural_log_exp_and_others")

        exp_ln_tables()
        act.do(nc.scalar.activation, ident_r[:, :], ident, ACT.Copy, after=[got_con])
        act.do(nc.scalar.activation, upper_r[:, :], C("upper"), ACT.Copy)
        act.do(nc.scalar.activation, ones_r[:, :], C("ones"), ACT.Copy, scale=-1.0)
        consts_r = act.do(nc.scalar.activation, block_r[:, :], C("block"), ACT.Copy)
        dve.wait(got_con, got_vec)
        act.wait(got_con, got_vec)
        pe.wait(got_con)
        pool.wait(got_con)

        NW, NRAW = 4, 3
        w_raw = sb("w_raw", [NRAW, HALF])
        w_hi = sb("w_hi", [NW, CH], F32R)
        w_lo = sb("w_lo", [NW, CH], F32R)
        raw_loads = [Loads(sem(f"raw_load{i}")) for i in range(NRAW)]
        raw_free = [[] for _ in range(NRAW)]
        chunks = plan()
        state = dict(loaded=0, raw=0, used=0, at=0)
        chunk_ready, chunk_free = {}, {}

        def bring():
            while state["loaded"] < len(chunks):
                n = state["loaded"]
                if n >= NW and n - NW not in chunk_free:
                    return
                state["loaded"] += 1
                _, _, _, nk, c = chunks[n]
                size = nk * len(c)
                slot = n % NW
                free = chunk_free.get(n - NW, [])
                at = state["at"]
                src = wstream[at:at + P * size].rearrange("(p n) -> p n", p=P)
                state["at"] += P * size
                chunk_ready[n] = []
                for a in range(0, size, HALF):
                    b = min(size, a + HALF)
                    r = state["raw"] % NRAW
                    lo_lane = pool if state["raw"] % 2 else dve
                    state["raw"] += 1
                    got = raw_loads[r].start(sp, w_raw[:, r, 0:b - a], src[:, a:b], raw_free[r])
                    hi, lo, raw = w_hi[:, slot, a:b], w_lo[:, slot, a:b], w_raw[:, r, 0:b - a]
                    m1 = act.do(nc.scalar.activation, hi, raw, ACT.Copy, after=[got, *free])
                    m2 = lo_lane.do(lo_lane.engine.tensor_tensor, lo, raw, hi.bitcast(F32), ALU.subtract,
                                    after=[m1, *free])
                    raw_free[r] = [m1, m2]
                    chunk_ready[n] += [m1, m2]

        def next_chunk(layer):
            n = state["used"]
            state["used"] += 1
            planned, _, _, nk, c = chunks[n]
            assert planned == layer, (planned, layer)
            pe.wait(*chunk_ready[n])
            hi, lo = (w[:, n % NW, 0:nk * len(c)].rearrange("p (k c) -> p k c", k=nk) for w in (w_hi, w_lo))
            return hi, lo, n

        def chunk_done(n, mark):
            chunk_free[n] = [mark]
            bring()

        def by_column_tiles(layer, act_hi, act_lo, ready, evacuate, n_tiles, nk=KD, width=P):
            f = 0
            while f < n_tiles:
                hi, lo, n = next_chunk(layer)
                here = len(chunks[n][4]) // width
                for t in range(here):
                    bank, free, readers = linear_banks.take()
                    pe.wait(*free, *ready(0))
                    o = bank[0:width, :]
                    for k in range(nk):
                        pe.wait(*ready(k))
                        ws = slice(t * width, (t + 1) * width)
                        for i, (a, b) in enumerate(((hi, act_hi), (lo, act_hi), (hi, act_lo))):
                            operands = (o, a[:, k, ws], b[:, k, :])
                            step = dict(start=(k == 0 and i == 0), stop=(k == nk - 1 and i == 2))
                            if k == nk - 1 and i == 2:
                                done = pe.do(nc.tensor.matmul, *operands, **step)
                            else:
                                pe.run(nc.tensor.matmul, *operands, **step)
                    if t == here - 1:
                        chunk_done(n, done)
                    readers += evacuate(f, o, done)
                    f += 1
                    yield

        def by_row_tiles(layer, act_hi, act_lo, ready, evacuate, nk, k0=0, halves=(0, 1)):
            for n in halves:
                held = [next_chunk(layer) for _ in range((nk + 3) // 4)]
                width = len(chunks[held[0][2]][4])
                for i in range(TT):
                    bank, free, readers = linear_banks.take()
                    pe.wait(*free)
                    o = bank[:, 0:width]
                    for k in range(nk):
                        pe.wait(*ready(k0 + k))
                        hi, lo, num = held[k // 4]
                        for j, (a, b) in enumerate(((act_hi, hi), (act_lo, hi), (act_hi, lo))):
                            operands = (o, a[:, k0 + k, P * i:P * (i + 1)], b[:, k % 4, :])
                            step = dict(start=(k == 0 and j == 0), stop=(k == nk - 1 and j == 2))
                            if j == 2 and (k == nk - 1 or (k % 4 == 3 and i == TT - 1)):
                                done = pe.do(nc.tensor.matmul, *operands, **step)
                                if i == TT - 1:
                                    chunk_done(num, done)
                            else:
                                pe.run(nc.tensor.matmul, *operands, **step)
                    readers += evacuate(n, i, o, done)
                    yield

        def finish(*gens):
            for g in gens:
                for _ in g:
                    pass

        def weave(main, filler, every=1):
            for _ in main:
                for _ in range(every):
                    next(filler, None)
            finish(filler)

        stat = sb("stat", [8, TT])
        junk = sb("junk", [512])

        def rstd_rows(rows_of, ready, last_readers):
            marks, squares = [], []
            for i in range(TT):
                for h in range(2):
                    squares.append(act.do(nc.scalar.activation, junk[:, :], rows_of(i)[:, 512 * h:512 * h + 512], ACT.Square,
                        accum_out=stat[:, 2 + h, i:i + 1], after=[*ready(i), *last_readers, *squares[-1:]]))
            for i in range(TT):
                m = dve.do(nc.vector.tensor_tensor, stat[:, 4, i:i + 1], stat[:, 2, i:i + 1],
                                                          stat[:, 3, i:i + 1], ALU.add, after=squares[2 * i:2 * i + 2])
                m = act.do(nc.scalar.activation, stat[:, 5, i:i + 1], stat[:, 4, i:i + 1], ACT.Ln,
                                                       bias=eps_rms, scale=1.0 / D, after=[m])
                marks.append(act.do(nc.scalar.activation, stat[:, 6, i:i + 1], stat[:, 5, i:i + 1],
                                                                ACT.Exp, scale=-0.5, after=[m]))
            return marks

        h_hi = sb("h_hi", [KD, S], F32R)
        h_lo = sb("h_lo", [KD, S], F32R)
        h_ready = [[] for _ in range(KD)]

        def norm_to_columns(rows_of, scaled, ready, gain, h_free, last_readers):
            rs = rstd_rows(rows_of, ready, last_readers)
            sc = []
            for i in range(TT):
                lane = dve if i % 2 else pool
                sc.append(lane.do(lane.engine.tensor_scalar, scaled[:, i, :], rows_of(i), stat[:, 6, i:i + 1],
                                                                 None, ALU.mult, after=[rs[i], *ready(i)]))
            for k in range(KD):
                bank, free, readers = core_banks.take()
                pe.wait(*free, *sc)
                for i in range(TT):
                    m = pe.do(nc.tensor.transpose, bank[:, P * i:P * (i + 1)], scaled[:, i, P * k:P * (k + 1)], ident)
                g = V(gain, k)
                hi = act.do(nc.scalar.activation, h_hi[:, k, :], bank[:, :], ACT.Copy, scale=g, after=[m, *h_free])
                lo = dve.do(nc.vector.scalar_tensor_tensor, h_lo[:, k, :], bank[:, :], g, h_hi[:, k, :].bitcast(F32), ALU.mult, ALU.subtract, after=[m, hi, *h_free])
                readers += [hi, lo]
                h_ready[k] = [hi, lo]
            return [m]

        def split(hi_ap, lo_ap, src, after, lo_lane=pool):
            hi = act.do(nc.scalar.activation, hi_ap, src, ACT.Copy, after=after)
            lo = lo_lane.do(lo_lane.engine.tensor_tensor, lo_ap, src, hi_ap.bitcast(F32), ALU.subtract, after=[hi, *after])
            return [hi, lo]

        def last(*lanes):
            return [(l, l.count) for l in (lanes or (pe, act, dve, pool)) if l.count]

        bring()

        x_rows = T["x"].rearrange("a (i p) d -> (a p) i d", p=P)

        with ExitStack() as scope:
            x0 = sb("x0", [TT, D], ctx=scope)
            loads = [Loads(sem(f"x0_load{i}")) for i in range(TT)]
            got = [loads[i].start(sp, x0[:, i, :], x_rows[:, i, :]) for i in range(TT)]
            norm_to_columns(lambda i: x0[:, i, :], x0, lambda i: [got[i]], "norm_mix_pre", [], [])
        x0_free = last()

        ready_h = lambda k: h_ready[k]

        mixer = ExitStack()
        nsa_io = ExitStack()
        o_gla = sb("o_gla", [KD, S], ctx=mixer)
        kc_vc = sb("kc_vc", [2, S], ctx=nsa_io)
        v_hi = sb("v_hi", [TT, 2 * P], F32R, ctx=nsa_io)
        v_lo = sb("v_lo", [TT, 2 * P], F32R, ctx=nsa_io)
        nsa_g = sb("nsa_g", [TT, 24], ctx=nsa_io)
        gla = ExitStack()
        rr = sb("rr", [2, S], ctx=gla)
        v_gla = sb("v_gla", [TT, GLA_H * DV], ctx=gla)
        a_low = sb("a_low", [S], ctx=gla)
        w_alpha = sb("w_alpha", [GLA_H * DK], ctx=gla)
        reset = sb("reset", [S], ctx=gla)
        gs = sb("gs", [5, S], ctx=gla)
        qkd_of = sb("qkd", [2, 3, S], ctx=gla)
        decay_of = sb("decay", [2, NCH], ctx=gla)
        attn = junk
        kd_rows = sb("kd_rows", [TT, P], ctx=gla)
        states = sb("states", [NCH - 1, DV], ctx=gla)

        load_alpha = Loads(sem("load_alpha"))
        got_alpha = load_alpha.start(sp, w_alpha[0:RANK, :], T["gla_w_alpha2"][0], x0_free)
        zero_attn = pool.do(nc.gpsimd.memset, attn[:, :], 0.0, after=x0_free)
        m = pool.do(nc.gpsimd.memset, reset[:, :], 1.0, after=x0_free)
        set_reset = pool.do(nc.gpsimd.memset, reset[:, 0:S:CHUNK], 0.0, after=[m])
        zero_attn_and_reset = [zero_attn, set_reset]

        got = {}

        def keep(name):
            def evac(f, o, done):
                got[name, f] = act.do(nc.scalar.activation, name_to[name](f), o, ACT.Copy, after=[done])
                return [got[name, f]]
            return evac

        name_to = {"ga": lambda f: a_low[0:RANK, :]}
        act.wait(*x0_free)
        dve.wait(*x0_free)
        pool.wait(*x0_free)
        finish(by_column_tiles("gla a", h_hi, h_lo, ready_h, keep("ga"), 1, width=RANK))

        v_marks = []

        def evac_v(n, i, o, done):
            m = act.do(nc.scalar.activation, v_gla[:, i, 512 * n:512 * n + 512], o, ACT.Copy, after=[done])
            v_marks.append(m)
            return [m]

        finish(by_row_tiles("gla v", h_hi, h_lo, ready_h, evac_v, KD))

        def chunked(ap):
            return ap.rearrange("p (n c) -> p n c", c=CHUNK)

        free = {"gs": [], ("qkd", 0): [], ("qkd", 1): [], "attn": zero_attn_and_reset, "kd_rows": [], ("states", 0): [],
                ("states", 1): []}

        def gla_gates(h):
            bank, bank_free, readers = core_banks.take()
            m = pe.do(nc.tensor.matmul, bank[:, :], w_alpha[0:RANK, DK * h:DK * (h + 1)], a_low[0:RANK, :],
                                         start=True, stop=True, after=[got_alpha, got["ga", 0], *bank_free])
            x_, e_, b_ = gs[:, 0, :], gs[:, 1, :], gs[:, 2, :]
            x = dve.do(nc.vector.tensor_scalar, x_, bank[:, :], V("gla_b_alpha", h), None, ALU.add, after=[m, *free["gs"]])
            readers.append(x)
            m = dve.do(nc.vector.scalar_tensor_tensor, e_, x_, -1.0, x_, ALU.mult, ALU.min, after=[x])
            m = act.do(nc.scalar.activation, e_, e_, ACT.Exp, after=[m])
            m = act.do(nc.scalar.activation, e_, e_, ACT.Ln, bias=1.0, after=[m])
            m = dve.do(nc.vector.scalar_tensor_tensor, x_, x_, 0.0, e_, ALU.min, ALU.subtract, after=[m])
            b = dve.do(nc.vector.tensor_tensor_scan, b_, reset[:, :], x_, 0.0, ALU.mult, ALU.add, after=[m, set_reset])
            b_last = chunked(b_)[:, :, CHUNK - 1:CHUNK]
            m = dve.do(nc.vector.tensor_tensor, chunked(e_), b_last.broadcast_to([P, NCH, CHUNK]), chunked(b_),
                                                 ALU.subtract, after=[b])
            act.do(nc.scalar.activation, gs[:, 3, :], b_, ACT.Exp, scale=1 / TAU, after=[b])
            act.do(nc.scalar.activation, gs[:, 4, :], b_, ACT.Exp, scale=-1 / TAU)
            act.do(nc.scalar.activation, decay_of[:, h % 2, :], b_last.squeeze(), ACT.Exp, scale=1 / TAU, after=free["states", h % 2])
            return act.do(nc.scalar.activation, e_, e_, ACT.Exp, scale=1 / TAU, after=[m])

        qk_marks = {}

        def gla_front(h):
            gates = gla_gates(h)
            qkd = qkd_of[:, h % 2, :, :]
            yield

            def evac(f, o, done):
                if f == 0:
                    m = dve.do(nc.vector.scalar_tensor_tensor, qkd[:, 0, :], o, DK ** -0.5, gs[:, 3, :], ALU.mult, ALU.mult,
                               after=[done, gates, *free["qkd", h % 2]])
                    qk_marks[h] = [m]
                    return [m]
                m1 = dve.do(nc.vector.tensor_tensor, qkd[:, 1, :], o, gs[:, 4, :], ALU.mult, after=[done])
                m2 = dve.do(nc.vector.tensor_tensor, qkd[:, 2, :], o, gs[:, 1, :], ALU.mult)
                qk_marks[h] += [m1, m2]
                free["gs"] = [m2]
                return [m1, m2]

            yield from by_column_tiles(f"gla qk {h}", h_hi, h_lo, ready_h, evac, 2)

        def gla_head(h):
            qkd, decay, qk = qkd_of[:, h % 2, :, :], decay_of[:, h % 2, :], qk_marks[h]
            o_sq = qkd[:, 1:3, :]
            o_rs = qkd[:, 0, :]
            bank, bank_free, readers = core_banks.take()
            pe.wait(*bank_free, *qk)
            for p in range(TT):
                m = pe.do(nc.tensor.matmul, bank[:, P * p:P * p + P], qkd[:, 1, P * p:P * p + P],
                                                  qkd[:, 0, P * p:P * p + P], start=True, stop=True)
            mask = C("gla_mask").bitcast(U32).unsqueeze(1).broadcast_to([P, TT, P])
            attn_ready = dve.do(nc.vector.copy_predicated, attn[:, :].rearrange("p (a c) -> p a c", c=P), mask,
                                                            bank[:, :].rearrange("p (a c) -> p a c", c=P), after=[m, *free["attn"]])
            readers.append(attn_ready)
            yield
            bank, bank_free, readers = core_banks.take()
            pe.wait(*bank_free)
            for p in range(TT):
                m = pe.do(nc.tensor.transpose, bank[:, P * p:P * p + P], qkd[:, 2, P * p:P * p + P], ident)
            kd_ready = act.do(nc.scalar.activation, kd_rows[:, :, :].rearrange("p a c -> p (a c)"), bank[:, :],
                                                                ACT.Copy, after=[m, *free["kd_rows"]])
            readers.append(kd_ready)
            yield
            step = None
            state_marks = {}
            states_free = free["states", (h + 1) % 2]
            for n0 in range(0, NCH - 1, 4):
                some = range(n0, min(n0 + 4, NCH - 1))
                pair = [core_banks.take() for _ in range(2)]
                pe.wait(*pair[0][1], *pair[1][1], kd_ready, *v_marks)
                update = {}
                for n in some:
                    p, r = n // 2, CHUNK * (n % 2)
                    update[n] = pair[n % 2][0][:, DV * (p % 2):DV * (p % 2) + DV]
                    m = pe.do(nc.tensor.matmul, update[n], kd_rows[r:r + CHUNK, p, :],
                                                 v_gla[r:r + CHUNK, p, DV * h:DV * (h + 1)], start=True, stop=True)
                yield
                for n in some:
                    new = states[:, n, :]
                    if n == 0:
                        step = dve.do(nc.vector.tensor_copy, new, update[n], after=[m, *states_free])
                    else:
                        step = dve.do(nc.vector.scalar_tensor_tensor, new, states[:, n - 1, :], decay[:, n:n + 1], update[n], ALU.mult,
                                                                       ALU.add, after=[m, step])
                    pair[n % 2][2].append(step)
                    state_marks[n + 1] = step
                yield
            free["kd_rows"] = [m]
            outs = []
            for j in range(2):
                bank, bank_free, readers = core_banks.take()
                pe.wait(*bank_free, attn_ready)
                e0 = DV * h + P * j
                for p in range(TT):
                    pe.run(nc.tensor.matmul, bank[:, P * p:P * p + P], v_gla[:, p, e0:e0 + P], attn[:, P * p:P * p + P],
                        start=(p == 0), stop=False, skip_group_check=True)
                for n in range(1, NCH):
                    pe.wait(state_marks[n])
                    m = pe.do(nc.tensor.matmul, bank[:, CHUNK * n:CHUNK * (n + 1)], states[:, n - 1, P * j:P * j + P],
                        qkd[:, 0, CHUNK * n:CHUNK * (n + 1)], start=False, stop=(n == NCH - 1), skip_group_check=True)
                sq = act.do(nc.scalar.activation, o_sq[:, j, :], bank[:, :], ACT.Square, after=[m])
                outs.append((bank, readers, sq, m))
                yield
            free["attn"] = free["states", h % 2] = [m]
            bank, bank_free, readers = core_banks.take()
            pe.wait(*bank_free, outs[0][2], outs[1][2])
            for j in range(2):
                m = pe.do(nc.tensor.matmul, bank[:, :], C("ones"), o_sq[:, j, :], start=(j == 0),
                                                             stop=(j == 1))
            m = act.do(nc.scalar.activation, o_rs, bank[:, :], ACT.Ln, bias=eps_rms, scale=1.0 / DV, after=[m])
            readers.append(m)
            m = act.do(nc.scalar.activation, o_rs, o_rs, ACT.Exp, scale=-0.5, after=[m])
            for j in range(2):
                bank, readers, sq, om = outs[j]
                k = dve.do(nc.vector.scalar_tensor_tensor, o_gla[:, 2 * h + j, :], bank[:, :], V("gla_norm_g", j), o_rs, ALU.mult, ALU.mult, after=[m, om])
                readers += [sq, k]
            free["qkd", h % 2] = [k]
            return_marks["o_gla", h] = k
            yield

        return_marks = {}
        def evac_nsa_rows(n, i, o, done):
            m2 = act.do(nc.scalar.activation, nsa_g[:, i, :], o[:, 2 * P:2 * P + 24], ACT.Exp, scale=-1.0, after=[done])
            got["nv", i] = split(v_hi[:, i, :], v_lo[:, i, :], o[:, 0:2 * P], [done], dve)
            m = dve.do(nc.vector.tensor_scalar, nsa_g[:, i, :], nsa_g[:, i, :], 1.0, None, ALU.add, after=[m2])
            got["gate", i] = dve.do(nc.vector.reciprocal, nsa_g[:, i, :], nsa_g[:, i, :], after=[m])
            return [*got["nv", i], m2]

        def sigmoid(t, o, after):
            m1 = act.do(nc.scalar.activation, t, o, ACT.Exp, scale=-1.0, after=after)
            m = act.do(nc.scalar.activation, t, t, ACT.Ln, bias=1.0, after=[m1])
            return m1, act.do(nc.scalar.activation, t, t, ACT.Exp, scale=-1.0, after=[m])

        def evac_r(f0, rot_rr):
            def evac(f, o, done):
                f += f0
                t, t_free, t_readers = rot_rr.take()
                m1, m = sigmoid(t, o, [done, *t_free])
                m = dve.do(nc.vector.tensor_tensor, t, t, o, ALU.mult, after=[m])
                got["og", f] = pool.do(nc.gpsimd.tensor_tensor, o_gla[:, f, :], o_gla[:, f, :], t, ALU.mult,
                                       after=[m, return_marks["o_gla", f // 2]])
                t_readers.append(got["og", f])
                return [m1, m]
            return evac

        def evac_kc_vc(f, o, done):
            got["kc_vc", f] = act.do(nc.scalar.activation, kc_vc[:, f, :], o, ACT.Copy, after=[done])
            return [got["kc_vc", f]]

        def fills():
            yield from by_row_tiles("nsa v gate", h_hi, h_lo, ready_h, evac_nsa_rows, KD, halves=(0,))
            yield from by_column_tiles("nsa kc vc", h_hi, h_lo, ready_h, evac_kc_vc, 2)
            yield from by_column_tiles("gla r", h_hi, h_lo, ready_h, evac_r(0, Rotating([rr[:, i, :] for i in range(2)])), KD - 2)

        rest = fills()
        finish(gla_front(0))
        for h in range(GLA_H):
            front = gla_front(h + 1) if h + 1 < GLA_H else iter(())
            for n, _ in enumerate(gla_head(h)):
                next(rest if n in FILLS[h] else front, None)
            finish(front)
        finish(rest)
        gla_free = last()
        gla.close()

        nsa = ExitStack()
        mix_gates = sb("mix_gates", [EARLY, S], ctx=nsa_io)
        top = (nc.sbuf_usable_end - 16 * 1024) // 32 * 32
        q_hi = nc.alloc_sbuf_tensor_at("q_hi", [P, 4, S], F32R, offset=top)
        q_lo = nc.alloc_sbuf_tensor_at("q_lo", [P, 4, S], F32R, offset=top + 8 * 1024)
        on_hi, on_lo = q_hi, q_lo
        for lane in (act, dve, pool, pe, sp):
            lane.wait(*gla_free)
        kc_hi, kc_lo = sb("kc_hi", [32], F32R, ctx=nsa), sb("kc_lo", [32], F32R, ctx=nsa)
        v4 = sb("v4", [NG, REP * DH], ctx=nsa)
        k_hi, k_lo = (sb(f"k_{n}", [2, S], F32R, ctx=nsa) for n in ("hi", "lo"))

        def evac_q(f, o, done):
            scale = C("q_scale")[:, f:f + 1]
            hi = act.do(nc.scalar.activation, q_hi[:, f, :], o, ACT.Copy, scale=scale, after=[done])
            lo = dve.do(nc.vector.scalar_tensor_tensor, q_lo[:, f, :], o, scale, q_hi[:, f, :].bitcast(F32), ALU.mult,
                        ALU.subtract, after=[hi])
            got["nq", f] = [hi, lo]
            return [hi, lo]

        def evac_k(f, o, done):
            got["nk", f] = split(k_hi[:, f, :], k_lo[:, f, :], o, [done], dve)
            return got["nk", f]

        def late_fills():
            yield from by_column_tiles("nsa q", h_hi, h_lo, ready_h, evac_q, REP)
            yield from by_column_tiles("nsa ks kw", h_hi, h_lo, ready_h, evac_k, 2)
            yield from by_column_tiles("gla r", h_hi, h_lo, ready_h, evac_r(KD - 2, Rotating([rr_late[:, i, :] for i in range(2)])), 2)

        cmp_scope = ExitStack()
        rr_late = sb("rr_late", [2, S], ctx=cmp_scope)
        w1 = sb("w1", [CL, P], ctx=cmp_scope)
        pe_t = sb("pe_t", [CL], ctx=cmp_scope)
        w2 = sb("w2", [2, P], ctx=cmp_scope)
        windows = sb("windows", [CL, NCMP], ctx=cmp_scope)
        hid = sb("hid", [3, 32], ctx=cmp_scope)
        m0 = dve.do(nc.vector.memset, w1[:, :, :], 0.0)
        m1 = pool.do(nc.gpsimd.memset, w2[:, :, :], 0.0)
        zero_hid = pool.do(nc.gpsimd.memset, hid[:, 2, :], 0.0)
        zero_v4 = pool.do(nc.gpsimd.memset, v4[:, :, :], 0.0)
        w1_free, win_free, pe_free, w2_free = [m0], [], [], [m1]
        loads_c = {n: Loads(sem(f"load_{n}")) for n in ("w1a", "w1b", "pe", "w20", "w21")}
        kc_ready, v4_marks = [], []

        def compression(w1_free, w2_free, win_free, pe_free):
            for x, name in ((0, "k"), (1, "v")):
                w1_src = T[f"nsa_cmp_w1_{name}"][0].rearrange("(l d) o -> d l o", d=DH)
                g1 = loads_c["w1a"].start(sp, w1[0:DH, :, 0:DH], w1_src, w1_free)
                g2 = loads_c["w1b"].start(sp, w1[DH:P, :, DH:P], w1_src, w1_free)
                g3 = loads_c["pe"].start(sp, pe_t[:, :], T[f"pe_{name}"], pe_free)
                w2_got = [loads_c[f"w2{g}"].start(sp, w2[DH * g:DH * g + DH, x, DH * g:DH * g + DH],
                                                  T[f"nsa_cmp_w2_{name}"][0], w2_free) for g in range(NG)]
                src = kc_vc[:, x, :]
                for half in range(2):
                    blk = src.rearrange("p (n l) -> p l n", l=CS)[:, :, half:half + NCMP]
                    pe_b = pe_t[:, CS * half:CS * half + CS].unsqueeze(2).broadcast_to([P, CS, NCMP])
                    win_ready = dve.do(nc.vector.tensor_tensor, windows[:, CS * half:CS * half + CS, :], blk, pe_b, ALU.add, after=[g3, got["kc_vc", x], *win_free])
                pe_free = [win_ready]
                bank, bank_free, readers = core_banks.take()
                pe.wait(*bank_free, g1, g2, win_ready)
                for l in range(CL):
                    m = pe.do(nc.tensor.matmul, bank[:, 0:NCMP], w1[:, l, :], windows[:, l, :], start=(l == 0),
                              stop=(l == CL - 1))
                    if l % 4 == 3:
                        yield
                w1_free, win_free = [m], [m]
                yield
                m = act.do(nc.scalar.activation, hid[:, 0, 0:NCMP], bank[:, 0:NCMP], ACT.Exp, scale=-1.0, after=[m])
                m2 = dve.do(nc.vector.tensor_scalar, hid[:, 1, 0:NCMP], hid[:, 0, 0:NCMP], 1.0, None, ALU.add, after=[m])
                m2 = dve.do(nc.vector.reciprocal, hid[:, 1, 0:NCMP], hid[:, 1, 0:NCMP], after=[m2])
                m2 = dve.do(nc.vector.tensor_tensor, hid[:, 2, 0:NCMP], bank[:, 0:NCMP], hid[:, 1, 0:NCMP],
                                                                 ALU.mult, after=[m2, zero_hid])
                readers += [m, m2]
                yield
                bank, bank_free, readers = core_banks.take()
                pe.wait(*bank_free, m2, *w2_got)
                if x == 0:
                    m = pe.do(nc.tensor.matmul, bank[:, 0:32], w2[:, 0, :], hid[:, 2, :], start=True,
                                                            stop=True)
                    kc_ready[:] = split(kc_hi[:, :], kc_lo[:, :], bank[:, 0:32], [m], dve)
                    readers += kc_ready
                    w2_free = [m]
                else:
                    for r in range(REP):
                        m = pe.do(nc.tensor.matmul, bank[32 * r:32 * r + NCMP, 0:P], hid[:, 2, 0:NCMP],
                                                                     w2[:, 1, :], start=True, stop=True)
                    for r in range(REP):
                        v4_marks[:] = [dve.do(nc.vector.tensor_copy, v4[32 * r:32 * r + NCMP, :, DH * r:DH * r + DH],
                            bank[32 * r:32 * r + NCMP, 0:P].rearrange("p (g d) -> p g d", g=NG), after=[m, zero_v4])]
                    readers += v4_marks
                yield

        late = late_fills()
        for n, _ in enumerate(compression(w1_free, w2_free, win_free, pe_free)):
            if n % FILL_EVERY == 0 or n > 20:
                next(late, None)
        finish(late)
        cmp_free = last()
        cmp_scope.close()

        for lane in (act, dve, pool, pe):
            lane.wait(*cmp_free)
        probs = sb("probs", [2, REP, S], ctx=nsa)
        pt_hi, pt_lo = (sb(f"pt_{n}", [2, S], F32R, ctx=nsa) for n in ("hi", "lo"))
        sc = sb("nsa_stats", [3, 40], ctx=nsa)
        pc = kc_vc[:, 0, 0:NH * 32].rearrange("p (h n) -> p h n", n=32)
        pc_t = kc_vc[:, 0, NH * 32:NH * 32 + NG * P].rearrange("p (g q) -> p g q", q=P)
        o_rows = kc_vc[:, 1, :]
        zero_pc = pool.do(nc.gpsimd.memset, pc[:, :, :], 0.0)
        rot_probs = Rotating([probs[:, i, :, :] for i in range(2)])
        rot_pt = Rotating([(pt_hi[:, i, :], pt_lo[:, i, :]) for i in range(2)])
        fr = {"pc": [zero_pc], "pc_t": [], "o_rows": [], "stats": []}
        o_banks = Rotating(banks[6:8])
        score_banks = Rotating(banks[2:4])
        turn_banks = Rotating(banks[4:6])
        score_banks.readers, turn_banks.readers = core_banks.readers[0:2], core_banks.readers[2:4]
        o_banks.readers = core_banks.readers[4:6]
        cmp_seen = C("cmp_mask").rearrange("p (i n) -> p i n", n=32)
        cmp_dist = C("cmp_dist").rearrange("p (i n) -> p i n", n=NCMP)
        gates = nsa_g[:, :, :].rearrange("p i (h b) -> p i h b", b=3)
        held = {}

        def products(out_ap, a_hi, a_lo, b_hi, b_lo, start=True, stop=True):
            step = dict(skip_group_check=not start)
            pe.run(nc.tensor.matmul, out_ap, a_hi, b_hi, start=start, stop=False, **step)
            pe.run(nc.tensor.matmul, out_ap, a_hi, b_lo, start=False, stop=False, **step)
            return pe.do(nc.tensor.matmul, out_ap, a_lo, b_hi, start=False, stop=stop, **step)

        def over_keys(ap, n=NH):
            return ap.unsqueeze(2).broadcast_to([P, n, NCMP])

        def cmp_scores(i):
            p = pc[:, :, 0:NCMP]
            mx, sm, wt = sc[:, 0, 32:40], sc[:, 1, 32:40], sc[:, 2, 32:40]
            for g in range(NG):
                bank, bank_free, readers = score_banks.take()
                pe.wait(*bank_free, *kc_ready, *sum((got["nq", j] for j in range(REP)), []))
                rows = slice(DH * g, DH * g + DH)
                for j in range(REP):
                    m = products(bank[:, 32 * j:32 * (j + 1)], q_hi[rows, j, P * i:P * i + P], q_lo[rows, j, P * i:P * i + P],
                                 kc_hi[rows, :], kc_lo[rows, :])
                scores = bank[:, 0:REP * 32].rearrange("p (h n) -> p h n", n=32)[:, :, 0:NCMP]
                m = dve.do(nc.vector.tensor_tensor, pc[:, REP * g:REP * (g + 1), 0:NCMP], scores,
                           cmp_dist[:, i, :].unsqueeze(1).broadcast_to([P, REP, NCMP]), ALU.add, after=[m, *fr["pc"]])
                readers.append(m)
            yield
            m = dve.do(nc.vector.tensor_reduce, mx, p, AXX, ALU.max, after=[m])
            m = dve.do(nc.vector.tensor_tensor, p, p, over_keys(mx), ALU.subtract, after=[m])
            m = dve.do(nc.vector.tensor_tensor, p, p, over_keys(C("slopes")), ALU.mult, after=[m])
            m = act.do(nc.scalar.activation, p, p, ACT.Exp, after=[m])
            m = dve.do(nc.vector.tensor_reduce, sm, p, AXX, ALU.add, after=[m])
            m = dve.do(nc.vector.reciprocal, wt, sm, after=[m])
            m = dve.do(nc.vector.tensor_tensor, wt, wt, gates[:, i, :, 0], ALU.mult, after=[m, got["gate", i]])
            m = dve.do(nc.vector.tensor_tensor, p, p, over_keys(wt), ALU.mult, after=[m])
            held["pc", i] = dve.do(nc.vector.tensor_tensor, p, p,
                                   cmp_seen[:, i, 0:NCMP].unsqueeze(1).broadcast_to([P, NH, NCMP]), ALU.mult, after=[m])
            yield

        def cmp_values(i):
            held["o", i] = [o_banks.take() for _ in range(NG)]
            o_free = held["o", i][0][1] + held["o", i][1][1]
            bank, bank_free, readers = turn_banks.take()
            pe.wait(*bank_free, held["pc", i])
            for g in range(NG):
                m = pe.do(nc.tensor.transpose, bank[:, P * g:P * g + P],
                          pc[:, REP * g:REP * (g + 1), :].rearrange("p h n -> p (h n)"), ident)
            fr["pc"] = [m]
            t = dve.do(nc.vector.tensor_copy, pc_t[:, :, :].rearrange("p g q -> p (g q)"), bank[:, 0:2 * P],
                       after=[m, *fr["pc_t"]])
            readers.append(t)
            yield
            pe.wait(*o_free, *v4_marks, t, *sum((got["nv", n] for n in range(TT)), []))
            for g in range(NG):
                for j in range(REP):
                    m = pe.do(nc.tensor.matmul, held["o", i][g][0][0:DH, P * j:P * j + P],
                              v4[:, g, DH * j:DH * j + DH], pc_t[:, g, :], start=(j == 0), stop=False,
                              skip_group_check=True)
            fr["pc_t"] = [m]

        def key_scores(i, br, g):
            width = P * (i + 1)
            rows, qs = slice(DH * g, DH * g + DH), slice(P * i, P * i + P)
            pr, pr_free, pr_readers = rot_probs.take()
            c0 = 8 * rot_probs.at
            mx, mb, sm = sc[:, 0, c0:c0 + REP], sc[:, 0, c0 + REP:c0 + 2 * REP], sc[:, 1, c0:c0 + REP]
            wt = sc[:, 2, c0:c0 + REP]
            for j in range(REP):
                bank, bank_free, readers = score_banks.take()
                pe.wait(*bank_free, *got["nq", j], *got["nk", br])
                m = products(bank[:, 0:width], q_hi[rows, j, qs], q_lo[rows, j, qs], k_hi[rows, br, 0:width],
                             k_lo[rows, br, 0:width])
                m = dve.do(nc.vector.tensor_tensor_reduce, pr[:, j, 0:width], bank[:, 0:width],
                           C("dist")[:, S - width:S], 1.0, -3e38, ALU.add, ALU.max, mx[:, j:j + 1], after=[m, *pr_free])
                readers.append(m)
                m = dve.do(nc.vector.tensor_tensor, mb[:, j:j + 1], mx[:, j:j + 1],
                           C("minus_slopes")[:, REP * g + j:REP * g + j + 1], ALU.mult, after=[m])
                yield
                m = act.do(nc.scalar.activation, pr[:, j, 0:width], pr[:, j, 0:width], ACT.Exp,
                           scale=float(SLOPES[REP * g + j]), bias=mb[:, j:j + 1], accum_out=sm[:, j:j + 1], after=[m])
            yield
            m = dve.do(nc.vector.reciprocal, wt, sm, after=[m])
            m = dve.do(nc.vector.tensor_tensor, wt, wt, gates[:, i, REP * g:REP * (g + 1), 1 + br], ALU.mult, after=[m])
            ready = [dve.do(nc.vector.tensor_scalar, pr[:, j, 0:width], pr[:, j, 0:width], wt[:, j:j + 1], None, ALU.mult,
                            after=[m]) for j in range(REP)]
            held[i, br, g] = pr, pr_readers, ready

        def key_values(i, br, g):
            o_bank = held["o", i][g][0]
            pr, pr_readers, ready = held[i, br, g]
            turned = {}

            def turn(kb):
                bank, bank_free, readers = turn_banks.take()
                pe.wait(*bank_free, *ready)
                for j in range(REP):
                    m = pe.do(nc.tensor.transpose, bank[:, P * j:P * j + P], pr[:, j, P * kb:P * kb + P], ident)
                (hi, lo), pt_free, pt_readers = rot_pt.take()
                t = split(hi, lo, bank[:, :], [m, *pt_free], dve)
                readers += t
                turned[kb] = hi, lo, pt_readers, t
                return m

            m = turn(0)
            for kb in range(i + 1):
                if kb < i:
                    m = turn(kb + 1)
                yield
                hi, lo, pt_readers, t = turned[kb]
                pe.wait(*t)
                vs = slice(P * br + DH * g, P * br + DH * g + DH)
                last_one = br == 1 and kb == i
                held["pv", i] = products(o_bank[0:DH, :], v_hi[:, kb, vs], v_lo[:, kb, vs], hi, lo,
                                         start=False, stop=last_one)
                pt_readers.append(held["pv", i])
            pr_readers.append(m)

        def tile_out(i):
            qs = slice(P * i, P * i + P)
            got["on", i] = []
            for g, (o_bank, _, o_readers) in enumerate(held["o", i]):
                rows = slice(DH * g, DH * g + DH)
                src = o_bank[0:DH, :].rearrange("p (f q) -> p f q", f=REP)
                marks = split(on_hi[rows, :, qs], on_lo[rows, :, qs], src, [held["pv", i]], dve)
                o_readers += marks
                got["on", i] += marks
            yield

        def nsa_core():
            order = [(i, b, g) for i in range(TT) for b, g in ((None, 0), (0, 0), (0, 1), (1, 0), (1, 1))]

            def back(i, b, g):
                if b is None:
                    yield from cmp_values(i)
                else:
                    yield from key_values(i, b, g)
                    if (b, g) == (1, 1):
                        yield from tile_out(i)

            behind = iter(())
            for i, b, g in order:
                front = cmp_scores(i) if b is None else key_scores(i, b, g)
                for _ in front:
                    next(behind, None)
                    yield
                yield from behind
                behind = back(i, b, g)
            yield from behind

        def evac_mix_gate(f, o, done):
            m, got["mix", 0, f] = sigmoid(mix_gates[:, f, :], o, [done])
            return [m]

        gate_tiles = by_column_tiles("merge gates", h_hi, h_lo, ready_h, evac_mix_gate, EARLY)
        for n, _ in enumerate(nsa_core()):
            if n % GATE_EVERY == 0:
                next(gate_tiles, None)
        finish(gate_tiles)
        core_banks.readers[:] = score_banks.readers + turn_banks.readers + o_banks.readers
        nsa_free = last()
        assert nc.sbuf_base <= top
        nsa.close()

        merge = ExitStack()
        og_hi = sb("og_hi", [KD, S], F32R, ctx=merge)
        og_lo = sb("og_lo", [KD, S], F32R, ctx=merge)
        for lane in (act, dve, pool, pe):
            lane.wait(*nsa_free)
        og_ready = [split(og_hi[:, f, :], og_lo[:, f, :], o_gla[:, f, :], [got["og", f]], pool) for f in range(KD)]
        on_ready = sum((got["on", i] for i in range(TT)), [])
        mixed_marks = []
        gla_gates = sb("gla_gates", [2, S], ctx=merge)
        late_gates = [gla_gates, kc_vc]
        late_free = {(w, f): [] for w in range(2) for f in range(2)}

        def merge_all():
            gla_part = {}

            def late_gate(which, j):
                def evac(f, o, done):
                    m, got["mix", which, j + f] = sigmoid(late_gates[which][:, f, :], o, [done, *late_free[which, f]])
                    return [m]
                return by_column_tiles("merge gates", h_hi, h_lo, ready_h, evac, 2)

            def evac_gla(j):
                def evac(f, o, done):
                    gate = mix_gates[:, j + f, :] if j < EARLY else gla_gates[:, f, :]
                    m = dve.do(nc.vector.tensor_tensor, o_gla[:, j + f, :], o, gate, ALU.mult,
                               after=[done, got["mix", 0, j + f], *og_ready[j + f]])
                    gla_part[j + f] = m
                    late_free[0, f] = [m]
                    return [m]
                return evac

            def evac_nsa(j):
                def evac(f, o, done):
                    t = kc_vc[:, f, :]
                    m = dve.do(nc.vector.tensor_tensor, t, o, t, ALU.mult, after=[done, got["mix", 1, j + f]])
                    s = dve.do(nc.vector.tensor_tensor, o_gla[:, j + f, :], o_gla[:, j + f, :], t, ALU.add,
                               after=[m, gla_part[j + f]])
                    mixed_marks.append(s)
                    late_free[1, f] = [s]
                    return [m]
                return evac

            for j in range(0, KD, 2):
                if j >= EARLY:
                    yield from late_gate(0, j)
                yield from by_column_tiles("proj gla", og_hi, og_lo, lambda k: og_ready[k], evac_gla(j), 2)
                yield from late_gate(1, j)
                yield from by_column_tiles("proj nsa", on_hi, on_lo, lambda k: on_ready, evac_nsa(j), 2, nk=4)

        finish(merge_all())
        h_free = [(pe, pe.count)]
        for f in range(KD):
            h_ready[f] = split(h_hi[:, f, :], h_lo[:, f, :], o_gla[:, f, :], [mixed_marks[f], *h_free],
                               dve if f % 2 else pool)
        merge_free = last()
        assert nc.sbuf_base <= top
        merge.close()
        nsa_io.close()
        mixer.close()

        x1 = sb("x1", [TT, D])
        gain_row = sb("gain_row", [D])
        load_gain = Loads(sem("load_gain"))
        for lane in (act, dve, pool, sp):
            lane.wait(*merge_free)
        load_x1 = Loads(sem("load_x1"))
        got_x1 = load_x1.start(sp, x1[:, :, :], x_rows)

        def load_gain_row(src, after):
            return load_gain.start(sp, gain_row[:, :], src.partition_broadcast(P), after)

        def residual(acc, ready, got_gain, x_ready):
            rs = rstd_rows(lambda i: acc[:, i, :], ready, [])
            marks = []
            for i in range(TT):
                m = dve.do(nc.vector.scalar_tensor_tensor, acc[:, i, :], acc[:, i, :], stat[:, 6, i:i + 1],
                                                                 gain_row[:, :], ALU.mult, ALU.mult, after=[rs[i], got_gain])
                marks.append([dve.do(nc.vector.tensor_tensor, x1[:, i, :], x1[:, i, :], acc[:, i, :], ALU.add, after=[m, *x_ready])])
            return marks

        with ExitStack() as scope:
            acc = sb("acc_mix", [TT, D], ctx=scope)
            acc_marks = {}

            def evac_out(n, i, o, done):
                m = act.do(nc.scalar.activation, acc[:, i, 512 * n:512 * n + 512], o, ACT.Copy, after=[done])
                acc_marks[n, i] = m
                return [m]

            got_gain = load_gain_row(T["norm_mix_post"][0], [])
            finish(by_row_tiles("out", h_hi, h_lo, ready_h, evac_out, KD))
            h_free = [(pe, pe.count)]
            x1_marks = residual(acc, lambda i: [acc_marks[0, i], acc_marks[1, i]], got_gain, [got_x1])
            norm_to_columns(lambda i: x1[:, i, :], acc, lambda i: x1_marks[i], "norm_ffn_pre", h_free, [])
        acc_free = last()

        def ffn(tag, groups, evac_pair, n_up, free):
            scope = ExitStack()
            acc = sb(f"acc{tag}", [TT, D], ctx=scope)
            most = max(n for _, n in groups)
            f_hi = sb(f"f_hi{tag}", [2, most, S], F32R, ctx=scope)
            f_lo = sb(f"f_lo{tag}", [2, most, S], F32R, ctx=scope)
            ft = sb(f"ft{tag}", [2, S], ctx=scope)
            rot = Rotating([ft[:, i, :] for i in range(2)])
            for lane in (act, dve, pool, sp):
                lane.wait(*free)
            f_free, f_ready, acc_ready = [[], []], {}, {}

            def up(g):
                t0, nt = groups[g]
                b = g % 2
                state_ = {}

                def evac(f, o, done):
                    t = f // n_up
                    if f % n_up == 0:
                        state_["s"] = rot.take()
                    s, s_free, s_readers = state_["s"]
                    marks, r = evac_pair(f % n_up, s, s_free, o, done, f_hi[:, b, t, :], f_lo[:, b, t, :], f_free[b],
                                         s_readers)
                    if marks:
                        f_ready[g, t] = marks
                    return r

                yield from by_column_tiles(f"up {tag}", h_hi, h_lo, ready_h, evac, nt * n_up)

            def down(g):
                t0, nt = groups[g]
                b = g % 2

                def evac(n, i, o, done):
                    a = acc[:, i, 512 * n:512 * n + 512]
                    if g == 0:
                        m = dve.do(nc.vector.tensor_copy, a, o, after=[done])
                    else:
                        m = dve.do(nc.vector.tensor_tensor, a, a, o, ALU.add, after=[done, acc_ready[n, i]])
                    acc_ready[n, i] = m
                    return [m]

                yield from by_row_tiles(f"down {tag}", f_hi[:, b, :, :], f_lo[:, b, :, :], lambda k: f_ready[g, k], evac, nt)
                f_free[b] = [(pe, pe.count)]

            for g in range(len(groups) + 1):
                if g < len(groups):
                    finish(up(g))
                if g:
                    finish(down(g - 1))
            return scope, acc, lambda i: [acc_ready[0, i], acc_ready[1, i]]

        def swiglu(which, s, s_free, o, done, hi, lo, free, s_readers):
            if which == 0:
                m = act.do(nc.scalar.activation, s, o, ACT.Silu, after=[done, *s_free])
                s_readers.append(m)
                return None, [m]
            m = dve.do(nc.vector.tensor_tensor, s, s, o, ALU.mult, after=[done, *s_readers, *s_free])
            a = act.do(nc.scalar.activation, hi, s, ACT.Copy, after=[m, *free])
            b = dve.do(nc.vector.tensor_tensor, lo, s, hi.bitcast(F32), ALU.subtract, after=[a, *free])
            s_readers[:] = [m, a, b]
            return [a, b], [m]

        def relu2(which, s, s_free, o, done, hi, lo, free, s_readers):
            r = act.do(nc.scalar.activation, s, o, ACT.Relu, after=[done, *s_free])
            m = dve.do(nc.vector.tensor_tensor, s, s, s, ALU.mult, after=[r, *s_free])
            a = act.do(nc.scalar.activation, hi, s, ACT.Copy, after=[m, *free])
            b = dve.do(nc.vector.tensor_tensor, lo, s, hi.bitcast(F32), ALU.subtract, after=[a, *free])
            s_readers[:] = [m, a, b]
            return [a, b], [r]

        got_gain = load_gain_row(T["norm_ffn_post"][0], last(dve))
        scope, acc, acc_r = ffn("1", FFN1_GROUPS, swiglu, 2, acc_free)
        h_free = [(pe, pe.count)]
        exp_ln_tables()
        x1_marks = residual(acc, acc_r, got_gain, [])
        norm_to_columns(lambda i: x1[:, i, :], acc, lambda i: x1_marks[i], "g_attn_2", h_free, [])
        b2_free = last()
        scope.close()

        scope = ExitStack()
        cat = sb("cat", [KD, S], ctx=scope)
        q2 = sb("q2", [3, S], ctx=scope)
        k2 = sb("k2", [3, S], ctx=scope)
        qk2_free = {f: [] for f in range(4)}
        v2 = sb("v2", [TT, 512], ctx=scope)
        ua = sb("ua", [2, KA - 1 + S], ctx=scope)
        gb = sb("gb", [2, KB - 1 + S], ctx=scope)
        wa = C("cmp_dist")[:, 0:2 * KA].rearrange("p (f k) -> p f k", k=KA)
        wb = C("cmp_mask")[:, 0:2 * KB].rearrange("p (f k) -> p f k", k=KB)
        for lane in (act, dve, pool, sp):
            lane.wait(*b2_free)
        load_wa, load_wb = Loads(sem("load_wa")), Loads(sem("load_wb"))
        got_wa = load_wa.start(sp, C("cmp_dist")[:, 0:2 * KA], T["taps_a"])
        got_wb = load_wb.start(sp, C("cmp_mask")[:, 0:2 * KB], T["taps_b"])
        zero_ua = pool.do(nc.gpsimd.memset, ua[:, :, 0:KA - 1], 0.0)
        zero_gb = pool.do(nc.gpsimd.memset, gb[:, :, 0:KB - 1], 0.0)

        def evac_v2(n, i, o, done):
            got["v2", i] = act.do(nc.scalar.activation, v2[:, i, :], o, ACT.Copy, after=[done])
            return [got["v2", i]]

        def evac_qk2(f, o, done):
            slot, after = f // 2 % 3, [done, *(qk2_free[f // 2 - 3] if f >= 6 else [])]
            if f % 2 == 0:
                m = act.do(nc.scalar.activation, q2[:, slot, :], o, ACT.Copy, scale=DH ** -0.5, after=after)
            else:
                m = act.do(nc.scalar.activation, k2[:, slot, :], o, ACT.Copy, after=after)
            got["qk2", f] = m
            return [m]

        def evac_glu(f, o, done):
            g = gb[:, f % 2, KB - 1:KB - 1 + S]
            if f < 2:
                got["glu", f] = act.do(nc.scalar.activation, g, o, ACT.Copy, after=[done])
                return [got["glu", f]]
            t, t_free, t_readers = rot_ct.take()
            m1, m = sigmoid(t, o, [done, *t_free])
            m = dve.do(nc.vector.tensor_tensor, g, g, t, ALU.mult, after=[m, got["glu", f - 2]])
            t_readers.append(m)
            got["gb", f - 2] = m
            return [m1]

        def evac_acah(f, o, done):
            u = ua[:, f % 2, KA - 1:KA - 1 + S]
            if f < 2:
                got["ac", f] = act.do(nc.scalar.activation, u, o, ACT.Copy, after=[done])
                return [got["ac", f]]
            got["ua", f - 2] = dve.do(nc.vector.tensor_tensor, u, u, o, ALU.mult, after=[done, got["ac", f - 2]])
            return [got["ua", f - 2]]

        def conv(name, out_ap, src, w, taps, after, bias_ap=None):
            more = [ALU.add] if bias_ap is not None else []
            m = dve.do(nc.vector.tensor_scalar, out_ap, src[:, 0:S], w[:, 0:1], bias_ap, ALU.mult, *more, after=after)
            for j in range(1, taps):
                yield
                m = dve.do(nc.vector.scalar_tensor_tensor, out_ap, src[:, j:j + S], w[:, j:j + 1], out_ap, ALU.mult,
                           ALU.add, after=[m])
            got[name] = m
            yield

        def evac_ab(f, o, done):
            got["cat", f] = dve.do(nc.vector.tensor_tensor, cat[:, f, :], cat[:, f, :], o, ALU.mult, after=[done, got["conv_a", f]])
            return [got["cat", f]]

        rot_ct = Rotating([junk[:, :], gain_row[:, 0:S], gain_row[:, S:2 * S], C("dist")])

        def conv_b():
            for f in range(2):
                yield from conv(("conv_b", f), cat[:, 2 + f, :], gb[:, f, :], wb[:, f, :], KB,
                                [got["gb", f], got_wb, zero_gb], V("b_conv_b_2", f))

        def norm_b():
            bank, bank_free, readers = core_banks.take()
            pe.wait(*bank_free, got["conv_b", 0], got["conv_b", 1])
            for f in range(2):
                m = pe.do(nc.tensor.matmul, bank[:, :], C("ones"), cat[:, 2 + f, :], start=(f == 0),
                                                             stop=(f == 1))
            sq = []
            for f in range(2):
                d = dve.do(nc.vector.scalar_tensor_tensor, cat[:, 2 + f, :], bank[:, :], -1.0 / CW, cat[:, 2 + f, :], ALU.mult, ALU.add, after=[m])
                readers.append(d)
                sq.append(act.do(nc.scalar.activation, gb[:, f, 0:S], cat[:, 2 + f, :], ACT.Square, after=[d]))
            yield
            bank, bank_free, readers = core_banks.take()
            pe.wait(*bank_free, *sq)
            for f in range(2):
                m = pe.do(nc.tensor.matmul, bank[:, :], C("ones"), gb[:, f, 0:S], start=(f == 0),
                                                             stop=(f == 1))
            t, t_free, t_readers = rot_ct.take()
            m = act.do(nc.scalar.activation, t, bank[:, :], ACT.Ln, bias=eps_ln, scale=1.0 / CW, after=[m, *t_free])
            readers.append(m)
            m = act.do(nc.scalar.activation, t, t, ACT.Exp, scale=-0.5, after=[m])
            yield
            for f in range(2):
                c = cat[:, 2 + f, :]
                k = dve.do(nc.vector.tensor_tensor, c, c, t, ALU.mult, after=[m, d])
                k = dve.do(nc.vector.tensor_scalar, c, c, V("ln_b_g_2", f), V("ln_b_b_2", f), ALU.mult,
                                                               ALU.add, after=[k])
                got["cat", 2 + f] = act.do(nc.scalar.activation, c, c, ACT.Silu, after=[k])
            exp_ln_tables()
            yield
            t_readers.append(k)

        widths = [S - P * j for j in range(TT)]
        units = [[(2, 0), (3, widths[2])], [(1, 0)], [(0, 0)]]
        n_units = len(units)
        u_width = [sum(widths[j] for j, _ in u) for u in units]
        u_start = [sum(u_width[:n]) for n in range(n_units)]
        start_of = {j: u_start[n] + c for n, u in enumerate(units) for j, c in u}
        total = sum(widths)
        at = sb("at", [total], ctx=scope)
        sp_hi = sb("sp_hi", [2, total], F32R, ctx=scope)
        sp_lo = sb("sp_lo", [2, total], F32R, ctx=scope)
        z_banks = Rotating(banks[2:8])
        y_bank, linear_bank = banks[1], banks[0]
        z_held, sp_marks, a_marks, y_free = {}, {}, {}, []
        at_free = [[] for _ in units]
        sp_free = [[], []]

        def softplus(h):
            f, r = h // 2, DH * (h % 2)
            for n, unit in enumerate(units):
                w = u_width[n]
                bank, bank_free, readers = z_banks.take()
                z_held[h, n] = bank, readers
                pe.wait(*bank_free, got["qk2", 2 * f], got["qk2", 2 * f + 1])
                for c, (j, at_col) in enumerate(unit):
                    m = pe.do(nc.tensor.matmul, bank[:, at_col:at_col + widths[j]], k2[r:r + DH, f % 3, P * j:P * j + P],
                              q2[r:r + DH, f % 3, P * j:S], start=(c == 0), stop=False, skip_group_check=True)
                qk2_free[f] = [m]
                buf, t_free, t_readers = rot_ct.take()
                t = buf[:, 0:w]
                m = act.do(nc.scalar.activation, t, bank[:, 0:w], ACT.Abs, after=[m, *t_free])
                m = act.do(nc.scalar.activation, t, t, ACT.Exp, scale=-1.0, after=[m])
                m = act.do(nc.scalar.activation, t, t, ACT.Ln, bias=1.0, after=[m])
                yield
                z_read = dve.do(nc.vector.scalar_tensor_tensor, t, bank[:, 0:w], 0.0, t, ALU.max, ALU.add, after=[m])
                for j, at_col in unit:
                    d = t[:, at_col:at_col + P]
                    m = dve.do(nc.vector.tensor_tensor, d, d, C("before"), ALU.mult, after=[z_read])
                cs = slice(u_start[n], u_start[n] + w)
                marks = split(sp_hi[:, h % 2, cs], sp_lo[:, h % 2, cs], t, [m, *sp_free[h % 2]], dve)
                t_readers += marks
                sp_marks[h, n] = [z_read, *marks]
                yield

        def stick(h):
            f, r = h // 2, DH * (h % 2)
            sp = [sp_hi[:, h % 2, :], sp_lo[:, h % 2, :]]

            def values(n):
                pe.wait(a_marks[h, n])
                for j, _ in units[n]:
                    a = at[:, start_of[j]:start_of[j] + widths[j]]
                    m = pe.do(nc.tensor.matmul, y_bank[r:r + DH, P * j:S], v2[:, j, DH * h:DH * h + DH], a,
                              start=(n == 0 and j == units[0][0][0]), stop=(j == 0), skip_group_check=True,
                              after=[got["v2", j]])
                at_free[n] = [m]
                return m

            for n, unit in enumerate(units):
                bank, readers = z_held[h, n]
                pe.wait(*sp_marks[h, n], consts_r)
                for j, c0 in unit:
                    for i in range(j, TT):
                        c = c0 + P * (i - j)
                        for src in sp:
                            pe.run(nc.tensor.matmul, bank[:, c:c0 + widths[j]], (upper_r if i == j else ones_r)[:, :],
                                   src[:, start_of[i]:start_of[i] + widths[i]], start=False, stop=False,
                                   skip_group_check=True)
                    m = pe.do(nc.tensor.matmul, bank[:, c0:c0 + P], ident_r[:, :], block_r[:, :], start=False,
                              stop=True, skip_group_check=True)
                a = at[:, u_start[n]:u_start[n] + u_width[n]]
                a_marks[h, n] = act.do(nc.scalar.activation, a, bank[:, 0:u_width[n]], ACT.Exp, after=[m, *at_free[n]])
                readers += [a_marks[h, n], sp_marks[h, n][0]]
                yield
                if n == 1 and h % 2 == 0:
                    pe.wait(*y_free)
                if n:
                    values(n - 1)
                    yield
            sp_free[h % 2] = [m]
            m = values(n_units - 1)
            if h % 2:
                got["cat", 4 + f] = act.do(nc.scalar.activation, cat[:, 4 + f, :], y_bank[:, :], ACT.Copy, after=[m])
                y_free[:] = [got["cat", 4 + f]]
            yield

        finish(by_column_tiles("glu 2", h_hi, h_lo, ready_h, evac_glu, 4))
        on_vector = conv_b()

        def with_conv(gen, taps):
            for _ in gen:
                for _ in range(taps):
                    next(on_vector, None)
                yield

        finish(with_conv(by_row_tiles("v 2", h_hi, h_lo, ready_h, evac_v2, KD, halves=(0,)), 3))
        tiles_qk = by_column_tiles("qk 2", h_hi, h_lo, ready_h, evac_qk2, 8)
        for _ in range(4):
            next(tiles_qk)
            for _ in range(3):
                next(on_vector, None)

        def rest():
            for _ in range(2):
                yield next(tiles_qk)
            yield from by_column_tiles("ac ah 2", h_hi, h_lo, ready_h, evac_acah, 4)
            for _ in range(2):
                yield next(tiles_qk)
            for f in range(2):
                finish(conv(("conv_a", f), cat[:, f, :], ua[:, f, :], wa[:, f, :], KA, [got["ua", f], got_wa, zero_ua]))
            yield from by_column_tiles("ab 2", h_hi, h_lo, ready_h, evac_ab, 2)

        linear_readers = list(linear_banks.readers)
        y_free += linear_readers[1]
        linear_banks.bufs, linear_banks.at, linear_banks.readers = [linear_bank], -1, [linear_readers[0]]
        z_banks.readers = core_banks.readers
        fills2 = rest()
        step = 0
        finish(softplus(0))
        for h in range(SBH):
            ahead = softplus(h + 1) if h + 1 < SBH else iter(())
            for _ in stick(h):
                next(ahead, None)
                if step % FILL2_EVERY == 0:
                    next(fills2, None)
                step += 1
                for _ in range(2):
                    next(on_vector, None)
            finish(ahead)
        finish(fills2, on_vector)
        linear_banks.bufs, linear_banks.at = banks[0:2], -1
        linear_banks.readers = [linear_banks.readers[0], list(y_free)]
        core_banks.readers[:] = z_banks.readers
        core_banks.at = -1
        h_free = [(pe, pe.count)]
        finish(norm_b())
        for f in range(KD):
            h_ready[f] = split(h_hi[:, f, :], h_lo[:, f, :], cat[:, f, :], [got["cat", f], *h_free],
                               dve if f % 2 else pool)
        cat_free = last()
        scope.close()

        with ExitStack() as scope:
            hs = sb("hs", [TT, D], ctx=scope)
            for lane in (dve, pool, act):
                lane.wait(*cat_free)
            x1_last = {}

            def evac_res(n, i, o, done):
                a = x1[:, i, 512 * n:512 * n + 512]
                m = dve.do(nc.vector.tensor_tensor, a, a, o, ALU.add, after=[done])
                x1_last[n, i] = m
                return [m]

            finish(by_row_tiles("out 2", h_hi, h_lo, ready_h, evac_res, KD))
            h_free = [(pe, pe.count)]
            norm_to_columns(lambda i: x1[:, i, :], hs, lambda i: [x1_last[0, i], x1_last[1, i]], "g_ffn_2", h_free, [])
        hs_free = last()

        got_gain = load_gain_row(T["g_final_2"], last(dve, act))
        scope, acc, acc_r = ffn("2", FFN2_GROUPS, relu2, 1, hs_free)
        sums = [dve.do(nc.vector.tensor_tensor, x1[:, i, :], x1[:, i, :], acc[:, i, :], ALU.add, after=acc_r(i))
                for i in range(TT)]
        rs = rstd_rows(lambda i: x1[:, i, :], lambda i: [sums[i]], [])
        out_rows = out.rearrange("a (i p) d -> (a p) i d", p=P)
        stored = Loads(sem("stored"))
        for i in range(TT):
            m = dve.do(nc.vector.scalar_tensor_tensor, acc[:, i, :], x1[:, i, :], stat[:, 6, i:i + 1],
                                                             gain_row[:, :], ALU.mult, ALU.mult, after=[rs[i], got_gain])
            end = stored.start(sp, out_rows[:, i, :], acc[:, i, :], [m])
        sp.wait(end)
        scope.close()
        assert state["used"] == len(chunks)

        block = outer.enter_context(nc.Block())

        @block.sync
        def _(e):
            sp.write()

        @block.tensor
        def _(e):
            pe.write()

        @block.scalar
        def _(e):
            act.write()

        @block.vector
        def _(e):
            dve.write()

        @block.gpsimd
        def _(e):
            pool.write()


def columns_of(v):
    return np.reshape(v, (-1, P)).T


def lay_out(inputs):
    parts = []
    for _, name, row0, nk, c in plan():
        w = inputs[name][0]
        if name == "w_proj_nsa":
            w = w[NSA_ROWS]
        w = w[row0:row0 + P * nk][:, c]
        parts.append(np.ascontiguousarray(w.reshape(nk, P, len(c)).transpose(1, 0, 2)).reshape(-1))
    return np.concatenate(parts)


_DIRECT = ["x", "gla_w_alpha2", "nsa_cmp_w1_k", "nsa_cmp_w2_k", "nsa_cmp_w1_v", "nsa_cmp_w2_v", "norm_mix_post",
           "norm_ffn_post", "g_final_2"]


def kernel(**inputs):
    import concourse.bacc as _bacc
    from concourse.bass_utils import run_bass_kernel_spmd as _run

    inputs = {k: np.asarray(v) for k, v in inputs.items()}
    nc = _bacc.Bacc("TRN2", target_bir_lowering=False, num_devices=1)
    arrays = {}

    def give(name, a):
        a = np.ascontiguousarray(a)
        arrays[f"in_{name}"] = a
        return nc.dram_tensor(f"in_{name}", a.shape, mybir.dt.from_np(a.dtype), kind="ExternalInput").ap()

    T = {name: give(name, inputs[name]) for name in _DIRECT}
    for n in "kv":
        T[f"pe_{n}"] = give(f"pe_{n}", np.concatenate([inputs[f"nsa_cmp_pe_{n}"][0].T] * NG))
    for n in "ab":
        w = inputs[f"w_conv_{n}_2"][0]
        T[f"taps_{n}"] = give(f"taps_{n}", w.reshape(len(w), 2, P).transpose(2, 1, 0).reshape(P, -1))
    wstream = give("wstream", lay_out(inputs))
    vectors = give("vectors", np.concatenate([columns_of(inputs[n]) for n, _ in _vec], axis=1))
    consts = give("constants", constants())
    out = nc.dram_tensor("out", (1, S, D), F32, kind="ExternalOutput").ap()
    program(nc, T, wstream, vectors, consts, out)
    r = _run(nc, [arrays], core_ids=[0])
    return r.results[0]["out"]
```

```python
from contextlib import ExitStack

import numpy as np

import concourse.bass as bass
from concourse import mybir

F32 = mybir.dt.float32
F32R = mybir.dt.float32r
U32 = mybir.dt.uint32
ALU = mybir.AluOpType
ACT = mybir.ActivationFunctionType
AXX = mybir.AxisListType.X

P = 128
S = 512
D = 1024
TT = S // P
KD = D // P
RMS_EPS = 1e-6
LN_EPS = 1e-5
NEG = -1e30

GLA_H, DK, DV, RANK, TAU, CHUNK = 4, 128, 256, 16, 16.0, 64
NCH = S // CHUNK
NH, NG, DH = 8, 2, 64
REP = NH // NG
CL, CS = 32, 16
NCMP = (S - CL) // CS + 1
D_FF, D_FF2 = 2816, 4096
CW, KA, KB = 256, 3, 31
SLOPES = 2.0 ** (-8.0 * (np.arange(NH) + 1) / NH)
SBH = 8

FILLS = [(1, 3, 5, 7), (1, 3, 5), (1, 3, 5), (0, 2)]
FILL_EVERY = 2

EARLY = 4
SCALED_BY_ACT = (3,)
LEAD = 2
GATE_EVERY = 12

FILL2_EVERY = 3

_w = dict(gq=512, gk=512, gv=1024, gr=1024, ga=16, nq=512, kc=128, vc=128, ks=128, vs=128, kw=128,
          vw=128, gate=24, mg=1024, mn=1024)
OFF1 = dict(zip(_w, np.cumsum([0] + list(_w.values()))[:-1].tolist()))
_w2 = dict(ab=256, ac=256, ah=256, glu=512, q=512, k=512, v=512)
OFF2 = dict(zip(_w2, np.cumsum([0] + list(_w2.values()))[:-1].tolist()))

CH = 2048
HALF = CH // 2


def cols(start, n):
    return list(range(start, start + n))


def groups_of(n, sizes):
    out, at = [], 0
    for s in sizes:
        out.append((at, s))
        at += s
    assert at == n
    return out


NSA_ROWS = sum((cols(DH * j, DH) + cols(DH * (REP + j), DH) for j in range(REP)), [])
FFN1_GROUPS = groups_of(D_FF // P, [6, 6, 5, 5])
FFN2_GROUPS = groups_of(D_FF2 // P, [6, 6, 5, 5, 5, 5])


def plan():
    out = []

    def by_column(layer, w, c, nk=KD):
        n = CH // nk
        for a in range(0, len(c), n):
            out.append((layer, w, 0, nk, c[a:a + n]))

    def by_row(layer, w, c, row0, nk):
        for a in range(0, nk, 4):
            out.append((layer, w, row0 + a * P, min(4, nk - a), c))

    o = OFF1
    by_column("gla a", "w_in", cols(o["ga"], 16))
    for n in range(2):
        by_row("gla v", "w_in", cols(o["gv"] + 512 * n, 512), 0, KD)

    def gla_qk(h):
        by_column(f"gla qk {h}", "w_in", cols(o["gq"] + DK * h, DK) + cols(o["gk"] + DK * h, DK))

    nq = [sum((cols(o["nq"] + DH * j, DH) + cols(o["nq"] + DH * (REP + j), DH) for j in pair), [])
          for pair in ((0, 1), (2, 3))]
    gla_qk(0)
    by_row("nsa v gate", "w_in", cols(o["vs"], P) + cols(o["vw"], P) + cols(o["gate"], 24), 0, KD)
    gla_qk(1)
    by_column("nsa kc vc", "w_in", cols(o["kc"], P) + cols(o["vc"], P))
    by_column("gla r", "w_in", cols(o["gr"], 2 * P))
    gla_qk(2)
    by_column("gla r", "w_in", cols(o["gr"] + 2 * P, 2 * P))
    gla_qk(3)
    by_column("gla r", "w_in", cols(o["gr"] + 4 * P, 2 * P))
    by_column("nsa ks kw", "w_in", cols(o["ks"], P) + cols(o["kw"], P))
    by_column("gla r", "w_in", cols(o["gr"] + D - 2 * P, 2 * P))
    by_column("nsa q", "w_in", nq[0])
    by_column("nsa q", "w_in", nq[1])
    by_column("merge gates", "w_in", cols(o["mg"], P * EARLY))
    for j in range(0, KD, 2):
        if j >= EARLY:
            by_column("merge gates", "w_in", cols(o["mg"] + P * j, 2 * P))
        by_column("proj gla", "w_proj_gla", cols(P * j, 2 * P))
        by_column("merge gates", "w_in", cols(o["mn"] + P * j, 2 * P))
        by_column("proj nsa", "w_proj_nsa", cols(P * j, 2 * P), 4)
    for n in range(2):
        by_row("out", "w_out", cols(512 * n, 512), 0, KD)

    def ffn(tag, groups, ups, down):
        for g in range(len(groups) + 1):
            if g < len(groups):
                t0, nt = groups[g]
                if len(ups) == 2:
                    for t in range(t0, t0 + nt):
                        for u in ups:
                            by_column(f"up {tag}", u, cols(P * t, P))
                else:
                    by_column(f"up {tag}", ups[0], cols(P * t0, P * nt))
            if g:
                t0, nt = groups[g - 1]
                for n in range(2):
                    by_row(f"down {tag}", down, cols(512 * n, 512), P * t0, nt)

    ffn(1, FFN1_GROUPS, ["w_ffn_gate", "w_ffn_up"], "w_ffn_down")
    o = OFF2
    by_column("glu 2", "w_in_2", cols(o["glu"], 512))
    by_row("v 2", "w_in_2", cols(o["v"], 512), 0, KD)

    def qk2(f):
        by_column("qk 2", "w_in_2", cols(o["q"] + P * f, P) + cols(o["k"] + P * f, P))

    for f in range(3):
        qk2(f)
    by_column("ac ah 2", "w_in_2", cols(o["ac"], 512))
    qk2(3)
    by_column("ab 2", "w_in_2", cols(o["ab"], 256))
    for n in range(2):
        by_row("out 2", "w_out_2", cols(512 * n, 512), 0, KD)
    ffn(2, FFN2_GROUPS, ["w_ff1_2"], "w_ff2_2")
    return out


_vec = [("norm_mix_pre", 8), ("norm_ffn_pre", 8), ("g_attn_2", 8), ("g_ffn_2", 8), ("gla_b_alpha", 4),
        ("gla_norm_g", 2), ("b_conv_b_2", 2), ("ln_b_g_2", 2), ("ln_b_b_2", 2)]
VEC, NVEC = {}, 0
for _name, _n in _vec:
    VEC[_name] = (NVEC, _n)
    NVEC += _n
_con = [("ident", P), ("gla_mask", P), ("upper", P), ("block", P), ("before", P), ("ones", P),
        ("eps", 2), ("dist", S), ("cmp_dist", TT * NCMP), ("cmp_mask", TT * 32),
        ("q_scale", REP), ("slopes", NH), ("minus_slopes", NH)]
CON, NCON = {}, 0
for _name, _n in _con:
    CON[_name] = (NCON, _n)
    NCON += _n


def constants():
    p, c = np.arange(P)[:, None], np.arange(P)[None, :]
    out = np.zeros((P, NCON), np.float32)

    def put(name, a):
        o, n = CON[name]
        out[:, o:o + n] = np.broadcast_to(a, (P, n))

    put("ident", p == c)
    put("gla_mask", (p <= c) & (p // CHUNK == c // CHUNK))
    put("upper", -1.0 * (p >= c))
    put("block", np.where(p < c, 0.0, NEG))
    put("before", p < c)
    put("ones", 1.0)
    put("eps", np.array([RMS_EPS, LN_EPS]))
    key = np.arange(S)[None, :] - (S - P)
    put("dist", np.where(key <= p, key - p, NEG))
    t = p + P * np.arange(TT)[None, :]
    end = CS * np.arange(NCMP) + CL - 1
    seen = end[None, None, :] <= t[:, :, None]
    put("cmp_dist", np.where(seen, end[None, None, :] - t[:, :, None], NEG).reshape(P, -1))
    m = np.zeros((P, TT, 32))
    m[:, :, :NCMP] = seen
    put("cmp_mask", m.reshape(P, -1))
    head = np.where(p < DH, 0, REP) + np.arange(REP)[None, :]
    put("q_scale", DH ** -0.5 / SLOPES[head])
    put("slopes", SLOPES)
    put("minus_slopes", -SLOPES)
    return out


class Lane:

    def __init__(self, engine, sem):
        self.engine, self.sem, self.count, self.queue, self.waited = engine, sem, 0, [], {}

    def wait(self, *marks):
        for lane, value in marks:
            if self.waited.get(id(lane), 0) < value:
                self.waited[id(lane)] = value
                self.queue.append((self.engine.wait_ge, (lane.sem, value), {}, None))

    def run(self, what, *args, after=(), **named):
        self.wait(*after)
        self.queue.append((what, args, named, None))

    def do(self, what, *args, after=(), **named):
        self.wait(*after)
        self.count += 1
        self.queue.append((what, args, named, (self.sem, 1)))
        return self, self.count

    def write(self):
        for what, args, named, signal in self.queue:
            instruction = what(*args, **named)
            if signal:
                instruction.then_inc(*signal)


class Loads:

    def __init__(self, sem):
        self.sem, self.count = sem, 0

    def start(self, lane, out, in_, after=()):
        lane.wait(*after)
        self.count += 16
        lane.queue.append((lane.engine.dma_start, (out, in_), {}, (self.sem, 16)))
        return self, self.count


class Rotating:

    def __init__(self, bufs):
        self.bufs, self.at, self.readers = bufs, -1, [[] for _ in bufs]

    def take(self):
        self.at = (self.at + 1) % len(self.bufs)
        marks, self.readers[self.at] = self.readers[self.at], []
        return self.bufs[self.at], marks, self.readers[self.at]


def program(nc, T, wstream, vectors, consts, out):
    outer = ExitStack()
    with outer:
        def sb(name, shape, dt=F32, ctx=outer):
            return ctx.enter_context(nc.sbuf_tensor(name, [P] + shape, dt))

        def sem(name):
            return outer.enter_context(nc.semaphore(name))

        pe = Lane(nc.tensor, sem("pe_done"))
        act = Lane(nc.scalar, sem("act_done"))
        dve = Lane(nc.vector, sem("dve_done"))
        pool = Lane(nc.gpsimd, sem("pool_done"))
        sp = Lane(nc.sync, sem("sp_done"))
        banks = [outer.enter_context(nc.psum_tensor(f"bank{i}", [P, 512], F32)) for i in range(8)]
        linear_banks = Rotating(banks[0:2])
        core_banks = Rotating(banks[2:8])

        con = sb("con", [NCON])
        vec = sb("vec", [NVEC])

        def C(name):
            o, n = CON[name]
            return con[:, o:o + n]

        def V(name, j):
            return vec[:, VEC[name][0] + j:VEC[name][0] + j + 1]

        eps_rms, eps_ln = C("eps")[:, 0:1], C("eps")[:, 1:2]
        ident = C("ident")
        ident_r, upper_r, ones_r, block_r = (sb(n, [P], F32R) for n in ("ident_r", "upper_r", "ones_r", "block_r"))
        got_con = Loads(sem("got_con")).start(sp, con[:, :], consts)
        got_vec = Loads(sem("got_vec")).start(sp, vec[:, :], vectors)

        def exp_ln_tables():
            act.run(nc.scalar.preload_act_table_set, "natural_log_exp_and_others")

        exp_ln_tables()
        act.do(nc.scalar.activation, ident_r[:, :], ident, ACT.Copy, after=[got_con])
        act.do(nc.scalar.activation, upper_r[:, :], C("upper"), ACT.Copy)
        act.do(nc.scalar.activation, ones_r[:, :], C("ones"), ACT.Copy, scale=-1.0)
        consts_r = act.do(nc.scalar.activation, block_r[:, :], C("block"), ACT.Copy)
        dve.wait(got_con, got_vec)
        act.wait(got_con, got_vec)
        pe.wait(got_con)
        pool.wait(got_con)

        NW, NRAW = 4, 3
        w_raw = sb("w_raw", [NRAW, HALF])
        w_hi = sb("w_hi", [NW, CH], F32R)
        w_lo = sb("w_lo", [NW, CH], F32R)
        raw_loads = [Loads(sem(f"raw_load{i}")) for i in range(NRAW)]
        raw_free = [[] for _ in range(NRAW)]
        chunks = plan()
        state = dict(split=0, used=0)
        chunk_ready, chunk_free = {}, {}

        parts, at = [], 0
        for n, (_, _, _, nk, c) in enumerate(chunks):
            size = nk * len(c)
            parts += [(n, a, min(size, a + HALF), at) for a in range(0, size, HALF)]
            at += P * size
        raw_got = {}

        def load_part(p):
            if p < len(parts):
                n, a, b, at = parts[p]
                size = chunks[n][3] * len(chunks[n][4])
                src = wstream[at:at + P * size].rearrange("(p n) -> p n", p=P)
                r = p % NRAW
                raw_got[p] = raw_loads[r].start(sp, w_raw[:, r, 0:b - a], src[:, a:b], raw_free[r])

        def bring():
            while state["split"] < len(parts):
                p = state["split"]
                n, a, b, _ = parts[p]
                if n >= NW and n - NW not in chunk_free:
                    return
                state["split"] += 1
                slot, r, free = n % NW, p % NRAW, chunk_free.get(n - NW, [])
                lo_lane = pool if p % 4 == 0 else dve
                hi, lo, raw = w_hi[:, slot, a:b], w_lo[:, slot, a:b], w_raw[:, r, 0:b - a]
                m1 = act.do(nc.scalar.activation, hi, raw, ACT.Copy, after=[raw_got[p], *free])
                m2 = lo_lane.do(lo_lane.engine.tensor_tensor, lo, raw, hi.bitcast(F32), ALU.subtract, after=[m1, *free])
                raw_free[r] = [m1, m2]
                chunk_ready.setdefault(n, []).append([m1, m2])
                load_part(p + NRAW)

        def next_chunk(layer):
            n = state["used"]
            state["used"] += 1
            planned, _, _, nk, c = chunks[n]
            assert planned == layer, (planned, layer)
            hi, lo = (w[:, n % NW, 0:nk * len(c)].rearrange("p (k c) -> p k c", k=nk) for w in (w_hi, w_lo))
            return hi, lo, n

        def need(n, k):
            pe.wait(*chunk_ready[n][k * len(chunks[n][4]) // HALF])

        def chunks_done(ns, mark):
            for n in ns:
                chunk_free[n] = [mark]
            bring()

        def by_column_tiles(layer, act_hi, act_lo, ready, evacuate, n_tiles, nk=KD, width=P):
            f = 0
            while f < n_tiles:
                hi, lo, n = next_chunk(layer)
                here = len(chunks[n][4]) // width
                for t in range(here):
                    bank, free, readers = linear_banks.take()
                    pe.wait(*free, *ready(0))
                    o = bank[0:width, :]
                    for k in range(nk):
                        pe.wait(*ready(k))
                        need(n, k)
                        ws = slice(t * width, (t + 1) * width)
                        for i, (a, b) in enumerate(((hi, act_hi), (lo, act_hi), (hi, act_lo))):
                            operands = (o, a[:, k, ws], b[:, k, :])
                            step = dict(start=(k == 0 and i == 0), stop=(k == nk - 1 and i == 2))
                            if k == nk - 1 and i == 2:
                                done = pe.do(nc.tensor.matmul, *operands, **step)
                            else:
                                pe.run(nc.tensor.matmul, *operands, **step)
                    readers += evacuate(f, o, done)
                    if t == here - 1:
                        chunks_done([n], done)
                    f += 1
                    yield

        def by_row_tiles(layer, act_hi, act_lo, ready, evacuate, nk, k0=0, halves=(0, 1)):
            for n in halves:
                held = [next_chunk(layer) for _ in range((nk + 3) // 4)]
                width = len(chunks[held[0][2]][4])
                for i in range(TT):
                    bank, free, readers = linear_banks.take()
                    pe.wait(*free)
                    o = bank[:, 0:width]
                    for k in range(nk):
                        pe.wait(*ready(k0 + k))
                        hi, lo, num = held[k // 4]
                        need(num, k % 4)
                        for j, (a, b) in enumerate(((act_hi, hi), (act_lo, hi), (act_hi, lo))):
                            operands = (o, a[:, k0 + k, P * i:P * (i + 1)], b[:, k % 4, :])
                            step = dict(start=(k == 0 and j == 0), stop=(k == nk - 1 and j == 2))
                            if j == 2 and k == nk - 1:
                                done = pe.do(nc.tensor.matmul, *operands, **step)
                            else:
                                pe.run(nc.tensor.matmul, *operands, **step)
                    readers += evacuate(n, i, o, done)
                    if i == TT - 1:
                        chunks_done([num for _, _, num in held], done)
                    yield

        def finish(*gens):
            for g in gens:
                for _ in g:
                    pass

        def weave(main, filler, every=1):
            for _ in main:
                for _ in range(every):
                    next(filler, None)
            finish(filler)

        stat = sb("stat", [2, 5, TT])
        junk = sb("junk", [512])
        halves = [slice(0, 512), slice(512, 1024)]
        squares = {}

        def square(which, i, n, src, after):
            m = act.do(nc.scalar.activation, junk[:, :], src, ACT.Square, accum_out=stat[:, which, n, i:i + 1],
                       after=[*after, *squares.get("last", [])])
            squares["last"] = [m]
            squares.setdefault((which, i), []).append(m)
            return m

        def rstd(which, i):
            s0, s1, total, log, out = (stat[:, which, n, i:i + 1] for n in range(5))
            m = dve.do(nc.vector.tensor_tensor, total, s0, s1, ALU.add, after=squares.pop((which, i)))
            m = act.do(nc.scalar.activation, log, total, ACT.Ln, bias=eps_rms, scale=1.0 / D, after=[m])
            return out, act.do(nc.scalar.activation, out, log, ACT.Exp, scale=-0.5, after=[m])

        h_hi = sb("h_hi", [KD, S], F32R)
        h_lo = sb("h_lo", [KD, S], F32R)
        h_ready = [[] for _ in range(KD)]

        def norm_tile(i, x, scaled, gain, h_free, ready=()):
            r, m = rstd(1, i)
            marks = [dve.do(nc.vector.tensor_scalar, scaled[:, halves[0]], x[:, halves[0]], r, None, ALU.mult,
                            after=[m, *ready]),
                     act.do(nc.scalar.activation, scaled[:, halves[1]], x[:, halves[1]], ACT.Copy, scale=r,
                            after=[m, *ready])]

            def turn():
                ts = slice(P * i, P * i + P)
                for k0 in range(0, KD, 4):
                    bank, free, readers = core_banks.take()
                    pe.wait(*free, *marks)
                    for k in range(4):
                        m = pe.do(nc.tensor.transpose, bank[:, P * k:P * (k + 1)], scaled[:, P * (k0 + k):P * (k0 + k + 1)],
                                  ident)
                    for k in range(4):
                        src, g = bank[:, P * k:P * (k + 1)], V(gain, k0 + k)
                        hi_ap, lo_ap = h_hi[:, k0 + k, ts], h_lo[:, k0 + k, ts]
                        hi = act.do(nc.scalar.activation, hi_ap, src, ACT.Copy, scale=g, after=[m, *h_free])
                        new_ready.setdefault(k0 + k, []).append(hi)
                    for k in range(4):
                        src, g = bank[:, P * k:P * (k + 1)], V(gain, k0 + k)
                        hi_ap, lo_ap = h_hi[:, k0 + k, ts], h_lo[:, k0 + k, ts]
                        lo = dve.do(nc.vector.scalar_tensor_tensor, lo_ap, src, g, hi_ap.bitcast(F32), ALU.mult,
                                    ALU.subtract, after=[hi, *h_free])
                        new_ready[k0 + k].append(lo)
                    readers += [hi, lo]

            return turn

        new_ready = {}

        def h_renewed():
            for k in range(KD):
                h_ready[k] = new_ready.pop(k)

        def turn_behind(turns, i, phases):
            if len(turns) == 2:
                turns.pop(0)()
            phases[0]()
            if i == TT - 1:
                turns.pop(0)()
                phases[1]()()
                h_renewed()
            else:
                turns.append(phases[1]())

        def split(hi_ap, lo_ap, src, after, lo_lane=pool):
            hi = act.do(nc.scalar.activation, hi_ap, src, ACT.Copy, after=after)
            lo = lo_lane.do(lo_lane.engine.tensor_tensor, lo_ap, src, hi_ap.bitcast(F32), ALU.subtract, after=[hi, *after])
            return [hi, lo]

        def last(*lanes):
            return [(l, l.count) for l in (lanes or (pe, act, dve, pool)) if l.count]

        x_rows = T["x"].rearrange("a (i p) d -> (a p) i d", p=P)

        with ExitStack() as scope:
            x0 = sb("x0", [TT, D], ctx=scope)
            loads = [Loads(sem(f"x0_load{i}")) for i in range(TT)]
            got = [loads[i].start(sp, x0[:, i, :], x_rows[:, i, :]) for i in range(TT)]
            for p in range(NRAW):
                load_part(p)
            turns = []
            for i in range(TT):
                for n, half in enumerate(halves):
                    square(1, i, n, x0[:, i, half], [got[i]])
                turn_behind(turns, i, [lambda: None,
                                       lambda: norm_tile(i, x0[:, i, :], x0[:, i, :], "norm_mix_pre", [], [got[i]])])
            bring()
        x0_free = last()

        ready_h = lambda k: h_ready[k]

        mixer = ExitStack()
        nsa_io = ExitStack()
        o_gla = sb("o_gla", [KD, S], ctx=mixer)
        kc_vc = sb("kc_vc", [2, S], ctx=nsa_io)
        v_hi = sb("v_hi", [TT, 2 * P], F32R, ctx=nsa_io)
        v_lo = sb("v_lo", [TT, 2 * P], F32R, ctx=nsa_io)
        nsa_g = sb("nsa_g", [TT, 24], ctx=nsa_io)
        gla = ExitStack()
        rr = sb("rr", [2, S], ctx=gla)
        v_gla = sb("v_gla", [TT, GLA_H * DV], ctx=gla)
        top = (nc.sbuf_usable_end - 16 * 1024) // 32 * 32

        def at_top(name, kb, shape, dt=F32):
            return nc.alloc_sbuf_tensor_at(name, [P] + shape, dt, offset=top + 1024 * kb)

        a_low = at_top("a_low", 0, [S])
        w_alpha = at_top("w_alpha", 2, [GLA_H * DK])
        reset = at_top("reset", 4, [S])
        gs = at_top("gs", 6, [5, S])
        qkd_of = sb("qkd", [2, 3, S], ctx=gla)
        decay_of = sb("decay", [2, NCH], ctx=gla)
        attn = junk
        kd_rows = sb("kd_rows", [TT, P], ctx=gla)
        states = sb("states", [NCH - 1, DV], ctx=gla)

        load_alpha = Loads(sem("load_alpha"))
        got_alpha = load_alpha.start(sp, w_alpha[0:RANK, :], T["gla_w_alpha2"][0], x0_free)
        zero_attn = pool.do(nc.gpsimd.memset, attn[:, :], 0.0, after=x0_free)
        m = pool.do(nc.gpsimd.memset, reset[:, :], 1.0, after=x0_free)
        set_reset = pool.do(nc.gpsimd.memset, reset[:, 0:S:CHUNK], 0.0, after=[m])
        zero_attn_and_reset = [zero_attn, set_reset]

        got = {}

        def keep(name):
            def evac(f, o, done):
                got[name, f] = act.do(nc.scalar.activation, name_to[name](f), o, ACT.Copy, after=[done])
                return [got[name, f]]
            return evac

        name_to = {"ga": lambda f: a_low[0:RANK, :]}
        act.wait(*x0_free)
        dve.wait(*x0_free)
        pool.wait(*x0_free)
        finish(by_column_tiles("gla a", h_hi, h_lo, ready_h, keep("ga"), 1, width=RANK))

        v_marks = []

        def evac_v(n, i, o, done):
            m = act.do(nc.scalar.activation, v_gla[:, i, 512 * n:512 * n + 512], o, ACT.Copy, after=[done])
            v_marks.append(m)
            return [m]

        def gla_v():
            yield from by_row_tiles("gla v", h_hi, h_lo, ready_h, evac_v, KD)

        def chunked(ap):
            return ap.rearrange("p (n c) -> p n c", c=CHUNK)

        free = {"gs": [], ("qkd", 0): [], ("qkd", 1): [], "attn": zero_attn_and_reset, "kd_rows": [], ("states", 0): [],
                ("states", 1): []}

        def gla_gates(h):
            bank, bank_free, readers = core_banks.take()
            m = pe.do(nc.tensor.matmul, bank[:, :], w_alpha[0:RANK, DK * h:DK * (h + 1)], a_low[0:RANK, :],
                                         start=True, stop=True, after=[got_alpha, got["ga", 0], *bank_free])
            x_, e_, b_ = gs[:, 0, :], gs[:, 1, :], gs[:, 2, :]
            x = dve.do(nc.vector.tensor_scalar, x_, bank[:, :], V("gla_b_alpha", h), None, ALU.add, after=[m, *free["gs"]])
            readers.append(x)
            m = dve.do(nc.vector.scalar_tensor_tensor, e_, x_, -1.0, x_, ALU.mult, ALU.min, after=[x])
            m = act.do(nc.scalar.activation, e_, e_, ACT.Exp, after=[m])
            m = act.do(nc.scalar.activation, e_, e_, ACT.Ln, bias=1.0, after=[m])
            yield
            m = dve.do(nc.vector.scalar_tensor_tensor, x_, x_, 0.0, e_, ALU.min, ALU.subtract, after=[m])
            b = dve.do(nc.vector.tensor_tensor_scan, b_, reset[:, :], x_, 0.0, ALU.mult, ALU.add, after=[m, set_reset])
            b_last = chunked(b_)[:, :, CHUNK - 1:CHUNK]
            m = dve.do(nc.vector.tensor_tensor, chunked(e_), b_last.broadcast_to([P, NCH, CHUNK]), chunked(b_),
                                                 ALU.subtract, after=[b])
            yield
            act.do(nc.scalar.activation, gs[:, 3, :], b_, ACT.Exp, scale=1 / TAU, after=[b])
            act.do(nc.scalar.activation, gs[:, 4, :], b_, ACT.Exp, scale=-1 / TAU)
            act.do(nc.scalar.activation, decay_of[:, h % 2, :], b_last.squeeze(), ACT.Exp, scale=1 / TAU, after=free["states", h % 2])
            gates_ready[h] = act.do(nc.scalar.activation, e_, e_, ACT.Exp, scale=1 / TAU, after=[m])

        qk_marks, gates_ready = {}, {}

        def gla_front(h):
            yield from gla_gates(h)
            qkd = qkd_of[:, h % 2, :, :]
            yield

            def evac(f, o, done):
                if f == 0:
                    m = dve.do(nc.vector.scalar_tensor_tensor, qkd[:, 0, :], o, DK ** -0.5, gs[:, 3, :], ALU.mult, ALU.mult,
                               after=[done, gates_ready[h], *free["qkd", h % 2]])
                    qk_marks[h] = [m]
                    return [m]
                m1 = dve.do(nc.vector.tensor_tensor, qkd[:, 1, :], o, gs[:, 4, :], ALU.mult, after=[done])
                m2 = dve.do(nc.vector.tensor_tensor, qkd[:, 2, :], o, gs[:, 1, :], ALU.mult)
                qk_marks[h] += [m1, m2]
                free["gs"] = [m2]
                return [m1, m2]

            yield from by_column_tiles(f"gla qk {h}", h_hi, h_lo, ready_h, evac, 2)

        def gla_head(h):
            qkd, decay, qk = qkd_of[:, h % 2, :, :], decay_of[:, h % 2, :], qk_marks[h]
            o_sq = qkd[:, 1:3, :]
            o_rs = qkd[:, 0, :]
            bank, bank_free, readers = core_banks.take()
            pe.wait(*bank_free, *qk)
            for p in range(TT):
                m = pe.do(nc.tensor.matmul, bank[:, P * p:P * p + P], qkd[:, 1, P * p:P * p + P],
                                                  qkd[:, 0, P * p:P * p + P], start=True, stop=True)
            mask = C("gla_mask").bitcast(U32).unsqueeze(1).broadcast_to([P, TT, P])
            attn_ready = dve.do(nc.vector.copy_predicated, attn[:, :].rearrange("p (a c) -> p a c", c=P), mask,
                                                            bank[:, :].rearrange("p (a c) -> p a c", c=P), after=[m, *free["attn"]])
            readers.append(attn_ready)
            yield
            bank, bank_free, readers = core_banks.take()
            pe.wait(*bank_free)
            for p in range(TT):
                m = pe.do(nc.tensor.transpose, bank[:, P * p:P * p + P], qkd[:, 2, P * p:P * p + P], ident)
            kd_ready = act.do(nc.scalar.activation, kd_rows[:, :, :].rearrange("p a c -> p (a c)"), bank[:, :],
                                                                ACT.Copy, after=[m, *free["kd_rows"]])
            readers.append(kd_ready)
            yield
            step = None
            state_marks = {}
            states_free = free["states", (h + 1) % 2]
            for n0 in range(0, NCH - 1, 4):
                some = range(n0, min(n0 + 4, NCH - 1))
                pair = [core_banks.take() for _ in range(2)]
                pe.wait(*pair[0][1], *pair[1][1], kd_ready, *v_marks)
                update = {}
                for n in some:
                    p, r = n // 2, CHUNK * (n % 2)
                    update[n] = pair[n % 2][0][:, DV * (p % 2):DV * (p % 2) + DV]
                    m = pe.do(nc.tensor.matmul, update[n], kd_rows[r:r + CHUNK, p, :],
                                                 v_gla[r:r + CHUNK, p, DV * h:DV * (h + 1)], start=True, stop=True)
                yield
                for n in some:
                    new = states[:, n, :]
                    if n == 0:
                        step = dve.do(nc.vector.tensor_copy, new, update[n], after=[m, *states_free])
                    else:
                        step = dve.do(nc.vector.scalar_tensor_tensor, new, states[:, n - 1, :], decay[:, n:n + 1], update[n], ALU.mult,
                                                                       ALU.add, after=[m, step])
                    pair[n % 2][2].append(step)
                    state_marks[n + 1] = step
                yield
            free["kd_rows"] = [m]
            outs = []
            for j in range(2):
                bank, bank_free, readers = core_banks.take()
                pe.wait(*bank_free, attn_ready)
                e0 = DV * h + P * j
                for p in range(TT):
                    pe.run(nc.tensor.matmul, bank[:, P * p:P * p + P], v_gla[:, p, e0:e0 + P], attn[:, P * p:P * p + P],
                        start=(p == 0), stop=False, skip_group_check=True)
                for n in range(1, NCH):
                    pe.wait(state_marks[n])
                    m = pe.do(nc.tensor.matmul, bank[:, CHUNK * n:CHUNK * (n + 1)], states[:, n - 1, P * j:P * j + P],
                        qkd[:, 0, CHUNK * n:CHUNK * (n + 1)], start=False, stop=(n == NCH - 1), skip_group_check=True)
                sq = act.do(nc.scalar.activation, o_sq[:, j, :], bank[:, :], ACT.Square, after=[m])
                outs.append((bank, readers, sq, m))
                yield
            free["attn"] = free["states", h % 2] = [m]
            bank, bank_free, readers = core_banks.take()
            pe.wait(*bank_free, outs[0][2], outs[1][2])
            for j in range(2):
                m = pe.do(nc.tensor.matmul, bank[:, :], C("ones"), o_sq[:, j, :], start=(j == 0),
                                                             stop=(j == 1))
            m = act.do(nc.scalar.activation, o_rs, bank[:, :], ACT.Ln, bias=eps_rms, scale=1.0 / DV, after=[m])
            readers.append(m)
            m = act.do(nc.scalar.activation, o_rs, o_rs, ACT.Exp, scale=-0.5, after=[m])
            for j in range(2):
                bank, readers, sq, om = outs[j]
                k = dve.do(nc.vector.scalar_tensor_tensor, o_gla[:, 2 * h + j, :], bank[:, :], V("gla_norm_g", j), o_rs, ALU.mult, ALU.mult, after=[m, om])
                readers += [sq, k]
            free["qkd", h % 2] = [k]
            return_marks["o_gla", h] = k
            yield

        return_marks = {}
        def evac_nsa_rows(n, i, o, done):
            m2 = act.do(nc.scalar.activation, nsa_g[:, i, :], o[:, 2 * P:2 * P + 24], ACT.Exp, scale=-1.0, after=[done])
            got["nv", i] = split(v_hi[:, i, :], v_lo[:, i, :], o[:, 0:2 * P], [done], dve)
            m = dve.do(nc.vector.tensor_scalar, nsa_g[:, i, :], nsa_g[:, i, :], 1.0, None, ALU.add, after=[m2])
            got["gate", i] = dve.do(nc.vector.reciprocal, nsa_g[:, i, :], nsa_g[:, i, :], after=[m])
            return [*got["nv", i], m2]

        def sigmoid(t, o, after):
            m1 = act.do(nc.scalar.activation, t, o, ACT.Exp, scale=-1.0, after=after)
            m = act.do(nc.scalar.activation, t, t, ACT.Ln, bias=1.0, after=[m1])
            return m1, act.do(nc.scalar.activation, t, t, ACT.Exp, scale=-1.0, after=[m])

        def evac_r(f0, rot_rr):
            def evac(f, o, done):
                f += f0
                t, t_free, t_readers = rot_rr.take()
                m1, m = sigmoid(t, o, [done, *t_free])
                m = dve.do(nc.vector.tensor_tensor, t, t, o, ALU.mult, after=[m])
                got["og", f] = pool.do(nc.gpsimd.tensor_tensor, o_gla[:, f, :], o_gla[:, f, :], t, ALU.mult,
                                       after=[m, return_marks["o_gla", f // 2]])
                t_readers.append(got["og", f])
                return [m1, m]
            return evac

        def evac_kc_vc(f, o, done):
            got["kc_vc", f] = act.do(nc.scalar.activation, kc_vc[:, f, :], o, ACT.Copy, after=[done])
            return [got["kc_vc", f]]

        def fills():
            yield from by_row_tiles("nsa v gate", h_hi, h_lo, ready_h, evac_nsa_rows, KD, halves=(0,))
            yield from by_column_tiles("nsa kc vc", h_hi, h_lo, ready_h, evac_kc_vc, 2)
            yield from by_column_tiles("gla r", h_hi, h_lo, ready_h, evac_r(0, Rotating([rr[:, i, :] for i in range(2)])), KD - 2)

        rest = fills()
        front = gla_front(0)
        for n, _ in enumerate(gla_v()):
            if n % 2 == 0 and n < 6:
                next(front)
        finish(front)
        for h in range(GLA_H):
            front = gla_front(h + 1) if h + 1 < GLA_H else iter(())
            if h == GLA_H - 1:
                w1_k = at_top("w1_k", 0, [CL, P])
                got_w1_k = Loads(sem("load_w1_k")).start(sp, w1_k[:, :, :].rearrange("p l o -> p (l o)"), T["w1_k"],
                                                         last())
            for n, _ in enumerate(gla_head(h)):
                next(rest if n in FILLS[h] else front, None)
            finish(front)
        finish(rest)
        assert nc.sbuf_base <= top
        gla_free = last()
        gla.close()

        nsa = ExitStack()
        mix_gates = sb("mix_gates", [EARLY, S], ctx=nsa_io)
        q_hi, q_lo = at_top("q_hi", 0, [4, S], F32R), at_top("q_lo", 8, [4, S], F32R)
        on_hi, on_lo = q_hi, q_lo
        for lane in (act, dve, pool, pe, sp):
            lane.wait(*gla_free)
        kc_hi, kc_lo = sb("kc_hi", [32], F32R, ctx=nsa), sb("kc_lo", [32], F32R, ctx=nsa)
        v4 = sb("v4", [NG, REP * DH], ctx=nsa)
        k_hi, k_lo = (sb(f"k_{n}", [2, S], F32R, ctx=nsa) for n in ("hi", "lo"))

        def evac_q(f, o, done):
            scale = C("q_scale")[:, f:f + 1]
            hi = act.do(nc.scalar.activation, q_hi[:, f, :], o, ACT.Copy, scale=scale, after=[done, *w1_k_free])
            lo = dve.do(nc.vector.scalar_tensor_tensor, q_lo[:, f, :], o, scale, q_hi[:, f, :].bitcast(F32), ALU.mult,
                        ALU.subtract, after=[hi])
            got["nq", f] = [hi, lo]
            return [hi, lo]

        def evac_k(f, o, done):
            got["nk", f] = split(k_hi[:, f, :], k_lo[:, f, :], o, [done], dve)
            return got["nk", f]

        def late_fills():
            yield from by_column_tiles("nsa ks kw", h_hi, h_lo, ready_h, evac_k, 2)
            yield from by_column_tiles("gla r", h_hi, h_lo, ready_h, evac_r(KD - 2, Rotating([rr_late[:, i, :] for i in range(2)])), 2)
            yield from by_column_tiles("nsa q", h_hi, h_lo, ready_h, evac_q, REP)

        cmp_scope = ExitStack()
        rr_late = sb("rr_late", [2, S], ctx=cmp_scope)
        w1 = sb("w1", [CL, P], ctx=cmp_scope)
        pe_t = sb("pe_t", [2, CL], ctx=cmp_scope)
        w2 = sb("w2", [2, P], ctx=cmp_scope)
        windows = sb("windows", [CL, NCMP], ctx=cmp_scope)
        hid = sb("hid", [3, 32], ctx=cmp_scope)
        zero_hid = pool.do(nc.gpsimd.memset, hid[:, 2, :], 0.0)
        zero_v4 = pool.do(nc.gpsimd.memset, v4[:, :, :], 0.0)

        def load(name, to):
            return Loads(sem(f"load_{name}")).start(sp, to, T[name])

        got_pe = [load(f"pe_{n}", pe_t[:, x, :]) for x, n in enumerate("kv")]
        got_w2 = [load(f"w2_{n}", w2[:, x, :]) for x, n in enumerate("kv")]
        w1_of = [w1_k, w1]
        got_w1 = [got_w1_k, load("w1_v", w1[:, :, :].rearrange("p l o -> p (l o)"))]
        kc_ready, v4_marks, w1_k_free = [], [], []

        def compression():
            win_free = []
            for x in range(2):
                src = kc_vc[:, x, :]
                for half in range(2):
                    blk = src.rearrange("p (n l) -> p l n", l=CS)[:, :, half:half + NCMP]
                    pe_b = pe_t[:, x, CS * half:CS * half + CS].unsqueeze(2).broadcast_to([P, CS, NCMP])
                    win_ready = dve.do(nc.vector.tensor_tensor, windows[:, CS * half:CS * half + CS, :], blk, pe_b, ALU.add, after=[got_pe[x], got["kc_vc", x], *win_free])
                bank, bank_free, readers = core_banks.take()
                pe.wait(*bank_free, got_w1[x], win_ready)
                for l in range(CL):
                    m = pe.do(nc.tensor.matmul, bank[:, 0:NCMP], w1_of[x][:, l, :], windows[:, l, :], start=(l == 0),
                              stop=(l == CL - 1))
                    if l % 4 == 3:
                        yield
                win_free = [m]
                if x == 0:
                    w1_k_free.append(m)
                yield
                m = act.do(nc.scalar.activation, hid[:, 0, 0:NCMP], bank[:, 0:NCMP], ACT.Exp, scale=-1.0, after=[m])
                m2 = dve.do(nc.vector.tensor_scalar, hid[:, 1, 0:NCMP], hid[:, 0, 0:NCMP], 1.0, None, ALU.add, after=[m])
                m2 = dve.do(nc.vector.reciprocal, hid[:, 1, 0:NCMP], hid[:, 1, 0:NCMP], after=[m2])
                m2 = dve.do(nc.vector.tensor_tensor, hid[:, 2, 0:NCMP], bank[:, 0:NCMP], hid[:, 1, 0:NCMP],
                                                                 ALU.mult, after=[m2, zero_hid])
                readers += [m, m2]
                yield
                bank, bank_free, readers = core_banks.take()
                pe.wait(*bank_free, m2, got_w2[x])
                if x == 0:
                    m = pe.do(nc.tensor.matmul, bank[:, 0:32], w2[:, 0, :], hid[:, 2, :], start=True,
                                                            stop=True)
                    kc_ready[:] = split(kc_hi[:, :], kc_lo[:, :], bank[:, 0:32], [m], dve)
                    readers += kc_ready
                else:
                    for r in range(REP):
                        m = pe.do(nc.tensor.matmul, bank[32 * r:32 * r + NCMP, 0:P], hid[:, 2, 0:NCMP],
                                                                     w2[:, 1, :], start=True, stop=True)
                    for r in range(REP):
                        v4_marks[:] = [dve.do(nc.vector.tensor_copy, v4[32 * r:32 * r + NCMP, :, DH * r:DH * r + DH],
                            bank[32 * r:32 * r + NCMP, 0:P].rearrange("p (g d) -> p g d", g=NG), after=[m, zero_v4])]
                    readers += v4_marks
                yield

        late = late_fills()
        for n, _ in enumerate(compression()):
            if n % FILL_EVERY == 0 or n > 20:
                next(late, None)
        finish(late)
        cmp_free = last()
        cmp_scope.close()

        for lane in (act, dve, pool, pe):
            lane.wait(*cmp_free)
        probs = sb("probs", [2, REP, S], ctx=nsa)
        pt_hi, pt_lo = (sb(f"pt_{n}", [2, S], F32R, ctx=nsa) for n in ("hi", "lo"))
        sc = sb("nsa_stats", [3, 40], ctx=nsa)
        pc = kc_vc[:, 0, 0:NH * 32].rearrange("p (h n) -> p h n", n=32)
        pc_t = kc_vc[:, 0, NH * 32:NH * 32 + NG * P].rearrange("p (g q) -> p g q", q=P)
        o_rows = kc_vc[:, 1, :]
        zero_pc = pool.do(nc.gpsimd.memset, pc[:, :, :], 0.0)
        rot_probs = Rotating([probs[:, i, :, :] for i in range(2)])
        rot_pt = Rotating([(pt_hi[:, i, :], pt_lo[:, i, :]) for i in range(2)])
        fr = {"pc": [zero_pc], "pc_t": [], "o_rows": [], "stats": []}
        o_banks = Rotating(banks[6:8])
        score_banks = Rotating(banks[2:4])
        turn_banks = Rotating(banks[4:6])
        score_banks.readers, turn_banks.readers = core_banks.readers[0:2], core_banks.readers[2:4]
        o_banks.readers = core_banks.readers[4:6]
        cmp_seen = C("cmp_mask").rearrange("p (i n) -> p i n", n=32)
        cmp_dist = C("cmp_dist").rearrange("p (i n) -> p i n", n=NCMP)
        gates = nsa_g[:, :, :].rearrange("p i (h b) -> p i h b", b=3)
        held = {}

        def products(out_ap, a_hi, a_lo, b_hi, b_lo, start=True, stop=True):
            step = dict(skip_group_check=not start)
            pe.run(nc.tensor.matmul, out_ap, a_hi, b_hi, start=start, stop=False, **step)
            pe.run(nc.tensor.matmul, out_ap, a_hi, b_lo, start=False, stop=False, **step)
            return pe.do(nc.tensor.matmul, out_ap, a_lo, b_hi, start=False, stop=stop, **step)

        def over_keys(ap, n=NH):
            return ap.unsqueeze(2).broadcast_to([P, n, NCMP])

        def cmp_scores(i):
            p = pc[:, :, 0:NCMP]
            mx, sm, wt = sc[:, 0, 32:40], sc[:, 1, 32:40], sc[:, 2, 32:40]
            for g in range(NG):
                bank, bank_free, readers = score_banks.take()
                pe.wait(*bank_free, *kc_ready, *sum((got["nq", j] for j in range(REP)), []))
                rows = slice(DH * g, DH * g + DH)
                for j in range(REP):
                    m = products(bank[:, 32 * j:32 * (j + 1)], q_hi[rows, j, P * i:P * i + P], q_lo[rows, j, P * i:P * i + P],
                                 kc_hi[rows, :], kc_lo[rows, :])
                scores = bank[:, 0:REP * 32].rearrange("p (h n) -> p h n", n=32)[:, :, 0:NCMP]
                m = dve.do(nc.vector.tensor_tensor, pc[:, REP * g:REP * (g + 1), 0:NCMP], scores,
                           cmp_dist[:, i, :].unsqueeze(1).broadcast_to([P, REP, NCMP]), ALU.add, after=[m, *fr["pc"]])
                readers.append(m)
            yield
            m = dve.do(nc.vector.tensor_reduce, mx, p, AXX, ALU.max, after=[m])
            m = dve.do(nc.vector.tensor_tensor, p, p, over_keys(mx), ALU.subtract, after=[m])
            m = dve.do(nc.vector.tensor_tensor, p, p, over_keys(C("slopes")), ALU.mult, after=[m])
            m = act.do(nc.scalar.activation, p, p, ACT.Exp, after=[m])
            m = dve.do(nc.vector.tensor_reduce, sm, p, AXX, ALU.add, after=[m])
            m = dve.do(nc.vector.reciprocal, wt, sm, after=[m])
            m = dve.do(nc.vector.tensor_tensor, wt, wt, gates[:, i, :, 0], ALU.mult, after=[m, got["gate", i]])
            m = dve.do(nc.vector.tensor_tensor, p, p, over_keys(wt), ALU.mult, after=[m])
            held["pc", i] = dve.do(nc.vector.tensor_tensor, p, p,
                                   cmp_seen[:, i, 0:NCMP].unsqueeze(1).broadcast_to([P, NH, NCMP]), ALU.mult, after=[m])
            yield

        def cmp_values(i):
            held["o", i] = [o_banks.take() for _ in range(NG)]
            o_free = held["o", i][0][1] + held["o", i][1][1]
            bank, bank_free, readers = turn_banks.take()
            pe.wait(*bank_free, held["pc", i])
            for g in range(NG):
                m = pe.do(nc.tensor.transpose, bank[:, P * g:P * g + P],
                          pc[:, REP * g:REP * (g + 1), :].rearrange("p h n -> p (h n)"), ident)
            fr["pc"] = [m]
            t = dve.do(nc.vector.tensor_copy, pc_t[:, :, :].rearrange("p g q -> p (g q)"), bank[:, 0:2 * P],
                       after=[m, *fr["pc_t"]])
            readers.append(t)
            yield
            pe.wait(*o_free, *v4_marks, t, *sum((got["nv", n] for n in range(TT)), []))
            for g in range(NG):
                for j in range(REP):
                    m = pe.do(nc.tensor.matmul, held["o", i][g][0][0:DH, P * j:P * j + P],
                              v4[:, g, DH * j:DH * j + DH], pc_t[:, g, :], start=(j == 0), stop=False,
                              skip_group_check=True)
            fr["pc_t"] = [m]

        def key_scores(i, br, g):
            width = P * (i + 1)
            rows, qs = slice(DH * g, DH * g + DH), slice(P * i, P * i + P)
            pr, pr_free, pr_readers = rot_probs.take()
            c0 = 8 * rot_probs.at
            mx, mb, sm = sc[:, 0, c0:c0 + REP], sc[:, 0, c0 + REP:c0 + 2 * REP], sc[:, 1, c0:c0 + REP]
            wt = sc[:, 2, c0:c0 + REP]
            for j in range(REP):
                bank, bank_free, readers = score_banks.take()
                pe.wait(*bank_free, *got["nq", j], *got["nk", br])
                m = products(bank[:, 0:width], q_hi[rows, j, qs], q_lo[rows, j, qs], k_hi[rows, br, 0:width],
                             k_lo[rows, br, 0:width])
                m = dve.do(nc.vector.tensor_tensor_reduce, pr[:, j, 0:width], bank[:, 0:width],
                           C("dist")[:, S - width:S], 1.0, -3e38, ALU.add, ALU.max, mx[:, j:j + 1], after=[m, *pr_free])
                readers.append(m)
                m = dve.do(nc.vector.tensor_tensor, mb[:, j:j + 1], mx[:, j:j + 1],
                           C("minus_slopes")[:, REP * g + j:REP * g + j + 1], ALU.mult, after=[m])
                yield
                m = act.do(nc.scalar.activation, pr[:, j, 0:width], pr[:, j, 0:width], ACT.Exp,
                           scale=float(SLOPES[REP * g + j]), bias=mb[:, j:j + 1], accum_out=sm[:, j:j + 1], after=[m])
            yield
            m = dve.do(nc.vector.reciprocal, wt, sm, after=[m])
            m = dve.do(nc.vector.tensor_tensor, wt, wt, gates[:, i, REP * g:REP * (g + 1), 1 + br], ALU.mult, after=[m])
            ready = []
            for j in range(REP):
                p = pr[:, j, 0:width]
                if j in SCALED_BY_ACT:
                    ready.append(act.do(nc.scalar.activation, p, p, ACT.Copy, scale=wt[:, j:j + 1], after=[m]))
                else:
                    ready.append(dve.do(nc.vector.tensor_scalar, p, p, wt[:, j:j + 1], None, ALU.mult, after=[m]))
            held[i, br, g] = pr, pr_readers, ready

        def key_values(i, br, g):
            o_bank = held["o", i][g][0]
            pr, pr_readers, ready = held[i, br, g]
            turned = {}

            def turn(kb):
                bank, bank_free, readers = turn_banks.take()
                pe.wait(*bank_free, *ready)
                for j in range(REP):
                    m = pe.do(nc.tensor.transpose, bank[:, P * j:P * j + P], pr[:, j, P * kb:P * kb + P], ident)
                (hi, lo), pt_free, pt_readers = rot_pt.take()
                t = split(hi, lo, bank[:, :], [m, *pt_free], dve)
                readers += t
                turned[kb] = hi, lo, pt_readers, t
                return m

            m = turn(0)
            for kb in range(i + 1):
                if kb < i:
                    m = turn(kb + 1)
                yield
                hi, lo, pt_readers, t = turned[kb]
                pe.wait(*t)
                vs = slice(P * br + DH * g, P * br + DH * g + DH)
                last_one = br == 1 and kb == i
                held["pv", i] = products(o_bank[0:DH, :], v_hi[:, kb, vs], v_lo[:, kb, vs], hi, lo,
                                         start=False, stop=last_one)
                pt_readers.append(held["pv", i])
            pr_readers.append(m)

        def tile_out(i):
            qs = slice(P * i, P * i + P)
            got["on", i] = []
            for g, (o_bank, _, o_readers) in enumerate(held["o", i]):
                rows = slice(DH * g, DH * g + DH)
                src = o_bank[0:DH, :].rearrange("p (f q) -> p f q", f=REP)
                marks = split(on_hi[rows, :, qs], on_lo[rows, :, qs], src, [held["pv", i]], dve)
                o_readers += marks
                got["on", i] += marks
            yield

        def nsa_core():
            order = [(i, b, g) for i in range(TT) for b, g in ((None, 0), (0, 0), (0, 1), (1, 0), (1, 1))]

            def back(i, b, g):
                if b is None:
                    yield from cmp_values(i)
                else:
                    yield from key_values(i, b, g)
                    if (b, g) == (1, 1):
                        yield from tile_out(i)

            behind = iter(())
            for i, b, g in order:
                front = cmp_scores(i) if b is None else key_scores(i, b, g)
                for n, _ in enumerate(front):
                    if n >= LEAD:
                        next(behind, None)
                    yield
                yield from behind
                behind = back(i, b, g)
            yield from behind

        def evac_mix_gate(f, o, done):
            m, got["mix", 0, f] = sigmoid(mix_gates[:, f, :], o, [done])
            return [m]

        gate_tiles = by_column_tiles("merge gates", h_hi, h_lo, ready_h, evac_mix_gate, EARLY)
        for n, _ in enumerate(nsa_core()):
            if n % GATE_EVERY == 0:
                next(gate_tiles, None)
        finish(gate_tiles)
        core_banks.readers[:] = score_banks.readers + turn_banks.readers + o_banks.readers
        nsa_free = last()
        assert nc.sbuf_base <= top
        nsa.close()

        merge = ExitStack()
        og_hi = sb("og_hi", [KD, S], F32R, ctx=merge)
        og_lo = sb("og_lo", [KD, S], F32R, ctx=merge)
        for lane in (act, dve, pool, pe):
            lane.wait(*nsa_free)
        og_ready = [split(og_hi[:, f, :], og_lo[:, f, :], o_gla[:, f, :], [got["og", f]], pool) for f in range(KD)]
        on_ready = sum((got["on", i] for i in range(TT)), [])
        mixed_marks = []
        gla_gates = sb("gla_gates", [2, S], ctx=merge)
        late_gates = [gla_gates, kc_vc]
        late_free = {(w, f): [] for w in range(2) for f in range(2)}

        def merge_all():
            gla_part = {}

            def late_gate(which, j):
                def evac(f, o, done):
                    m, got["mix", which, j + f] = sigmoid(late_gates[which][:, f, :], o, [done, *late_free[which, f]])
                    return [m]
                return by_column_tiles("merge gates", h_hi, h_lo, ready_h, evac, 2)

            def evac_gla(j):
                def evac(f, o, done):
                    gate = mix_gates[:, j + f, :] if j < EARLY else gla_gates[:, f, :]
                    m = dve.do(nc.vector.tensor_tensor, o_gla[:, j + f, :], o, gate, ALU.mult,
                               after=[done, got["mix", 0, j + f], *og_ready[j + f]])
                    gla_part[j + f] = m
                    late_free[0, f] = [m]
                    return [m]
                return evac

            def evac_nsa(j):
                def evac(f, o, done):
                    t = kc_vc[:, f, :]
                    m = dve.do(nc.vector.tensor_tensor, t, o, t, ALU.mult, after=[done, got["mix", 1, j + f]])
                    s = dve.do(nc.vector.tensor_tensor, o_gla[:, j + f, :], o_gla[:, j + f, :], t, ALU.add,
                               after=[m, gla_part[j + f]])
                    mixed_marks.append(s)
                    late_free[1, f] = [s]
                    return [m]
                return evac

            for j in range(0, KD, 2):
                if j >= EARLY:
                    yield from late_gate(0, j)
                yield from by_column_tiles("proj gla", og_hi, og_lo, lambda k: og_ready[k], evac_gla(j), 2)
                yield from late_gate(1, j)
                yield from by_column_tiles("proj nsa", on_hi, on_lo, lambda k: on_ready, evac_nsa(j), 2, nk=4)

        finish(merge_all())
        h_free = [(pe, pe.count)]
        for f in range(KD):
            h_ready[f] = split(h_hi[:, f, :], h_lo[:, f, :], o_gla[:, f, :], [mixed_marks[f], *h_free],
                               dve if f % 2 else pool)
        merge_free = last()
        assert nc.sbuf_base <= top
        merge.close()
        nsa_io.close()
        mixer.close()

        x1 = sb("x1", [TT, D])
        gain_row = sb("gain_row", [D])
        load_gain = Loads(sem("load_gain"))
        for lane in (act, dve, pool, sp):
            lane.wait(*merge_free)
        load_x1 = Loads(sem("load_x1"))
        got_x1 = load_x1.start(sp, x1[:, :, :], x_rows)

        def load_gain_row(src, after):
            return load_gain.start(sp, gain_row[:, :], src.partition_broadcast(P), after)

        def add_to_x1(i, acc, ready, got_gain, x_ready):
            r, m = rstd(0, i)
            for n, half in enumerate(halves):
                a, x = acc[:, i, half], x1[:, i, half]
                p = dve.do(nc.vector.scalar_tensor_tensor, a, a, r, gain_row[:, half], ALU.mult, ALU.mult,
                           after=[m, got_gain, *ready])
                p = dve.do(nc.vector.tensor_tensor, x, x, a, ALU.add, after=[p, *x_ready])
                square(1, i, n, x, [p])

        with ExitStack() as scope:
            acc = sb("acc_mix", [TT, D], ctx=scope)
            acc_marks = {}
            turns = []
            got_gain = load_gain_row(T["norm_mix_post"][0], [])

            def evac_out(n, i, o, done):
                m = act.do(nc.scalar.activation, acc[:, i, halves[n]], o, ACT.Copy, after=[done])
                acc_marks[n, i] = m
                s = square(0, i, n, o, [done])
                if n == 1:
                    turn_behind(turns, i, [lambda: add_to_x1(i, acc, [acc_marks[0, i], m], got_gain, [got_x1]),
                                           lambda: norm_tile(i, x1[:, i, :], acc[:, i, :], "norm_ffn_pre", [done])])
                return [m, s]

            finish(by_row_tiles("out", h_hi, h_lo, ready_h, evac_out, KD))
        acc_free = last()

        h_last = []

        def ffn(tag, groups, evac_pair, n_up, free, into, then):
            scope = ExitStack()
            acc = sb(f"acc{tag}", [TT, D], ctx=scope)
            total = acc if into is None else into
            most = max(n for _, n in groups)
            f_hi = sb(f"f_hi{tag}", [2, most, S], F32R, ctx=scope)
            f_lo = sb(f"f_lo{tag}", [2, most, S], F32R, ctx=scope)
            ft = sb(f"ft{tag}", [2, S], ctx=scope)
            rot = Rotating([ft[:, i, :] for i in range(2)])
            for lane in (act, dve, pool, sp):
                lane.wait(*free)
            f_free, f_ready, acc_ready = [[], []], {}, {}

            def up(g):
                t0, nt = groups[g]
                b = g % 2
                state_ = {}

                def evac(f, o, done):
                    t = f // n_up
                    if f % n_up == 0:
                        state_["s"] = rot.take()
                    s, s_free, s_readers = state_["s"]
                    marks, r = evac_pair(f % n_up, s, s_free, o, done, f_hi[:, b, t, :], f_lo[:, b, t, :], f_free[b],
                                         s_readers)
                    if marks:
                        f_ready[g, t] = marks
                    return r

                yield from by_column_tiles(f"up {tag}", h_hi, h_lo, ready_h, evac, nt * n_up)

            def down(g):
                t0, nt = groups[g]
                b = g % 2

                def evac(n, i, o, done):
                    a = total[:, i, halves[n]]
                    if g == 0 and into is None:
                        m = dve.do(nc.vector.tensor_copy, a, o, after=[done])
                    else:
                        m = dve.do(nc.vector.tensor_tensor, a, a, o, ALU.add, after=[done, *acc_ready.get((n, i), [])])
                    acc_ready[n, i] = [m]
                    if g == len(groups) - 1:
                        then(acc, n, i, m)
                    return [m]

                yield from by_row_tiles(f"down {tag}", f_hi[:, b, :, :], f_lo[:, b, :, :], lambda k: f_ready[g, k], evac, nt)
                f_free[b] = [(pe, pe.count)]

            for g in range(len(groups) + 1):
                if g < len(groups):
                    finish(up(g))
                if g == len(groups):
                    h_last[:] = [(pe, pe.count)]
                    exp_ln_tables()
                if g:
                    finish(down(g - 1))
            return scope

        def swiglu(which, s, s_free, o, done, hi, lo, free, s_readers):
            if which == 0:
                m = act.do(nc.scalar.activation, s, o, ACT.Silu, after=[done, *s_free])
                s_readers.append(m)
                return None, [m]
            m = dve.do(nc.vector.tensor_tensor, s, s, o, ALU.mult, after=[done, *s_readers, *s_free])
            a = act.do(nc.scalar.activation, hi, s, ACT.Copy, after=[m, *free])
            b = dve.do(nc.vector.tensor_tensor, lo, s, hi.bitcast(F32), ALU.subtract, after=[a, *free])
            s_readers[:] = [m, a, b]
            return [a, b], [m]

        def relu2(which, s, s_free, o, done, hi, lo, free, s_readers):
            r = act.do(nc.scalar.activation, s, o, ACT.Relu, after=[done, *s_free])
            m = dve.do(nc.vector.tensor_tensor, s, s, s, ALU.mult, after=[r, *s_free])
            a = act.do(nc.scalar.activation, hi, s, ACT.Copy, after=[m, *free])
            b = dve.do(nc.vector.tensor_tensor, lo, s, hi.bitcast(F32), ALU.subtract, after=[a, *free])
            s_readers[:] = [m, a, b]
            return [a, b], [r]

        got_gain = load_gain_row(T["norm_ffn_post"][0], last(dve))

        def then_1(acc, n, i, m):
            square(0, i, n, acc[:, i, halves[n]], [m])
            if n == 1:
                turn_behind(turns, i, [lambda: add_to_x1(i, acc, [m], got_gain, []),
                                       lambda: norm_tile(i, x1[:, i, :], acc[:, i, :], "g_attn_2", h_last)])

        scope = ffn("1", FFN1_GROUPS, swiglu, 2, acc_free, None, then_1)
        b2_free = last()
        scope.close()

        scope = ExitStack()
        cat = sb("cat", [KD, S], ctx=scope)
        q2 = sb("q2", [3, S], ctx=scope)
        k2 = sb("k2", [3, S], ctx=scope)
        qk2_free = {f: [] for f in range(4)}
        v2 = sb("v2", [TT, 512], ctx=scope)
        ua = sb("ua", [2, KA - 1 + S], ctx=scope)
        gb = sb("gb", [2, KB - 1 + S], ctx=scope)
        wa = C("cmp_dist")[:, 0:2 * KA].rearrange("p (f k) -> p f k", k=KA)
        wb = C("cmp_mask")[:, 0:2 * KB].rearrange("p (f k) -> p f k", k=KB)
        for lane in (act, dve, pool, sp):
            lane.wait(*b2_free)
        load_wa, load_wb = Loads(sem("load_wa")), Loads(sem("load_wb"))
        got_wa = load_wa.start(sp, C("cmp_dist")[:, 0:2 * KA], T["taps_a"])
        got_wb = load_wb.start(sp, C("cmp_mask")[:, 0:2 * KB], T["taps_b"])
        zero_ua = pool.do(nc.gpsimd.memset, ua[:, :, 0:KA - 1], 0.0)
        zero_gb = pool.do(nc.gpsimd.memset, gb[:, :, 0:KB - 1], 0.0)

        def evac_v2(n, i, o, done):
            got["v2", i] = act.do(nc.scalar.activation, v2[:, i, :], o, ACT.Copy, after=[done])
            return [got["v2", i]]

        def evac_qk2(f, o, done):
            slot, after = f // 2 % 3, [done, *(qk2_free[f // 2 - 3] if f >= 6 else [])]
            if f % 2 == 0:
                m = act.do(nc.scalar.activation, q2[:, slot, :], o, ACT.Copy, scale=DH ** -0.5, after=after)
            else:
                m = act.do(nc.scalar.activation, k2[:, slot, :], o, ACT.Copy, after=after)
            got["qk2", f] = m
            return [m]

        def evac_glu(f, o, done):
            g = gb[:, f % 2, KB - 1:KB - 1 + S]
            if f < 2:
                got["glu", f] = act.do(nc.scalar.activation, g, o, ACT.Copy, after=[done])
                return [got["glu", f]]
            t, t_free, t_readers = rot_ct.take()
            m1, m = sigmoid(t, o, [done, *t_free])
            m = dve.do(nc.vector.tensor_tensor, g, g, t, ALU.mult, after=[m, got["glu", f - 2]])
            t_readers.append(m)
            got["gb", f - 2] = m
            return [m1]

        def evac_acah(f, o, done):
            u = ua[:, f % 2, KA - 1:KA - 1 + S]
            if f < 2:
                got["ac", f] = act.do(nc.scalar.activation, u, o, ACT.Copy, after=[done])
                return [got["ac", f]]
            got["ua", f - 2] = dve.do(nc.vector.tensor_tensor, u, u, o, ALU.mult, after=[done, got["ac", f - 2]])
            return [got["ua", f - 2]]

        def conv(name, out_ap, src, w, taps, after, bias_ap=None):
            more = [ALU.add] if bias_ap is not None else []
            m = dve.do(nc.vector.tensor_scalar, out_ap, src[:, 0:S], w[:, 0:1], bias_ap, ALU.mult, *more, after=after)
            for j in range(1, taps):
                yield
                m = dve.do(nc.vector.scalar_tensor_tensor, out_ap, src[:, j:j + S], w[:, j:j + 1], out_ap, ALU.mult,
                           ALU.add, after=[m])
            got[name] = m
            yield

        def evac_ab(f, o, done):
            got["cat", f] = dve.do(nc.vector.tensor_tensor, cat[:, f, :], cat[:, f, :], o, ALU.mult, after=[done, got["conv_a", f]])
            return [got["cat", f]]

        rot_ct = Rotating([junk[:, :], gain_row[:, 0:S], gain_row[:, S:2 * S], C("dist")])

        def conv_b():
            for f in range(2):
                yield from conv(("conv_b", f), cat[:, 2 + f, :], gb[:, f, :], wb[:, f, :], KB,
                                [got["gb", f], got_wb, zero_gb], V("b_conv_b_2", f))

        def norm_b():
            bank, bank_free, readers = core_banks.take()
            pe.wait(*bank_free, got["conv_b", 0], got["conv_b", 1])
            for f in range(2):
                m = pe.do(nc.tensor.matmul, bank[:, :], C("ones"), cat[:, 2 + f, :], start=(f == 0),
                                                             stop=(f == 1))
            sq = []
            for f in range(2):
                d = dve.do(nc.vector.scalar_tensor_tensor, cat[:, 2 + f, :], bank[:, :], -1.0 / CW, cat[:, 2 + f, :], ALU.mult, ALU.add, after=[m])
                readers.append(d)
                sq.append(act.do(nc.scalar.activation, gb[:, f, 0:S], cat[:, 2 + f, :], ACT.Square, after=[d]))
            yield
            bank, bank_free, readers = core_banks.take()
            pe.wait(*bank_free, *sq)
            for f in range(2):
                m = pe.do(nc.tensor.matmul, bank[:, :], C("ones"), gb[:, f, 0:S], start=(f == 0),
                                                             stop=(f == 1))
            t, t_free, t_readers = rot_ct.take()
            m = act.do(nc.scalar.activation, t, bank[:, :], ACT.Ln, bias=eps_ln, scale=1.0 / CW, after=[m, *t_free])
            readers.append(m)
            m = act.do(nc.scalar.activation, t, t, ACT.Exp, scale=-0.5, after=[m])
            yield
            for f in range(2):
                c = cat[:, 2 + f, :]
                k = dve.do(nc.vector.tensor_tensor, c, c, t, ALU.mult, after=[m, d])
                k = dve.do(nc.vector.tensor_scalar, c, c, V("ln_b_g_2", f), V("ln_b_b_2", f), ALU.mult,
                                                               ALU.add, after=[k])
                got["cat", 2 + f] = act.do(nc.scalar.activation, c, c, ACT.Silu, after=[k])
            exp_ln_tables()
            yield
            t_readers.append(k)

        widths = [S - P * j for j in range(TT)]
        units = [[(2, 0), (3, widths[2])], [(1, 0)], [(0, 0)]]
        n_units = len(units)
        u_width = [sum(widths[j] for j, _ in u) for u in units]
        u_start = [sum(u_width[:n]) for n in range(n_units)]
        start_of = {j: u_start[n] + c for n, u in enumerate(units) for j, c in u}
        total = sum(widths)
        at = sb("at", [total], ctx=scope)
        sp_hi = sb("sp_hi", [2, total], F32R, ctx=scope)
        sp_lo = sb("sp_lo", [2, total], F32R, ctx=scope)
        z_banks = Rotating(banks[2:8])
        y_bank, linear_bank = banks[1], banks[0]
        z_held, sp_marks, a_marks, y_free = {}, {}, {}, []
        at_free = [[] for _ in units]
        sp_free = [[], []]

        def softplus(h):
            f, r = h // 2, DH * (h % 2)
            for n, unit in enumerate(units):
                w = u_width[n]
                bank, bank_free, readers = z_banks.take()
                z_held[h, n] = bank, readers
                pe.wait(*bank_free, got["qk2", 2 * f], got["qk2", 2 * f + 1])
                for c, (j, at_col) in enumerate(unit):
                    m = pe.do(nc.tensor.matmul, bank[:, at_col:at_col + widths[j]], k2[r:r + DH, f % 3, P * j:P * j + P],
                              q2[r:r + DH, f % 3, P * j:S], start=(c == 0), stop=False, skip_group_check=True)
                qk2_free[f] = [m]
                buf, t_free, t_readers = rot_ct.take()
                t = buf[:, 0:w]
                m = act.do(nc.scalar.activation, t, bank[:, 0:w], ACT.Abs, after=[m, *t_free])
                m = act.do(nc.scalar.activation, t, t, ACT.Exp, scale=-1.0, after=[m])
                m = act.do(nc.scalar.activation, t, t, ACT.Ln, bias=1.0, after=[m])
                yield
                z_read = dve.do(nc.vector.scalar_tensor_tensor, t, bank[:, 0:w], 0.0, t, ALU.max, ALU.add, after=[m])
                for j, at_col in unit:
                    d = t[:, at_col:at_col + P]
                    m = dve.do(nc.vector.tensor_tensor, d, d, C("before"), ALU.mult, after=[z_read])
                cs = slice(u_start[n], u_start[n] + w)
                marks = split(sp_hi[:, h % 2, cs], sp_lo[:, h % 2, cs], t, [m, *sp_free[h % 2]], dve)
                t_readers += marks
                sp_marks[h, n] = [z_read, *marks]
                yield

        def stick(h):
            f, r = h // 2, DH * (h % 2)
            sp = [sp_hi[:, h % 2, :], sp_lo[:, h % 2, :]]

            def values(n):
                pe.wait(a_marks[h, n])
                for j, _ in units[n]:
                    a = at[:, start_of[j]:start_of[j] + widths[j]]
                    m = pe.do(nc.tensor.matmul, y_bank[r:r + DH, P * j:S], v2[:, j, DH * h:DH * h + DH], a,
                              start=(n == 0 and j == units[0][0][0]), stop=(j == 0), skip_group_check=True,
                              after=[got["v2", j]])
                at_free[n] = [m]
                return m

            for n, unit in enumerate(units):
                bank, readers = z_held[h, n]
                pe.wait(*sp_marks[h, n], consts_r)
                for j, c0 in unit:
                    for i in range(j, TT):
                        c = c0 + P * (i - j)
                        for src in sp:
                            pe.run(nc.tensor.matmul, bank[:, c:c0 + widths[j]], (upper_r if i == j else ones_r)[:, :],
                                   src[:, start_of[i]:start_of[i] + widths[i]], start=False, stop=False,
                                   skip_group_check=True)
                    m = pe.do(nc.tensor.matmul, bank[:, c0:c0 + P], ident_r[:, :], block_r[:, :], start=False,
                              stop=True, skip_group_check=True)
                a = at[:, u_start[n]:u_start[n] + u_width[n]]
                a_marks[h, n] = act.do(nc.scalar.activation, a, bank[:, 0:u_width[n]], ACT.Exp, after=[m, *at_free[n]])
                readers += [a_marks[h, n], sp_marks[h, n][0]]
                yield
                if n == 1 and h % 2 == 0:
                    pe.wait(*y_free)
                if n:
                    values(n - 1)
                    yield
            sp_free[h % 2] = [m]
            m = values(n_units - 1)
            if h % 2:
                got["cat", 4 + f] = act.do(nc.scalar.activation, cat[:, 4 + f, :], y_bank[:, :], ACT.Copy, after=[m])
                y_free[:] = [got["cat", 4 + f]]
            yield

        finish(by_column_tiles("glu 2", h_hi, h_lo, ready_h, evac_glu, 4))
        on_vector = conv_b()

        def with_conv(gen, taps):
            for _ in gen:
                for _ in range(taps):
                    next(on_vector, None)
                yield

        finish(with_conv(by_row_tiles("v 2", h_hi, h_lo, ready_h, evac_v2, KD, halves=(0,)), 3))
        tiles_qk = by_column_tiles("qk 2", h_hi, h_lo, ready_h, evac_qk2, 8)
        for _ in range(4):
            next(tiles_qk)
            for _ in range(3):
                next(on_vector, None)

        def rest():
            for _ in range(2):
                yield next(tiles_qk)
            yield from by_column_tiles("ac ah 2", h_hi, h_lo, ready_h, evac_acah, 4)
            for _ in range(2):
                yield next(tiles_qk)
            for f in range(2):
                finish(conv(("conv_a", f), cat[:, f, :], ua[:, f, :], wa[:, f, :], KA, [got["ua", f], got_wa, zero_ua]))
            yield from by_column_tiles("ab 2", h_hi, h_lo, ready_h, evac_ab, 2)

        linear_readers = list(linear_banks.readers)
        y_free += linear_readers[1]
        linear_banks.bufs, linear_banks.at, linear_banks.readers = [linear_bank], -1, [linear_readers[0]]
        z_banks.readers = core_banks.readers
        fills2 = rest()
        step = 0
        finish(softplus(0))
        for h in range(SBH):
            ahead = softplus(h + 1) if h + 1 < SBH else iter(())
            for _ in stick(h):
                next(ahead, None)
                if step % FILL2_EVERY == 0:
                    next(fills2, None)
                step += 1
                for _ in range(2):
                    next(on_vector, None)
            finish(ahead)
        finish(fills2, on_vector)
        linear_banks.bufs, linear_banks.at = banks[0:2], -1
        linear_banks.readers = [linear_banks.readers[0], list(y_free)]
        core_banks.readers[:] = z_banks.readers
        core_banks.at = -1
        h_free = [(pe, pe.count)]
        finish(norm_b())
        for f in range(KD):
            h_ready[f] = split(h_hi[:, f, :], h_lo[:, f, :], cat[:, f, :], [got["cat", f], *h_free],
                               dve if f % 2 else pool)
        cat_free = last()
        scope.close()

        with ExitStack() as scope:
            hs = sb("hs", [TT, D], ctx=scope)
            for lane in (dve, pool, act):
                lane.wait(*cat_free)

            def evac_res(n, i, o, done):
                a = x1[:, i, halves[n]]
                m = dve.do(nc.vector.tensor_tensor, a, a, o, ALU.add, after=[done])
                square(1, i, n, a, [m])
                if n == 1:
                    turn_behind(turns, i, [lambda: None,
                                           lambda: norm_tile(i, x1[:, i, :], hs[:, i, :], "g_ffn_2", [done], [m])])
                return [m]

            finish(by_row_tiles("out 2", h_hi, h_lo, ready_h, evac_res, KD))
        hs_free = last()

        got_gain = load_gain_row(T["g_final_2"], last(dve, act))
        out_rows = out.rearrange("a (i p) d -> (a p) i d", p=P)
        stored = Loads(sem("stored"))
        ends = []

        def then_2(acc, n, i, m):
            square(1, i, n, x1[:, i, halves[n]], [m])
            if n == 1:
                r, m = rstd(1, i)
                for half in halves:
                    k = dve.do(nc.vector.scalar_tensor_tensor, acc[:, i, half], x1[:, i, half], r, gain_row[:, half],
                               ALU.mult, ALU.mult, after=[m, got_gain])
                    ends.append(stored.start(sp, out_rows[:, i, half], acc[:, i, half], [k]))

        scope = ffn("2", FFN2_GROUPS, relu2, 1, hs_free, x1, then_2)
        sp.wait(ends[-1])
        scope.close()
        assert state["used"] == len(chunks)

        block = outer.enter_context(nc.Block())

        @block.sync
        def _(e):
            sp.write()

        @block.tensor
        def _(e):
            pe.write()

        @block.scalar
        def _(e):
            act.write()

        @block.vector
        def _(e):
            dve.write()

        @block.gpsimd
        def _(e):
            pool.write()


def columns_of(v):
    return np.reshape(v, (-1, P)).T


def block_diagonal(w):
    out = np.zeros((NG * DH, w.shape[1], NG * DH), w.dtype)
    for g in range(NG):
        out[DH * g:DH * g + DH, :, DH * g:DH * g + DH] = w
    return out.reshape(NG * DH, -1)


def lay_out(inputs):
    parts = []
    for _, name, row0, nk, c in plan():
        w = inputs[name][0]
        if name == "w_proj_nsa":
            w = w[NSA_ROWS]
        w = w[row0:row0 + P * nk][:, c]
        parts.append(np.ascontiguousarray(w.reshape(nk, P, len(c)).transpose(1, 0, 2)).reshape(-1))
    return np.concatenate(parts)


_DIRECT = ["x", "gla_w_alpha2", "norm_mix_post",
           "norm_ffn_post", "g_final_2"]


def kernel(**inputs):
    import concourse.bacc as _bacc
    from concourse.bass_utils import run_bass_kernel_spmd as _run

    inputs = {k: np.asarray(v) for k, v in inputs.items()}
    nc = _bacc.Bacc("TRN2", target_bir_lowering=False, num_devices=1)
    arrays = {}

    def give(name, a):
        a = np.ascontiguousarray(a)
        arrays[f"in_{name}"] = a
        return nc.dram_tensor(f"in_{name}", a.shape, mybir.dt.from_np(a.dtype), kind="ExternalInput").ap()

    T = {name: give(name, inputs[name]) for name in _DIRECT}
    for n in "kv":
        T[f"pe_{n}"] = give(f"pe_{n}", np.concatenate([inputs[f"nsa_cmp_pe_{n}"][0].T] * NG))
    for n in "ab":
        w = inputs[f"w_conv_{n}_2"][0]
        T[f"taps_{n}"] = give(f"taps_{n}", w.reshape(len(w), 2, P).transpose(2, 1, 0).reshape(P, -1))
    for n in "kv":
        w = inputs[f"nsa_cmp_w1_{n}"][0].reshape(CL, DH, DH).transpose(1, 0, 2)
        T[f"w1_{n}"] = give(f"w1_{n}", block_diagonal(w))
        T[f"w2_{n}"] = give(f"w2_{n}", block_diagonal(inputs[f"nsa_cmp_w2_{n}"][0][:, None, :]))
    wstream = give("wstream", lay_out(inputs))
    vectors = give("vectors", np.concatenate([columns_of(inputs[n]) for n, _ in _vec], axis=1))
    consts = give("constants", constants())
    out = nc.dram_tensor("out", (1, S, D), F32, kind="ExternalOutput").ap()
    program(nc, T, wstream, vectors, consts, out)
    r = _run(nc, [arrays], core_ids=[0])
    return r.results[0]["out"]
```

```python
from contextlib import ExitStack

import numpy as np

import concourse.bass as bass
from concourse import mybir

F32 = mybir.dt.float32
F32R = mybir.dt.float32r
U32 = mybir.dt.uint32
ALU = mybir.AluOpType
ACT = mybir.ActivationFunctionType
AXX = mybir.AxisListType.X

P = 128
S = 512
D = 1024
TT = S // P
KD = D // P
RMS_EPS = 1e-6
LN_EPS = 1e-5
NEG = -1e30

GLA_H, DK, DV, RANK, TAU, CHUNK = 4, 128, 256, 16, 16.0, 64
NCH = S // CHUNK
NH, NG, DH = 8, 2, 64
REP = NH // NG
CL, CS = 32, 16
NCMP = (S - CL) // CS + 1
D_FF, D_FF2 = 2816, 4096
CW, KA, KB = 256, 3, 31
SLOPES = 2.0 ** (-8.0 * (np.arange(NH) + 1) / NH)
SBH = 8

FILLS = [(1, 3, 5, 7), (1, 3, 5), (1, 3, 5), (0, 2, 4, 6)]
FILL_EVERY = 5

SCALED_BY_ACT = (3,)
BETWEEN = 3
LEAD = 2
GATE_STEPS = (4, 14, 24, 36, 50, 66, 84, 104)

FILL2_STEPS = (0, 3, 6, 9, 12, 15, 20, 24, 30, 36, 37)

_w = dict(gq=512, gk=512, gv=1024, gr=1024, ga=16, nq=512, kc=128, vc=128, ks=128, vs=128, kw=128,
          vw=128, gate=24, mg=1024, mn=1024)
OFF1 = dict(zip(_w, np.cumsum([0] + list(_w.values()))[:-1].tolist()))
_w2 = dict(ab=256, ac=256, ah=256, glu=512, q=512, k=512, v=512)
OFF2 = dict(zip(_w2, np.cumsum([0] + list(_w2.values()))[:-1].tolist()))

CH = 2048
HALF = CH // 2


def cols(start, n):
    return list(range(start, start + n))


def groups_of(n, sizes):
    out, at = [], 0
    for s in sizes:
        out.append((at, s))
        at += s
    assert at == n
    return out


NSA_ROWS = sum((cols(DH * j, DH) + cols(DH * (REP + j), DH) for j in range(REP)), [])
FFN1_GROUPS = groups_of(D_FF // P, [6, 6, 5, 5])
FFN2_GROUPS = groups_of(D_FF2 // P, [6, 6, 5, 5, 5, 5])


def plan():
    out = []

    def by_column(layer, w, c, nk=KD):
        n = CH // nk
        for a in range(0, len(c), n):
            out.append((layer, w, 0, nk, c[a:a + n]))

    def by_row(layer, w, c, row0, nk):
        for a in range(0, nk, 4):
            out.append((layer, w, row0 + a * P, min(4, nk - a), c))

    o = OFF1
    by_column("gla a", "w_in", cols(o["ga"], 16))
    for n in range(2):
        by_row("gla v", "w_in", cols(o["gv"] + 512 * n, 512), 0, KD)

    def gla_qk(h):
        by_column(f"gla qk {h}", "w_in", cols(o["gq"] + DK * h, DK) + cols(o["gk"] + DK * h, DK))

    nq = [sum((cols(o["nq"] + DH * j, DH) + cols(o["nq"] + DH * (REP + j), DH) for j in pair), [])
          for pair in ((0, 1), (2, 3))]
    gla_qk(0)
    by_row("nsa v gate", "w_in", cols(o["vs"], P) + cols(o["vw"], P) + cols(o["gate"], 24), 0, KD)
    gla_qk(1)
    by_column("nsa kc vc", "w_in", cols(o["kc"], P) + cols(o["vc"], P))
    by_column("gla r", "w_in", cols(o["gr"], 2 * P))
    gla_qk(2)
    by_column("gla r", "w_in", cols(o["gr"] + 2 * P, 2 * P))
    gla_qk(3)
    by_column("gla r", "w_in", cols(o["gr"] + 4 * P, 2 * P))
    by_column("nsa ks kw", "w_in", cols(o["ks"], P) + cols(o["kw"], P))
    by_column("gla r", "w_in", cols(o["gr"] + D - 2 * P, 2 * P))
    by_column("nsa q", "w_in", nq[0])
    by_column("nsa q", "w_in", nq[1])
    by_column("merge gates", "w_in", cols(o["mg"], D))
    for j in range(0, KD, 2):
        by_column("merge gates", "w_in", cols(o["mn"] + P * j, 2 * P))
        by_column("proj gla", "w_proj_gla", cols(P * j, 2 * P))
        by_column("proj nsa", "w_proj_nsa", cols(P * j, 2 * P), 4)
    for n in range(2):
        by_row("out", "w_out", cols(512 * n, 512), 0, KD)

    def ffn(tag, groups, ups, down):
        for g in range(len(groups) + 1):
            if g < len(groups):
                t0, nt = groups[g]
                if len(ups) == 2:
                    for t in range(t0, t0 + nt):
                        for u in ups:
                            by_column(f"up {tag}", u, cols(P * t, P))
                else:
                    by_column(f"up {tag}", ups[0], cols(P * t0, P * nt))
            if g:
                t0, nt = groups[g - 1]
                for n in range(2):
                    by_row(f"down {tag}", down, cols(512 * n, 512), P * t0, nt)

    ffn(1, FFN1_GROUPS, ["w_ffn_gate", "w_ffn_up"], "w_ffn_down")
    o = OFF2
    by_column("glu 2", "w_in_2", cols(o["glu"], 512))
    by_row("v 2", "w_in_2", cols(o["v"], 512), 0, KD)

    def qk2(f):
        by_column("qk 2", "w_in_2", cols(o["q"] + P * f, P) + cols(o["k"] + P * f, P))

    for f in range(3):
        qk2(f)
    by_column("ac ah 2", "w_in_2", cols(o["ac"], 512))
    qk2(3)
    by_column("ab 2", "w_in_2", cols(o["ab"], 256))
    for n in range(2):
        by_row("out 2", "w_out_2", cols(512 * n, 512), 0, KD)
    ffn(2, FFN2_GROUPS, ["w_ff1_2"], "w_ff2_2")
    return out


_vec = [("norm_mix_pre", 8), ("norm_ffn_pre", 8), ("g_attn_2", 8), ("g_ffn_2", 8), ("gla_b_alpha", 4),
        ("gla_norm_g", 2), ("b_conv_b_2", 2), ("ln_b_g_2", 2), ("ln_b_b_2", 2)]
VEC, NVEC = {}, 0
for _name, _n in _vec:
    VEC[_name] = (NVEC, _n)
    NVEC += _n
_con = [("ident", P), ("gla_mask", P), ("upper", P), ("block", P), ("before", P), ("ones", P),
        ("eps", 2), ("dist", S), ("cmp_dist", TT * NCMP), ("cmp_mask", TT * 32),
        ("q_scale", REP), ("slopes", NH), ("minus_slopes", NH)]
CON, NCON = {}, 0
for _name, _n in _con:
    CON[_name] = (NCON, _n)
    NCON += _n


def constants():
    p, c = np.arange(P)[:, None], np.arange(P)[None, :]
    out = np.zeros((P, NCON), np.float32)

    def put(name, a):
        o, n = CON[name]
        out[:, o:o + n] = np.broadcast_to(a, (P, n))

    put("ident", p == c)
    put("gla_mask", (p <= c) & (p // CHUNK == c // CHUNK))
    put("upper", -1.0 * (p >= c))
    put("block", np.where(p < c, 0.0, NEG))
    put("before", p < c)
    put("ones", 1.0)
    put("eps", np.array([RMS_EPS, LN_EPS]))
    key = np.arange(S)[None, :] - (S - P)
    put("dist", np.where(key <= p, key - p, NEG))
    t = p + P * np.arange(TT)[None, :]
    end = CS * np.arange(NCMP) + CL - 1
    seen = end[None, None, :] <= t[:, :, None]
    put("cmp_dist", np.where(seen, end[None, None, :] - t[:, :, None], NEG).reshape(P, -1))
    m = np.zeros((P, TT, 32))
    m[:, :, :NCMP] = seen
    put("cmp_mask", m.reshape(P, -1))
    head = np.where(p < DH, 0, REP) + np.arange(REP)[None, :]
    put("q_scale", DH ** -0.5 / SLOPES[head])
    put("slopes", SLOPES)
    put("minus_slopes", -SLOPES)
    return out


class Lane:

    def __init__(self, engine, sem):
        self.engine, self.sem, self.count, self.queue, self.waited = engine, sem, 0, [], {}

    def wait(self, *marks):
        for lane, value in marks:
            if self.waited.get(id(lane), 0) < value:
                self.waited[id(lane)] = value
                self.queue.append((self.engine.wait_ge, (lane.sem, value), {}, None))

    def run(self, what, *args, after=(), **named):
        self.wait(*after)
        self.queue.append((what, args, named, None))

    def do(self, what, *args, after=(), **named):
        self.wait(*after)
        self.count += 1
        self.queue.append((what, args, named, (self.sem, 1)))
        return self, self.count

    def write(self):
        for what, args, named, signal in self.queue:
            instruction = what(*args, **named)
            if signal:
                instruction.then_inc(*signal)


class Loads:

    def __init__(self, sem):
        self.sem, self.count = sem, 0

    def start(self, lane, out, in_, after=()):
        lane.wait(*after)
        self.count += 16
        lane.queue.append((lane.engine.dma_start, (out, in_), {}, (self.sem, 16)))
        return self, self.count


class Rotating:

    def __init__(self, bufs):
        self.bufs, self.at, self.readers = bufs, -1, [[] for _ in bufs]

    def take(self):
        self.at = (self.at + 1) % len(self.bufs)
        marks, self.readers[self.at] = self.readers[self.at], []
        return self.bufs[self.at], marks, self.readers[self.at]


def program(nc, T, wstream, vectors, consts, out):
    outer = ExitStack()
    with outer:
        def sb(name, shape, dt=F32, ctx=outer):
            return ctx.enter_context(nc.sbuf_tensor(name, [P] + shape, dt))

        def sem(name):
            return outer.enter_context(nc.semaphore(name))

        pe = Lane(nc.tensor, sem("pe_done"))
        act = Lane(nc.scalar, sem("act_done"))
        dve = Lane(nc.vector, sem("dve_done"))
        pool = Lane(nc.gpsimd, sem("pool_done"))
        sp = Lane(nc.sync, sem("sp_done"))
        banks = [outer.enter_context(nc.psum_tensor(f"bank{i}", [P, 512], F32)) for i in range(8)]
        linear_banks = Rotating(banks[0:2])
        core_banks = Rotating(banks[2:8])

        con = sb("con", [NCON])
        vec = sb("vec", [NVEC])

        def C(name):
            o, n = CON[name]
            return con[:, o:o + n]

        def V(name, j):
            return vec[:, VEC[name][0] + j:VEC[name][0] + j + 1]

        eps_rms, eps_ln = C("eps")[:, 0:1], C("eps")[:, 1:2]
        ident = C("ident")
        ident_r, upper_r, ones_r, block_r = (sb(n, [P], F32R) for n in ("ident_r", "upper_r", "ones_r", "block_r"))
        got_con = Loads(sem("got_con")).start(sp, con[:, :], consts)
        got_vec = Loads(sem("got_vec")).start(sp, vec[:, :], vectors)

        def exp_ln_tables():
            act.run(nc.scalar.preload_act_table_set, "natural_log_exp_and_others")

        exp_ln_tables()
        act.do(nc.scalar.activation, ident_r[:, :], ident, ACT.Copy, after=[got_con])
        act.do(nc.scalar.activation, upper_r[:, :], C("upper"), ACT.Copy)
        act.do(nc.scalar.activation, ones_r[:, :], C("ones"), ACT.Copy, scale=-1.0)
        consts_r = act.do(nc.scalar.activation, block_r[:, :], C("block"), ACT.Copy)
        dve.wait(got_con, got_vec)
        act.wait(got_con, got_vec)
        pe.wait(got_con)
        pool.wait(got_con)

        NW, NRAW = 4, 3
        w_raw = sb("w_raw", [NRAW, HALF])
        w_hi = sb("w_hi", [NW, CH], F32R)
        w_lo = sb("w_lo", [NW, CH], F32R)
        raw_loads = [Loads(sem(f"raw_load{i}")) for i in range(NRAW)]
        raw_free = [[] for _ in range(NRAW)]
        chunks = plan()
        state = dict(split=0, used=0)
        chunk_ready, chunk_free = {}, {}

        parts, at = [], 0
        for n, (_, _, _, nk, c) in enumerate(chunks):
            size = nk * len(c)
            parts += [(n, a, min(size, a + HALF), at) for a in range(0, size, HALF)]
            at += P * size
        raw_got = {}

        def load_part(p):
            if p < len(parts):
                n, a, b, at = parts[p]
                size = chunks[n][3] * len(chunks[n][4])
                src = wstream[at:at + P * size].rearrange("(p n) -> p n", p=P)
                r = p % NRAW
                raw_got[p] = raw_loads[r].start(sp, w_raw[:, r, 0:b - a], src[:, a:b], raw_free[r])

        def bring(most=len(parts)):
            end = min(len(parts), state["split"] + most)
            while state["split"] < end:
                p = state["split"]
                n, a, b, _ = parts[p]
                if n >= NW and n - NW not in chunk_free:
                    return
                state["split"] += 1
                slot, r, free = n % NW, p % NRAW, chunk_free.get(n - NW, [])
                lo_lane = pool if p % 5 == 0 else dve
                hi, lo, raw = w_hi[:, slot, a:b], w_lo[:, slot, a:b], w_raw[:, r, 0:b - a]
                m1 = act.do(nc.scalar.activation, hi, raw, ACT.Copy, after=[raw_got[p], *free])
                m2 = lo_lane.do(lo_lane.engine.tensor_tensor, lo, raw, hi.bitcast(F32), ALU.subtract,
                                after=[m1, *free])
                raw_free[r] = [m1, m2]
                chunk_ready.setdefault(n, []).append([m1, m2])
                load_part(p + NRAW)

        def next_chunk(layer):
            n = state["used"]
            state["used"] += 1
            planned, _, _, nk, c = chunks[n]
            assert planned == layer, (planned, layer)
            hi, lo = (w[:, n % NW, 0:nk * len(c)].rearrange("p (k c) -> p k c", k=nk) for w in (w_hi, w_lo))
            return hi, lo, n

        def need(n, k):
            pe.wait(*chunk_ready[n][k * len(chunks[n][4]) // HALF])

        def chunks_done(ns, mark, most=len(parts)):
            for n in ns:
                chunk_free[n] = [mark]
            bring(most)

        def by_column_tiles(layer, act_hi, act_lo, ready, evacuate, n_tiles, nk=KD, width=P):
            f = 0
            while f < n_tiles:
                hi, lo, n = next_chunk(layer)
                here = len(chunks[n][4]) // width
                for t in range(here):
                    bank, free, readers = linear_banks.take()
                    pe.wait(*free, *ready(0))
                    o = bank[0:width, :]
                    for k in range(nk):
                        pe.wait(*ready(k))
                        need(n, k)
                        ws = slice(t * width, (t + 1) * width)
                        for i, (a, b) in enumerate(((hi, act_hi), (lo, act_hi), (hi, act_lo))):
                            operands = (o, a[:, k, ws], b[:, k, :])
                            step = dict(start=(k == 0 and i == 0), stop=(k == nk - 1 and i == 2))
                            if k == nk - 1 and i == 2:
                                done = pe.do(nc.tensor.matmul, *operands, **step)
                            else:
                                pe.run(nc.tensor.matmul, *operands, **step)
                    readers += evacuate(f, o, done)
                    if t == here - 1:
                        chunks_done([n], done)
                    f += 1
                    yield

        def by_row_tiles(layer, act_hi, act_lo, ready, evacuate, nk, halves=(0, 1), tile_by_tile=False):
            held = {}
            order = [(n, i) for n in halves for i in range(TT)]
            if tile_by_tile:
                order.sort(key=lambda step: step[1])
            for n, i in order:
                if n not in held:
                    held[n] = [next_chunk(layer) for _ in range((nk + 3) // 4)]
                width = len(chunks[held[n][0][2]][4])
                bank, free, readers = linear_banks.take()
                pe.wait(*free)
                o = bank[:, 0:width]
                for k in range(nk):
                    pe.wait(*ready(k))
                    hi, lo, num = held[n][k // 4]
                    need(num, k % 4)
                    for j, (a, b) in enumerate(((act_hi, hi), (act_lo, hi), (act_hi, lo))):
                        operands = (o, a[:, k, P * i:P * (i + 1)], b[:, k % 4, :])
                        step = dict(start=(k == 0 and j == 0), stop=(k == nk - 1 and j == 2))
                        if j == 2 and k == nk - 1:
                            done = pe.do(nc.tensor.matmul, *operands, **step)
                        else:
                            pe.run(nc.tensor.matmul, *operands, **step)
                readers += evacuate(n, i, o, done)
                if i == TT - 1:
                    chunks_done([num for _, _, num in held[n]], done,
                                0 if tile_by_tile and n != halves[-1] else len(parts))
                yield

        def finish(*gens):
            for g in gens:
                for _ in g:
                    pass

        stat = sb("stat", [2, 5, TT])
        junk = sb("junk", [512])
        halves = [slice(0, 512), slice(512, 1024)]
        squares = {}

        def square(which, i, n, src, after):
            m = act.do(nc.scalar.activation, junk[:, :], src, ACT.Square, accum_out=stat[:, which, n, i:i + 1],
                       after=[*after, *squares.get("last", [])])
            squares["last"] = [m]
            squares.setdefault((which, i), []).append(m)
            return m

        def rstd(which, i):
            s0, s1, total, log, out = (stat[:, which, n, i:i + 1] for n in range(5))
            m = dve.do(nc.vector.tensor_tensor, total, s0, s1, ALU.add, after=squares.pop((which, i)))
            m = act.do(nc.scalar.activation, log, total, ACT.Ln, bias=eps_rms, scale=1.0 / D, after=[m])
            return out, act.do(nc.scalar.activation, out, log, ACT.Exp, scale=-0.5, after=[m])

        h_hi = sb("h_hi", [KD, S], F32R)
        h_lo = sb("h_lo", [KD, S], F32R)
        h_ready = [[] for _ in range(KD)]

        def norm_tile(i, x, scaled, gain, h_free, ready=()):
            r, m = rstd(1, i)
            marks = [dve.do(nc.vector.tensor_scalar, scaled[:, halves[0]], x[:, halves[0]], r, None, ALU.mult,
                            after=[m, *ready]),
                     act.do(nc.scalar.activation, scaled[:, halves[1]], x[:, halves[1]], ACT.Copy, scale=r,
                            after=[m, *ready])]

            def turn():
                ts = slice(P * i, P * i + P)
                for k0 in range(0, KD, 4):
                    bank, free, readers = core_banks.take()
                    pe.wait(*free, *marks)
                    for k in range(4):
                        m = pe.do(nc.tensor.transpose, bank[:, P * k:P * (k + 1)],
                                  scaled[:, P * (k0 + k):P * (k0 + k + 1)], ident)
                    for k in range(4):
                        src, g = bank[:, P * k:P * (k + 1)], V(gain, k0 + k)
                        hi_ap, lo_ap = h_hi[:, k0 + k, ts], h_lo[:, k0 + k, ts]
                        hi = act.do(nc.scalar.activation, hi_ap, src, ACT.Copy, scale=g, after=[m, *h_free])
                        new_ready.setdefault(k0 + k, []).append(hi)
                    for k in range(4):
                        src, g = bank[:, P * k:P * (k + 1)], V(gain, k0 + k)
                        hi_ap, lo_ap = h_hi[:, k0 + k, ts], h_lo[:, k0 + k, ts]
                        lo = dve.do(nc.vector.scalar_tensor_tensor, lo_ap, src, g, hi_ap.bitcast(F32), ALU.mult,
                                    ALU.subtract, after=[hi, *h_free])
                        new_ready[k0 + k].append(lo)
                    readers += [hi, lo]

            return turn

        new_ready = {}

        def h_renewed():
            for k in range(KD):
                h_ready[k] = new_ready.pop(k)

        def turn_behind(turns, i, phases):
            if i == TT - 1:
                phases[0]()
                bring(BETWEEN)
                turns.pop(0)()
                phases[1]()()
                h_renewed()
                return
            if turns:
                turns.pop(0)()
            phases[0]()
            turns.append(phases[1]())

        def split(hi_ap, lo_ap, src, after, lo_lane=pool):
            hi = act.do(nc.scalar.activation, hi_ap, src, ACT.Copy, after=after)
            lo = lo_lane.do(lo_lane.engine.tensor_tensor, lo_ap, src, hi_ap.bitcast(F32), ALU.subtract,
                            after=[hi, *after])
            return [hi, lo]

        def last(*lanes):
            return [(l, l.count) for l in (lanes or (pe, act, dve, pool)) if l.count]

        x_rows = T["x"].rearrange("a (i p) d -> (a p) i d", p=P)

        with ExitStack() as scope:
            x0 = sb("x0", [TT, D], ctx=scope)
            loads = [Loads(sem(f"x0_load{i}")) for i in range(TT)]
            got = [loads[i].start(sp, x0[:, i, :], x_rows[:, i, :]) for i in range(TT)]
            for p in range(NRAW):
                load_part(p)
            turns = []
            for i in range(TT):
                for n, half in enumerate(halves):
                    square(1, i, n, x0[:, i, half], [got[i]])
                turn_behind(turns, i, [lambda: None,
                                       lambda: norm_tile(i, x0[:, i, :], x0[:, i, :], "norm_mix_pre", [], [got[i]])])
            bring()
        x0_free = last()

        ready_h = lambda k: h_ready[k]

        mixer = ExitStack()
        nsa_io = ExitStack()
        o_gla = sb("o_gla", [KD, S], ctx=mixer)
        kc_vc = sb("kc_vc", [2, S], ctx=nsa_io)
        nsa_k = sb("nsa_k", [2, S], ctx=nsa_io)
        nsa_v = sb("nsa_v", [TT, 2 * P], ctx=nsa_io)
        nsa_g = sb("nsa_g", [TT, 24], ctx=nsa_io)
        gla = ExitStack()
        rr = sb("rr", [2, S], ctx=gla)
        v_gla = sb("v_gla", [TT, GLA_H * DV], ctx=gla)
        top = (nc.sbuf_usable_end - 16 * 1024) // 32 * 32

        def at_top(name, kb, shape, dt=F32):
            return nc.alloc_sbuf_tensor_at(name, [P] + shape, dt, offset=top + 1024 * kb)

        a_low = at_top("a_low", 0, [S])
        w_alpha = at_top("w_alpha", 2, [GLA_H * DK])
        reset = at_top("reset", 4, [S])
        gs = at_top("gs", 6, [5, S])
        qkd_of = sb("qkd", [2, 3, S], ctx=gla)
        decay_of = sb("decay", [2, NCH], ctx=gla)
        attn = junk
        kd_rows = sb("kd_rows", [TT, P], ctx=gla)
        states = sb("states", [NCH - 1, DV], ctx=gla)

        load_alpha = Loads(sem("load_alpha"))
        got_alpha = load_alpha.start(sp, w_alpha[0:RANK, :], T["gla_w_alpha2"][0], x0_free)
        zero_attn = pool.do(nc.gpsimd.memset, attn[:, :], 0.0, after=x0_free)
        m = pool.do(nc.gpsimd.memset, reset[:, :], 1.0, after=x0_free)
        set_reset = pool.do(nc.gpsimd.memset, reset[:, 0:S:CHUNK], 0.0, after=[m])
        zero_attn_and_reset = [zero_attn, set_reset]

        got = {}

        def evac_ga(f, o, done):
            got["ga"] = act.do(nc.scalar.activation, a_low[0:RANK, :], o, ACT.Copy, after=[done])
            return [got["ga"]]

        for lane in (act, dve, pool):
            lane.wait(*x0_free)
        finish(by_column_tiles("gla a", h_hi, h_lo, ready_h, evac_ga, 1, width=RANK))

        v_marks = []

        def evac_v(n, i, o, done):
            m = act.do(nc.scalar.activation, v_gla[:, i, 512 * n:512 * n + 512], o, ACT.Copy, after=[done])
            v_marks.append(m)
            return [m]

        def gla_v():
            yield from by_row_tiles("gla v", h_hi, h_lo, ready_h, evac_v, KD)

        def chunked(ap):
            return ap.rearrange("p (n c) -> p n c", c=CHUNK)

        free = {"gs": [], ("qkd", 0): [], ("qkd", 1): [], "attn": zero_attn_and_reset, "kd_rows": [],
                ("states", 0): [], ("states", 1): []}

        def gla_gates(h):
            bank, bank_free, readers = core_banks.take()
            m = pe.do(nc.tensor.matmul, bank[:, :], w_alpha[0:RANK, DK * h:DK * (h + 1)], a_low[0:RANK, :],
                                         start=True, stop=True, after=[got_alpha, got["ga"], *bank_free])
            x_, e_, b_ = gs[:, 0, :], gs[:, 1, :], gs[:, 2, :]
            x = dve.do(nc.vector.tensor_scalar, x_, bank[:, :], V("gla_b_alpha", h), None, ALU.add,
                       after=[m, *free["gs"]])
            readers.append(x)
            m = dve.do(nc.vector.scalar_tensor_tensor, e_, x_, -1.0, x_, ALU.mult, ALU.min, after=[x])
            m = act.do(nc.scalar.activation, e_, e_, ACT.Exp, after=[m])
            m = act.do(nc.scalar.activation, e_, e_, ACT.Ln, bias=1.0, after=[m])
            yield
            m = dve.do(nc.vector.scalar_tensor_tensor, x_, x_, 0.0, e_, ALU.min, ALU.subtract, after=[m])
            b = dve.do(nc.vector.tensor_tensor_scan, b_, reset[:, :], x_, 0.0, ALU.mult, ALU.add,
                       after=[m, set_reset])
            b_last = chunked(b_)[:, :, CHUNK - 1:CHUNK]
            m = dve.do(nc.vector.tensor_tensor, chunked(e_), b_last.broadcast_to([P, NCH, CHUNK]), chunked(b_),
                                                 ALU.subtract, after=[b])
            yield
            act.do(nc.scalar.activation, gs[:, 3, :], b_, ACT.Exp, scale=1 / TAU, after=[b])
            act.do(nc.scalar.activation, gs[:, 4, :], b_, ACT.Exp, scale=-1 / TAU)
            act.do(nc.scalar.activation, decay_of[:, h % 2, :], b_last.squeeze(), ACT.Exp, scale=1 / TAU,
                   after=free["states", h % 2])
            gates_ready[h] = act.do(nc.scalar.activation, e_, e_, ACT.Exp, scale=1 / TAU, after=[m])

        qk_marks, gates_ready, o_gla_ready = {}, {}, {}

        def gla_front(h):
            yield from gla_gates(h)
            qkd = qkd_of[:, h % 2, :, :]
            yield

            def evac(f, o, done):
                if f == 0:
                    m = dve.do(nc.vector.scalar_tensor_tensor, qkd[:, 0, :], o, DK ** -0.5, gs[:, 3, :],
                               ALU.mult, ALU.mult, after=[done, gates_ready[h], *free["qkd", h % 2]])
                    qk_marks[h] = [m]
                    return [m]
                m1 = dve.do(nc.vector.tensor_tensor, qkd[:, 1, :], o, gs[:, 4, :], ALU.mult, after=[done])
                m2 = dve.do(nc.vector.tensor_tensor, qkd[:, 2, :], o, gs[:, 1, :], ALU.mult)
                qk_marks[h] += [m1, m2]
                free["gs"] = [m2]
                return [m1, m2]

            yield from by_column_tiles(f"gla qk {h}", h_hi, h_lo, ready_h, evac, 2)

        def gla_head(h):
            qkd, decay, qk = qkd_of[:, h % 2, :, :], decay_of[:, h % 2, :], qk_marks[h]
            o_sq = qkd[:, 1:3, :]
            o_rs = qkd[:, 0, :]
            bank, bank_free, readers = core_banks.take()
            pe.wait(*bank_free, *qk)
            for p in range(TT):
                m = pe.do(nc.tensor.matmul, bank[:, P * p:P * p + P], qkd[:, 1, P * p:P * p + P],
                                                  qkd[:, 0, P * p:P * p + P], start=True, stop=True)
            mask = C("gla_mask").bitcast(U32).unsqueeze(1).broadcast_to([P, TT, P])
            attn_ready = dve.do(nc.vector.copy_predicated, attn[:, :].rearrange("p (a c) -> p a c", c=P), mask,
                                bank[:, :].rearrange("p (a c) -> p a c", c=P), after=[m, *free["attn"]])
            readers.append(attn_ready)
            yield
            bank, bank_free, readers = core_banks.take()
            pe.wait(*bank_free)
            for p in range(TT):
                m = pe.do(nc.tensor.transpose, bank[:, P * p:P * p + P], qkd[:, 2, P * p:P * p + P], ident)
            kd_ready = act.do(nc.scalar.activation, kd_rows[:, :, :].rearrange("p a c -> p (a c)"), bank[:, :],
                              ACT.Copy, after=[m, *free["kd_rows"]])
            readers.append(kd_ready)
            yield
            step = None
            state_marks = {}
            states_free = free["states", (h + 1) % 2]
            for n0 in range(0, NCH - 1, 4):
                some = range(n0, min(n0 + 4, NCH - 1))
                pair = [core_banks.take() for _ in range(2)]
                pe.wait(*pair[0][1], *pair[1][1], kd_ready, *v_marks)
                update = {}
                for n in some:
                    p, r = n // 2, CHUNK * (n % 2)
                    update[n] = pair[n % 2][0][:, DV * (p % 2):DV * (p % 2) + DV]
                    m = pe.do(nc.tensor.matmul, update[n], kd_rows[r:r + CHUNK, p, :],
                                                 v_gla[r:r + CHUNK, p, DV * h:DV * (h + 1)], start=True, stop=True)
                yield
                for n in some:
                    new = states[:, n, :]
                    if n == 0:
                        step = dve.do(nc.vector.tensor_copy, new, update[n], after=[m, *states_free])
                    else:
                        step = dve.do(nc.vector.scalar_tensor_tensor, new, states[:, n - 1, :],
                                      decay[:, n:n + 1], update[n], ALU.mult, ALU.add, after=[m, step])
                    pair[n % 2][2].append(step)
                    state_marks[n + 1] = step
                yield
            free["kd_rows"] = [m]
            outs = []
            for j in range(2):
                bank, bank_free, readers = core_banks.take()
                pe.wait(*bank_free, attn_ready)
                e0 = DV * h + P * j
                for p in range(TT):
                    pe.run(nc.tensor.matmul, bank[:, P * p:P * p + P], v_gla[:, p, e0:e0 + P],
                           attn[:, P * p:P * p + P], start=(p == 0), stop=False, skip_group_check=True)
                for n in range(1, NCH):
                    pe.wait(state_marks[n])
                    m = pe.do(nc.tensor.matmul, bank[:, CHUNK * n:CHUNK * (n + 1)], states[:, n - 1, P * j:P * j + P],
                        qkd[:, 0, CHUNK * n:CHUNK * (n + 1)], start=False, stop=(n == NCH - 1), skip_group_check=True)
                sq = act.do(nc.scalar.activation, o_sq[:, j, :], bank[:, :], ACT.Square, after=[m])
                outs.append((bank, readers, sq, m))
                yield
            free["attn"] = free["states", h % 2] = [m]
            bank, bank_free, readers = core_banks.take()
            pe.wait(*bank_free, outs[0][2], outs[1][2])
            for j in range(2):
                m = pe.do(nc.tensor.matmul, bank[:, :], C("ones"), o_sq[:, j, :], start=(j == 0), stop=(j == 1))
            m = act.do(nc.scalar.activation, o_rs, bank[:, :], ACT.Ln, bias=eps_rms, scale=1.0 / DV, after=[m])
            readers.append(m)
            m = act.do(nc.scalar.activation, o_rs, o_rs, ACT.Exp, scale=-0.5, after=[m])
            for j in range(2):
                bank, readers, sq, om = outs[j]
                k = dve.do(nc.vector.scalar_tensor_tensor, o_gla[:, 2 * h + j, :], bank[:, :],
                           V("gla_norm_g", j), o_rs, ALU.mult, ALU.mult, after=[m, om])
                readers += [sq, k]
            free["qkd", h % 2] = [k]
            o_gla_ready[h] = k
            yield

        def evac_nsa_rows(n, i, o, done):
            m2 = act.do(nc.scalar.activation, nsa_g[:, i, :], o[:, 2 * P:2 * P + 24], ACT.Exp, scale=-1.0,
                        after=[done])
            got["nv", i] = act.do(nc.scalar.activation, nsa_v[:, i, :], o[:, 0:2 * P], ACT.Copy, after=[done])
            m = dve.do(nc.vector.tensor_scalar, nsa_g[:, i, :], nsa_g[:, i, :], 1.0, None, ALU.add, after=[m2])
            got["gate", i] = dve.do(nc.vector.reciprocal, nsa_g[:, i, :], nsa_g[:, i, :], after=[m])
            return [got["nv", i], m2]

        def sigmoid(t, o, after):
            m1 = act.do(nc.scalar.activation, t, o, ACT.Exp, scale=-1.0, after=after)
            m = act.do(nc.scalar.activation, t, t, ACT.Ln, bias=1.0, after=[m1])
            return m1, act.do(nc.scalar.activation, t, t, ACT.Exp, scale=-1.0, after=[m])

        def evac_r(f0, rot_rr):
            def evac(f, o, done):
                f += f0
                t, t_free, t_readers = rot_rr.take()
                m1, m = sigmoid(t, o, [done, *t_free])
                m = dve.do(nc.vector.tensor_tensor, t, t, o, ALU.mult, after=[m])
                got["og", f] = pool.do(nc.gpsimd.tensor_tensor, o_gla[:, f, :], o_gla[:, f, :], t, ALU.mult,
                                       after=[m, o_gla_ready[f // 2]])
                t_readers.append(got["og", f])
                return [m1, m]
            return evac

        def evac_kc_vc(f, o, done):
            got["kc_vc", f] = act.do(nc.scalar.activation, kc_vc[:, f, :], o, ACT.Copy, after=[done])
            return [got["kc_vc", f]]

        def evac_k(f, o, done):
            got["nk", f] = act.do(nc.scalar.activation, nsa_k[:, f, :], o, ACT.Copy, after=[done])
            return [got["nk", f]]

        def fills():
            yield from by_row_tiles("nsa v gate", h_hi, h_lo, ready_h, evac_nsa_rows, KD, halves=(0,))
            yield from by_column_tiles("nsa kc vc", h_hi, h_lo, ready_h, evac_kc_vc, 2)
            rot = Rotating([rr[:, i, :] for i in range(2)])
            yield from by_column_tiles("gla r", h_hi, h_lo, ready_h, evac_r(0, rot), KD - 2)
            yield from by_column_tiles("nsa ks kw", h_hi, h_lo, ready_h, evac_k, 2)

        rest = fills()
        front = gla_front(0)
        for n, _ in enumerate(gla_v()):
            if n % 2 == 0 and n < 6:
                next(front)
        finish(front)
        for h in range(GLA_H):
            front = gla_front(h + 1) if h + 1 < GLA_H else iter(())
            if h == GLA_H - 1:
                w1_k = at_top("w1_k", 0, [CL, P])
                got_w1_k = Loads(sem("load_w1_k")).start(sp, w1_k[:, :, :].rearrange("p l o -> p (l o)"), T["w1_k"],
                                                         last())
            for n, _ in enumerate(gla_head(h)):
                next(rest if n in FILLS[h] else front, None)
            finish(front)
        finish(rest)
        assert nc.sbuf_base <= top
        gla_free = last()
        gla.close()

        nsa = ExitStack()
        mix_gates = at_top("mix_gates", -16, [KD, S])
        nsa_q = at_top("nsa_q", 0, [4, S])
        on_hi, on_lo = at_top("on_hi", 0, [4, S], F32R), at_top("on_lo", 8, [4, S], F32R)
        for lane in (act, dve, pool, pe, sp):
            lane.wait(*gla_free)
        kc_t = sb("kc_t", [32], ctx=nsa)
        v4 = sb("v4", [NG, REP * DH], ctx=nsa)

        def evac_q(f, o, done):
            got["nq", f] = act.do(nc.scalar.activation, nsa_q[:, f, :], o, ACT.Copy, scale=C("q_scale")[:, f:f + 1],
                                  after=[done, *w1_k_free])
            return [got["nq", f]]

        def late_fills():
            rot = Rotating([rr_late[:, i, :] for i in range(2)])
            yield from by_column_tiles("gla r", h_hi, h_lo, ready_h, evac_r(KD - 2, rot), 2)
            yield from by_column_tiles("nsa q", h_hi, h_lo, ready_h, evac_q, REP)

        cmp_scope = ExitStack()
        rr_late = sb("rr_late", [2, S], ctx=cmp_scope)
        w1 = sb("w1", [CL, P], ctx=cmp_scope)
        pe_t = sb("pe_t", [2, CL], ctx=cmp_scope)
        w2 = sb("w2", [2, P], ctx=cmp_scope)
        windows = sb("windows", [CL, NCMP], ctx=cmp_scope)
        hid = sb("hid", [3, 32], ctx=cmp_scope)
        zero_v4 = pool.do(nc.gpsimd.memset, v4[:, :, :], 0.0)

        def load(name, to):
            return Loads(sem(f"load_{name}")).start(sp, to, T[name])

        got_pe = [load(f"pe_{n}", pe_t[:, x, :]) for x, n in enumerate("kv")]
        got_w2 = [load(f"w2_{n}", w2[:, x, :]) for x, n in enumerate("kv")]
        w1_of = [w1_k, w1]
        got_w1 = [got_w1_k, load("w1_v", w1[:, :, :].rearrange("p l o -> p (l o)"))]
        kc_ready, v4_marks, w1_k_free = [], [], []

        def compression():
            win_free = []
            for x in range(2):
                src = kc_vc[:, x, :]
                for half in range(2):
                    blk = src.rearrange("p (n l) -> p l n", l=CS)[:, :, half:half + NCMP]
                    pe_b = pe_t[:, x, CS * half:CS * half + CS].unsqueeze(2).broadcast_to([P, CS, NCMP])
                    win_ready = dve.do(nc.vector.tensor_tensor, windows[:, CS * half:CS * half + CS, :], blk,
                                       pe_b, ALU.add, after=[got_pe[x], got["kc_vc", x], *win_free])
                bank, bank_free, readers = core_banks.take()
                pe.wait(*bank_free, got_w1[x], win_ready)
                for l in range(CL):
                    m = pe.do(nc.tensor.matmul, bank[:, 0:NCMP], w1_of[x][:, l, :], windows[:, l, :], start=(l == 0),
                              stop=(l == CL - 1))
                    if l % 4 == 3:
                        yield
                win_free = [m]
                if x == 0:
                    w1_k_free.append(m)
                yield
                m = act.do(nc.scalar.activation, hid[:, 0, 0:NCMP], bank[:, 0:NCMP], ACT.Exp, scale=-1.0, after=[m])
                m2 = dve.do(nc.vector.tensor_scalar, hid[:, 1, 0:NCMP], hid[:, 0, 0:NCMP], 1.0, None, ALU.add,
                            after=[m])
                m2 = dve.do(nc.vector.reciprocal, hid[:, 1, 0:NCMP], hid[:, 1, 0:NCMP], after=[m2])
                m2 = dve.do(nc.vector.tensor_tensor, hid[:, 2, 0:NCMP], bank[:, 0:NCMP], hid[:, 1, 0:NCMP],
                            ALU.mult, after=[m2])
                readers += [m, m2]
                yield
                bank, bank_free, readers = core_banks.take()
                pe.wait(*bank_free, m2, got_w2[x])
                if x == 0:
                    m = pe.do(nc.tensor.matmul, bank[:, 0:NCMP], w2[:, 0, :], hid[:, 2, 0:NCMP], start=True,
                              stop=True)
                    kc_ready.append(dve.do(nc.vector.tensor_copy, kc_t[:, 0:NCMP], bank[:, 0:NCMP], after=[m]))
                    readers += kc_ready
                else:
                    for r in range(REP):
                        m = pe.do(nc.tensor.matmul, bank[32 * r:32 * r + NCMP, 0:P], hid[:, 2, 0:NCMP],
                                  w2[:, 1, :], start=True, stop=True)
                    for r in range(REP):
                        v4_marks[:] = [dve.do(nc.vector.tensor_copy, v4[32 * r:32 * r + NCMP, :, DH * r:DH * r + DH],
                            bank[32 * r:32 * r + NCMP, 0:P].rearrange("p (g d) -> p g d", g=NG), after=[m, zero_v4])]
                    readers += v4_marks
                yield

        late = late_fills()
        for n, _ in enumerate(compression()):
            if n % FILL_EVERY == 0 or n > 20:
                next(late, None)
        finish(late)
        assert nc.sbuf_base <= top - 16 * 1024
        cmp_free = last()
        cmp_scope.close()

        for lane in (act, dve, pool, pe):
            lane.wait(*cmp_free)
        probs = sb("probs", [2, REP, S], ctx=nsa)
        probs_t = sb("probs_t", [3, S], ctx=nsa)
        sc = sb("nsa_stats", [3, 40], ctx=nsa)
        pc = kc_vc[:, 0, 0:NH * 32].rearrange("p (h n) -> p h n", n=32)
        pc_t = kc_vc[:, 0, NH * 32:NH * 32 + NG * P].rearrange("p (g q) -> p g q", q=P)
        o_rows = kc_vc[:, 1, :]
        zero_pc = pool.do(nc.gpsimd.memset, pc[:, :, :], 0.0)
        rot_probs = Rotating([probs[:, i, :, :] for i in range(2)])
        rot_pt = Rotating([probs_t[:, i, :] for i in range(3)])
        fr = {"pc": [zero_pc], "pc_t": [], "o_rows": []}
        o_banks = Rotating(banks[6:8])
        score_banks = Rotating(banks[2:4])
        turn_banks = Rotating(banks[4:6])
        score_banks.readers, turn_banks.readers = core_banks.readers[0:2], core_banks.readers[2:4]
        o_banks.readers = core_banks.readers[4:6]
        cmp_seen = C("cmp_mask").rearrange("p (i n) -> p i n", n=32)
        cmp_dist = C("cmp_dist").rearrange("p (i n) -> p i n", n=NCMP)
        gates = nsa_g[:, :, :].rearrange("p i (h b) -> p i h b", b=3)
        held = {}

        def over_keys(ap, n=NH):
            return ap.unsqueeze(2).broadcast_to([P, n, NCMP])

        def cmp_scores(i):
            p = pc[:, :, 0:NCMP]
            mx, sm, wt = sc[:, 0, 32:40], sc[:, 1, 32:40], sc[:, 2, 32:40]
            for g in range(NG):
                bank, bank_free, readers = score_banks.take()
                pe.wait(*bank_free, *kc_ready, *[got["nq", j] for j in range(REP)])
                rows = slice(DH * g, DH * g + DH)
                for j in range(REP):
                    m = pe.do(nc.tensor.matmul, bank[:, NCMP * j:NCMP * (j + 1)], nsa_q[rows, j, P * i:P * i + P],
                              kc_t[rows, 0:NCMP], start=True, stop=True)
                scores = bank[:, 0:REP * NCMP].rearrange("p (h n) -> p h n", n=NCMP)
                m = dve.do(nc.vector.tensor_tensor, pc[:, REP * g:REP * (g + 1), 0:NCMP], scores,
                           cmp_dist[:, i, :].unsqueeze(1).broadcast_to([P, REP, NCMP]), ALU.add, after=[m, *fr["pc"]])
                readers.append(m)
            yield
            m = dve.do(nc.vector.tensor_reduce, mx, p, AXX, ALU.max, after=[m])
            m = dve.do(nc.vector.tensor_tensor, p, p, over_keys(mx), ALU.subtract, after=[m])
            m = dve.do(nc.vector.tensor_tensor, p, p, over_keys(C("slopes")), ALU.mult, after=[m])
            m = act.do(nc.scalar.activation, p, p, ACT.Exp, after=[m])
            m = dve.do(nc.vector.tensor_reduce, sm, p, AXX, ALU.add, after=[m])
            m = dve.do(nc.vector.reciprocal, wt, sm, after=[m])
            m = dve.do(nc.vector.tensor_tensor, wt, wt, gates[:, i, :, 0], ALU.mult, after=[m, got["gate", i]])
            m = dve.do(nc.vector.tensor_tensor, p, p, over_keys(wt), ALU.mult, after=[m])
            held["pc", i] = dve.do(nc.vector.tensor_tensor, p, p,
                                   cmp_seen[:, i, 0:NCMP].unsqueeze(1).broadcast_to([P, NH, NCMP]), ALU.mult,
                                   after=[m])
            yield

        def cmp_values(i):
            held["o", i] = [o_banks.take() for _ in range(NG)]
            o_free = held["o", i][0][1] + held["o", i][1][1]
            bank, bank_free, readers = turn_banks.take()
            pe.wait(*bank_free, held["pc", i])
            for g in range(NG):
                m = pe.do(nc.tensor.transpose, bank[:, P * g:P * g + P],
                          pc[:, REP * g:REP * (g + 1), :].rearrange("p h n -> p (h n)"), ident)
            fr["pc"] = [m]
            t = dve.do(nc.vector.tensor_copy, pc_t[:, :, :].rearrange("p g q -> p (g q)"), bank[:, 0:2 * P],
                       after=[m, *fr["pc_t"]])
            readers.append(t)
            yield
            pe.wait(*o_free, *v4_marks, t, *[got["nv", n] for n in range(TT)])
            for g in range(NG):
                for j in range(REP):
                    m = pe.do(nc.tensor.matmul, held["o", i][g][0][0:DH, P * j:P * j + P],
                              v4[:, g, DH * j:DH * j + DH], pc_t[:, g, :], start=(j == 0), stop=False,
                              skip_group_check=True)
            fr["pc_t"] = [m]

        def key_scores(i, br, g):
            width = P * (i + 1)
            rows, qs = slice(DH * g, DH * g + DH), slice(P * i, P * i + P)
            pr, pr_free, pr_readers = rot_probs.take()
            c0 = 8 * rot_probs.at
            mx, mb, sm = sc[:, 0, c0:c0 + REP], sc[:, 0, c0 + REP:c0 + 2 * REP], sc[:, 1, c0:c0 + REP]
            wt = sc[:, 2, c0:c0 + REP]
            for j in range(REP):
                bank, bank_free, readers = score_banks.take()
                m = pe.do(nc.tensor.matmul, bank[:, 0:width], nsa_q[rows, j, qs], nsa_k[rows, br, 0:width],
                          start=True, stop=True, after=[*bank_free, got["nq", j], got["nk", br]])
                m = dve.do(nc.vector.tensor_tensor_reduce, pr[:, j, 0:width], bank[:, 0:width],
                           C("dist")[:, S - width:S], 1.0, -3e38, ALU.add, ALU.max, mx[:, j:j + 1],
                           after=[m, *pr_free])
                readers.append(m)
                m = dve.do(nc.vector.tensor_tensor, mb[:, j:j + 1], mx[:, j:j + 1],
                           C("minus_slopes")[:, REP * g + j:REP * g + j + 1], ALU.mult, after=[m])
                yield
                m = act.do(nc.scalar.activation, pr[:, j, 0:width], pr[:, j, 0:width], ACT.Exp,
                           scale=float(SLOPES[REP * g + j]), bias=mb[:, j:j + 1], accum_out=sm[:, j:j + 1], after=[m])
            yield
            m = dve.do(nc.vector.reciprocal, wt, sm, after=[m])
            m = dve.do(nc.vector.tensor_tensor, wt, wt, gates[:, i, REP * g:REP * (g + 1), 1 + br], ALU.mult,
                       after=[m])
            ready = []
            for j in range(REP):
                p = pr[:, j, 0:width]
                if j in SCALED_BY_ACT:
                    ready.append(act.do(nc.scalar.activation, p, p, ACT.Copy, scale=wt[:, j:j + 1], after=[m]))
                else:
                    ready.append(dve.do(nc.vector.tensor_scalar, p, p, wt[:, j:j + 1], None, ALU.mult, after=[m]))
            held[i, br, g] = pr, pr_readers, ready

        def key_values(i, br, g):
            o_bank = held["o", i][g][0]
            pr, pr_readers, ready = held[i, br, g]
            turned = {}

            def turn(kb):
                bank, bank_free, readers = turn_banks.take()
                pe.wait(*bank_free, *ready)
                for j in range(REP):
                    m = pe.do(nc.tensor.transpose, bank[:, P * j:P * j + P], pr[:, j, P * kb:P * kb + P], ident)
                pt, pt_free, pt_readers = rot_pt.take()
                t = act.do(nc.scalar.activation, pt, bank[:, :], ACT.Copy, after=[m, *pt_free])
                readers.append(t)
                turned[kb] = pt, pt_readers, t
                return m

            m = turn(0)
            for kb in range(i + 1):
                if kb < i:
                    m = turn(kb + 1)
                yield
                pt, pt_readers, t = turned[kb]
                vs = slice(P * br + DH * g, P * br + DH * g + DH)
                held["pv", i] = pe.do(nc.tensor.matmul, o_bank[0:DH, :], nsa_v[:, kb, vs], pt, start=False,
                                      stop=(br == 1 and kb == i), skip_group_check=True, after=[t])
                pt_readers.append(held["pv", i])
            pr_readers.append(m)

        def tile_out(i):
            qs = slice(P * i, P * i + P)
            got["on", i] = []
            for g, (o_bank, _, o_readers) in enumerate(held["o", i]):
                rows = slice(DH * g, DH * g + DH)
                src = o_bank[0:DH, :].rearrange("p (f q) -> p f q", f=REP)
                marks = split(on_hi[rows, :, qs], on_lo[rows, :, qs], src, [held["pv", i]], dve)
                o_readers += marks
                got["on", i] += marks
            yield

        def nsa_core():
            order = [(i, b, g) for i in range(TT) for b, g in ((None, 0), (0, 0), (0, 1), (1, 0), (1, 1))]

            def back(i, b, g):
                if b is None:
                    yield from cmp_values(i)
                else:
                    yield from key_values(i, b, g)
                    if (b, g) == (1, 1):
                        yield from tile_out(i)

            behind = iter(())
            for i, b, g in order:
                front = cmp_scores(i) if b is None else key_scores(i, b, g)
                for n, _ in enumerate(front):
                    if n >= LEAD:
                        next(behind, None)
                    yield
                yield from behind
                behind = back(i, b, g)
            yield from behind

        def evac_mix_gate(f, o, done):
            m, got["mix", 0, f] = sigmoid(mix_gates[:, f, :], o, [done])
            return [m]

        gate_tiles = by_column_tiles("merge gates", h_hi, h_lo, ready_h, evac_mix_gate, KD)
        for n, _ in enumerate(nsa_core()):
            if n in GATE_STEPS:
                next(gate_tiles, None)
        finish(gate_tiles)
        core_banks.readers[:] = score_banks.readers + turn_banks.readers + o_banks.readers
        nsa_free = last()
        assert nc.sbuf_base <= top - 16 * 1024
        nsa.close()
        nsa_io.close()

        merge = ExitStack()
        og_hi = sb("og_hi", [KD, S], F32R, ctx=merge)
        og_lo = sb("og_lo", [KD, S], F32R, ctx=merge)
        for lane in (act, dve, pool, pe):
            lane.wait(*nsa_free)
        og_ready = [split(og_hi[:, f, :], og_lo[:, f, :], o_gla[:, f, :], [got["og", f]], dve if f % 2 else pool)
                    for f in range(KD)]
        on_ready = sum((got["on", i] for i in range(TT)), [])
        mixed_marks = []
        nsa_gates = sb("nsa_gates", [2, S], ctx=merge)
        late_free = [[], []]

        def merge_all():
            gla_part = {}

            def evac_gla(j):
                def evac(f, o, done):
                    m = dve.do(nc.vector.tensor_tensor, o_gla[:, j + f, :], o, mix_gates[:, j + f, :], ALU.mult,
                               after=[done, got["mix", 0, j + f], *og_ready[j + f]])
                    gla_part[j + f] = m
                    return [m]
                return evac

            def evac_gate(f, o, done):
                m, nsa_gate[f] = sigmoid(nsa_gates[:, f, :], o, [done, *late_free[f]])
                return [m]

            nsa_gate = {}

            def evac_nsa(j):
                def evac(f, o, done):
                    t = nsa_gates[:, f, :]
                    m = dve.do(nc.vector.tensor_tensor, t, o, t, ALU.mult, after=[done, nsa_gate[f]])
                    s = dve.do(nc.vector.tensor_tensor, o_gla[:, j + f, :], o_gla[:, j + f, :], t, ALU.add,
                               after=[m, gla_part[j + f]])
                    mixed_marks.append(s)
                    late_free[f] = [s]
                    return [m]
                return evac

            for j in range(0, KD, 2):
                yield from by_column_tiles("merge gates", h_hi, h_lo, ready_h, evac_gate, 2)
                yield from by_column_tiles("proj gla", og_hi, og_lo, lambda k: og_ready[k], evac_gla(j), 2)
                yield from by_column_tiles("proj nsa", on_hi, on_lo, lambda k: on_ready, evac_nsa(j), 2, nk=4)

        finish(merge_all())
        h_free = [(pe, pe.count)]
        for f in range(KD):
            h_ready[f] = split(h_hi[:, f, :], h_lo[:, f, :], o_gla[:, f, :], [mixed_marks[f], *h_free],
                               dve if f % 2 else pool)
        merge_free = last()
        assert nc.sbuf_base <= top - 16 * 1024
        merge.close()
        mixer.close()

        x1 = sb("x1", [TT, D])
        gain_row = sb("gain_row", [D])
        load_gain = Loads(sem("load_gain"))
        for lane in (act, dve, pool, sp):
            lane.wait(*merge_free)
        load_x1 = Loads(sem("load_x1"))
        got_x1 = load_x1.start(sp, x1[:, :, :], x_rows)

        def load_gain_row(src, after):
            return load_gain.start(sp, gain_row[:, :], src.partition_broadcast(P), after)

        def add_to_x1(i, acc, ready, got_gain, x_ready):
            r, m = rstd(0, i)
            for n, half in enumerate(halves):
                a, x = acc[:, i, half], x1[:, i, half]
                p = dve.do(nc.vector.scalar_tensor_tensor, a, a, r, gain_row[:, half], ALU.mult, ALU.mult,
                           after=[m, got_gain, *ready])
                p = dve.do(nc.vector.tensor_tensor, x, x, a, ALU.add, after=[p, *x_ready])
                square(1, i, n, x, [p])

        with ExitStack() as scope:
            acc = sb("acc_mix", [TT, D], ctx=scope)
            acc_marks = {}
            turns = []
            got_gain = load_gain_row(T["norm_mix_post"][0], [])

            def evac_out(n, i, o, done):
                m = act.do(nc.scalar.activation, acc[:, i, halves[n]], o, ACT.Copy, after=[done])
                acc_marks[n, i] = m
                s = square(0, i, n, o, [done])
                if n == 1:
                    turn_behind(turns, i, [lambda: add_to_x1(i, acc, [acc_marks[0, i], m], got_gain, [got_x1]),
                                           lambda: norm_tile(i, x1[:, i, :], acc[:, i, :], "norm_ffn_pre", [done])])
                return [m, s]

            finish(by_row_tiles("out", h_hi, h_lo, ready_h, evac_out, KD, tile_by_tile=True))
        acc_free = last()

        h_last = []

        def ffn(tag, groups, evac_pair, n_up, free, into, then):
            scope = ExitStack()
            acc = sb(f"acc{tag}", [TT, D], ctx=scope)
            total = acc if into is None else into
            most = max(n for _, n in groups)
            f_hi = sb(f"f_hi{tag}", [2, most, S], F32R, ctx=scope)
            f_lo = sb(f"f_lo{tag}", [2, most, S], F32R, ctx=scope)
            ft = sb(f"ft{tag}", [2, S], ctx=scope)
            rot = Rotating([ft[:, i, :] for i in range(2)])
            for lane in (act, dve, pool, sp):
                lane.wait(*free)
            f_free, f_ready, acc_ready = [[], []], {}, {}

            def up(g):
                t0, nt = groups[g]
                b = g % 2
                state_ = {}

                def evac(f, o, done):
                    t = f // n_up
                    if f % n_up == 0:
                        state_["s"] = rot.take()
                    s, s_free, s_readers = state_["s"]
                    marks, r = evac_pair(f % n_up, s, s_free, o, done, f_hi[:, b, t, :], f_lo[:, b, t, :], f_free[b],
                                         s_readers)
                    if marks:
                        f_ready[g, t] = marks
                    return r

                yield from by_column_tiles(f"up {tag}", h_hi, h_lo, ready_h, evac, nt * n_up)

            def down(g):
                t0, nt = groups[g]
                b = g % 2

                def evac(n, i, o, done):
                    a = total[:, i, halves[n]]
                    if g == 0 and into is None:
                        m = dve.do(nc.vector.tensor_copy, a, o, after=[done])
                    else:
                        m = dve.do(nc.vector.tensor_tensor, a, a, o, ALU.add,
                                   after=[done, *acc_ready.get((n, i), [])])
                    acc_ready[n, i] = [m]
                    if g == len(groups) - 1:
                        then(acc, n, i, m)
                    return [m]

                yield from by_row_tiles(f"down {tag}", f_hi[:, b, :, :], f_lo[:, b, :, :],
                                        lambda k: f_ready[g, k], evac, nt,
                                        tile_by_tile=(g == len(groups) - 1))
                f_free[b] = [(pe, pe.count)]

            for g in range(len(groups) + 1):
                if g < len(groups):
                    finish(up(g))
                if g == len(groups):
                    h_last[:] = [(pe, pe.count)]
                    exp_ln_tables()
                if g:
                    finish(down(g - 1))
            return scope

        def swiglu(which, s, s_free, o, done, hi, lo, free, s_readers):
            if which == 0:
                m = act.do(nc.scalar.activation, s, o, ACT.Silu, after=[done, *s_free])
                s_readers.append(m)
                return None, [m]
            m = dve.do(nc.vector.tensor_tensor, s, s, o, ALU.mult, after=[done, *s_readers, *s_free])
            a = act.do(nc.scalar.activation, hi, s, ACT.Copy, after=[m, *free])
            b = dve.do(nc.vector.tensor_tensor, lo, s, hi.bitcast(F32), ALU.subtract, after=[a, *free])
            s_readers[:] = [m, a, b]
            return [a, b], [m]

        def relu2(which, s, s_free, o, done, hi, lo, free, s_readers):
            r = act.do(nc.scalar.activation, s, o, ACT.Relu, after=[done, *s_free])
            m = dve.do(nc.vector.tensor_tensor, s, s, s, ALU.mult, after=[r, *s_free])
            a = act.do(nc.scalar.activation, hi, s, ACT.Copy, after=[m, *free])
            b = dve.do(nc.vector.tensor_tensor, lo, s, hi.bitcast(F32), ALU.subtract, after=[a, *free])
            s_readers[:] = [m, a, b]
            return [a, b], [r]

        got_gain = load_gain_row(T["norm_ffn_post"][0], last(dve))

        def then_1(acc, n, i, m):
            square(0, i, n, acc[:, i, halves[n]], [m])
            if n == 1:
                turn_behind(turns, i, [lambda: add_to_x1(i, acc, [m], got_gain, []),
                                       lambda: norm_tile(i, x1[:, i, :], acc[:, i, :], "g_attn_2", h_last)])

        scope = ffn("1", FFN1_GROUPS, swiglu, 2, acc_free, None, then_1)
        b2_free = last()
        scope.close()

        scope = ExitStack()
        cat = sb("cat", [KD, S], ctx=scope)
        q2 = sb("q2", [3, S], ctx=scope)
        k2 = sb("k2", [3, S], ctx=scope)
        qk2_free = {f: [] for f in range(4)}
        v2 = sb("v2", [TT, 512], ctx=scope)
        ua = sb("ua", [2, KA - 1 + S], ctx=scope)
        gb = sb("gb", [2, KB - 1 + S], ctx=scope)
        wa = C("cmp_dist")[:, 0:2 * KA].rearrange("p (f k) -> p f k", k=KA)
        wb = C("cmp_mask")[:, 0:2 * KB].rearrange("p (f k) -> p f k", k=KB)
        for lane in (act, dve, pool, sp):
            lane.wait(*b2_free)
        load_wa, load_wb = Loads(sem("load_wa")), Loads(sem("load_wb"))
        got_wa = load_wa.start(sp, C("cmp_dist")[:, 0:2 * KA], T["taps_a"])
        got_wb = load_wb.start(sp, C("cmp_mask")[:, 0:2 * KB], T["taps_b"])
        zero_ua = pool.do(nc.gpsimd.memset, ua[:, :, 0:KA - 1], 0.0)
        zero_gb = pool.do(nc.gpsimd.memset, gb[:, :, 0:KB - 1], 0.0)

        def evac_v2(n, i, o, done):
            got["v2", i] = act.do(nc.scalar.activation, v2[:, i, :], o, ACT.Copy, after=[done])
            return [got["v2", i]]

        def evac_qk2(f, o, done):
            slot, after = f // 2 % 3, [done, *(qk2_free[f // 2 - 3] if f >= 6 else [])]
            if f % 2 == 0:
                m = act.do(nc.scalar.activation, q2[:, slot, :], o, ACT.Copy, scale=DH ** -0.5, after=after)
            else:
                m = act.do(nc.scalar.activation, k2[:, slot, :], o, ACT.Copy, after=after)
            got["qk2", f] = m
            return [m]

        def evac_glu(f, o, done):
            g = gb[:, f % 2, KB - 1:KB - 1 + S]
            if f < 2:
                got["glu", f] = act.do(nc.scalar.activation, g, o, ACT.Copy, after=[done])
                return [got["glu", f]]
            t, t_free, t_readers = rot_ct.take()
            m1, m = sigmoid(t, o, [done, *t_free])
            m = dve.do(nc.vector.tensor_tensor, g, g, t, ALU.mult, after=[m, got["glu", f - 2]])
            t_readers.append(m)
            got["gb", f - 2] = m
            return [m1]

        def evac_acah(f, o, done):
            u = ua[:, f % 2, KA - 1:KA - 1 + S]
            if f < 2:
                got["ac", f] = act.do(nc.scalar.activation, u, o, ACT.Copy, after=[done])
                return [got["ac", f]]
            got["ua", f - 2] = dve.do(nc.vector.tensor_tensor, u, u, o, ALU.mult, after=[done, got["ac", f - 2]])
            return [got["ua", f - 2]]

        def conv(name, out_ap, src, w, taps, after, bias_ap=None):
            more = [ALU.add] if bias_ap is not None else []
            m = dve.do(nc.vector.tensor_scalar, out_ap, src[:, 0:S], w[:, 0:1], bias_ap, ALU.mult, *more, after=after)
            for j in range(1, taps):
                yield
                m = dve.do(nc.vector.scalar_tensor_tensor, out_ap, src[:, j:j + S], w[:, j:j + 1], out_ap, ALU.mult,
                           ALU.add, after=[m])
            got[name] = m
            yield

        def evac_ab(f, o, done):
            got["cat", f] = dve.do(nc.vector.tensor_tensor, cat[:, f, :], cat[:, f, :], o, ALU.mult,
                                   after=[done, got["conv_a", f]])
            return [got["cat", f]]

        rot_ct = Rotating([junk[:, :], gain_row[:, 0:S], gain_row[:, S:2 * S], C("dist")])

        def conv_b():
            for f in range(2):
                yield from conv(("conv_b", f), cat[:, 2 + f, :], gb[:, f, :], wb[:, f, :], KB,
                                [got["gb", f], got_wb, zero_gb], V("b_conv_b_2", f))

        def norm_b():
            c = [cat[:, 2 + f, :] for f in range(2)]
            scratch = [gb[:, f, 0:S] for f in range(2)]
            bank, bank_free, readers = linear_banks.take()
            pe.wait(*bank_free, got["conv_b", 0], got["conv_b", 1])
            for f in range(2):
                m = pe.do(nc.tensor.matmul, bank[:, :], C("ones"), c[f], start=(f == 0), stop=(f == 1))
            centred = [dve.do(nc.vector.scalar_tensor_tensor, c[f], bank[:, :], -1.0 / CW, c[f], ALU.mult, ALU.add,
                              after=[m]) for f in range(2)]
            readers += centred
            yield
            sq = [act.do(nc.scalar.activation, scratch[f], c[f], ACT.Square, after=[centred[f]]) for f in range(2)]
            yield
            bank, bank_free, readers = linear_banks.take()
            pe.wait(*bank_free, *sq)
            for f in range(2):
                m = pe.do(nc.tensor.matmul, bank[:, :], C("ones"), scratch[f], start=(f == 0), stop=(f == 1))
            m = act.do(nc.scalar.activation, scratch[0], bank[:, :], ACT.Ln, bias=eps_ln, scale=1.0 / CW, after=[m])
            readers.append(m)
            m = act.do(nc.scalar.activation, scratch[0], scratch[0], ACT.Exp, scale=-0.5, after=[m])
            yield
            k = [dve.do(nc.vector.tensor_tensor, c[f], c[f], scratch[0], ALU.mult, after=[m]) for f in range(2)]
            k = [dve.do(nc.vector.tensor_scalar, c[f], c[f], V("ln_b_g_2", f), V("ln_b_b_2", f), ALU.mult, ALU.add,
                        after=[k[f]]) for f in range(2)]
            yield
            for f in range(2):
                got["cat", 2 + f] = act.do(nc.scalar.activation, c[f], c[f], ACT.Silu, after=[k[f]])
            exp_ln_tables()
            yield

        widths = [S - P * j for j in range(TT)]
        units = [[(2, 0), (3, widths[2])], [(1, 0)], [(0, 0)]]
        n_units = len(units)
        u_width = [sum(widths[j] for j, _ in u) for u in units]
        u_start = [sum(u_width[:n]) for n in range(n_units)]
        start_of = {j: u_start[n] + c for n, u in enumerate(units) for j, c in u}
        total = sum(widths)
        at = sb("at", [total], ctx=scope)
        sp_hi = sb("sp_hi", [2, total], F32R, ctx=scope)
        sp_lo = sb("sp_lo", [2, total], F32R, ctx=scope)
        z_banks = Rotating(banks[2:8])
        y_bank, linear_bank = banks[1], banks[0]
        z_held, sp_marks, a_marks, y_free = {}, {}, {}, []
        at_free = [[] for _ in units]
        sp_free = [[], []]

        def softplus(h):
            f, r = h // 2, DH * (h % 2)
            for n, unit in enumerate(units):
                w = u_width[n]
                bank, bank_free, readers = z_banks.take()
                z_held[h, n] = bank, readers
                pe.wait(*bank_free, got["qk2", 2 * f], got["qk2", 2 * f + 1])
                for c, (j, at_col) in enumerate(unit):
                    m = pe.do(nc.tensor.matmul, bank[:, at_col:at_col + widths[j]],
                              k2[r:r + DH, f % 3, P * j:P * j + P], q2[r:r + DH, f % 3, P * j:S],
                              start=(c == 0), stop=False, skip_group_check=True)
                qk2_free[f] = [m]
                buf, t_free, t_readers = rot_ct.take()
                t = buf[:, 0:w]
                m = act.do(nc.scalar.activation, t, bank[:, 0:w], ACT.Abs, after=[m, *t_free])
                m = act.do(nc.scalar.activation, t, t, ACT.Exp, scale=-1.0, after=[m])
                m = act.do(nc.scalar.activation, t, t, ACT.Ln, bias=1.0, after=[m])
                yield
                z_read = dve.do(nc.vector.scalar_tensor_tensor, t, bank[:, 0:w], 0.0, t, ALU.max, ALU.add, after=[m])
                for j, at_col in unit:
                    d = t[:, at_col:at_col + P]
                    m = dve.do(nc.vector.tensor_tensor, d, d, C("before"), ALU.mult, after=[z_read])
                cs = slice(u_start[n], u_start[n] + w)
                hi, lo = sp_hi[:, h % 2, cs], sp_lo[:, h % 2, cs]
                m = dve.do(nc.vector.tensor_copy, hi, t, after=[m, *sp_free[h % 2]])
                marks = [dve.do(nc.vector.tensor_tensor, lo, t, hi.bitcast(F32), ALU.subtract, after=[m])]
                t_readers += marks
                sp_marks[h, n] = [z_read, *marks]
                yield

        def stick(h):
            f, r = h // 2, DH * (h % 2)
            sp = [sp_hi[:, h % 2, :], sp_lo[:, h % 2, :]]

            def values(n):
                pe.wait(a_marks[h, n])
                for j, _ in units[n]:
                    a = at[:, start_of[j]:start_of[j] + widths[j]]
                    m = pe.do(nc.tensor.matmul, y_bank[r:r + DH, P * j:S], v2[:, j, DH * h:DH * h + DH], a,
                              start=(n == 0 and j == units[0][0][0]), stop=(j == 0), skip_group_check=True,
                              after=[got["v2", j]])
                at_free[n] = [m]
                return m

            for n, unit in enumerate(units):
                bank, readers = z_held[h, n]
                pe.wait(*sp_marks[h, n], consts_r)
                for j, c0 in unit:
                    for i in range(j, TT):
                        c = c0 + P * (i - j)
                        for src in sp:
                            pe.run(nc.tensor.matmul, bank[:, c:c0 + widths[j]], (upper_r if i == j else ones_r)[:, :],
                                   src[:, start_of[i]:start_of[i] + widths[i]], start=False, stop=False,
                                   skip_group_check=True)
                    m = pe.do(nc.tensor.matmul, bank[:, c0:c0 + P], ident_r[:, :], block_r[:, :], start=False,
                              stop=True, skip_group_check=True)
                a = at[:, u_start[n]:u_start[n] + u_width[n]]
                a_marks[h, n] = act.do(nc.scalar.activation, a, bank[:, 0:u_width[n]], ACT.Exp,
                                       after=[m, *at_free[n]])
                readers += [a_marks[h, n], sp_marks[h, n][0]]
                yield
                if n == 1 and h % 2 == 0:
                    pe.wait(*y_free)
                if n:
                    values(n - 1)
                    yield
            sp_free[h % 2] = [m]
            m = values(n_units - 1)
            if h % 2:
                got["cat", 4 + f] = act.do(nc.scalar.activation, cat[:, 4 + f, :], y_bank[:, :], ACT.Copy, after=[m])
                y_free[:] = [got["cat", 4 + f]]
            yield

        finish(by_column_tiles("glu 2", h_hi, h_lo, ready_h, evac_glu, 4))
        on_vector = conv_b()

        def with_conv(gen, taps):
            for _ in gen:
                for _ in range(taps):
                    next(on_vector, None)
                yield

        finish(with_conv(by_row_tiles("v 2", h_hi, h_lo, ready_h, evac_v2, KD, halves=(0,)), 3))
        tiles_qk = by_column_tiles("qk 2", h_hi, h_lo, ready_h, evac_qk2, 8)
        for _ in range(4):
            next(tiles_qk)
            for _ in range(3):
                next(on_vector, None)

        def rest():
            for _ in range(2):
                yield next(tiles_qk)
            yield from by_column_tiles("ac ah 2", h_hi, h_lo, ready_h, evac_acah, 4)
            for _ in range(2):
                yield next(tiles_qk)
            for f in range(2):
                finish(conv(("conv_a", f), cat[:, f, :], ua[:, f, :], wa[:, f, :], KA,
                            [got["ua", f], got_wa, zero_ua]))
            yield from by_column_tiles("ab 2", h_hi, h_lo, ready_h, evac_ab, 2)

        linear_readers = list(linear_banks.readers)
        y_free += linear_readers[1]
        linear_banks.bufs, linear_banks.at, linear_banks.readers = [linear_bank], -1, [linear_readers[0]]
        z_banks.readers = core_banks.readers
        fills2 = rest()
        step = 0
        finish(softplus(0))
        unsplit = list(range(KD))

        def split_cat():
            for f in [f for f in unsplit if ("cat", f) in got]:
                unsplit.remove(f)
                h_ready[f] = split(h_hi[:, f, :], h_lo[:, f, :], cat[:, f, :], [got["cat", f], *h_free], dve)
                yield

        norm = norm_b()
        h_free = []
        for h in range(SBH):
            ahead = softplus(h + 1) if h + 1 < SBH else iter(())
            for _ in stick(h):
                next(ahead, None)
                if step in FILL2_STEPS:
                    if next(fills2, "done") == "done":
                        h_free = [(pe, pe.count)]
                elif h_free:
                    next(split_cat(), None)
                step += 1
                for _ in range(2):
                    if next(on_vector, "done") == "done" and step % 2:
                        next(norm, None)
                        break
            finish(ahead)
        finish(fills2, on_vector, norm)
        h_free = [(pe, pe.count)]
        linear_banks.bufs, linear_banks.at = banks[0:2], -1
        linear_banks.readers = [linear_banks.readers[0], list(y_free)]
        core_banks.readers[:] = z_banks.readers
        core_banks.at = -1
        finish(split_cat())
        cat_free = last()
        scope.close()

        with ExitStack() as scope:
            hs = sb("hs", [TT, D], ctx=scope)
            for lane in (dve, pool, act):
                lane.wait(*cat_free)

            def evac_res(n, i, o, done):
                a = x1[:, i, halves[n]]
                m = dve.do(nc.vector.tensor_tensor, a, a, o, ALU.add, after=[done])
                square(1, i, n, a, [m])
                if n == 1:
                    turn_behind(turns, i, [lambda: None,
                                           lambda: norm_tile(i, x1[:, i, :], hs[:, i, :], "g_ffn_2", [done], [m])])
                return [m]

            finish(by_row_tiles("out 2", h_hi, h_lo, ready_h, evac_res, KD, tile_by_tile=True))
        hs_free = last()

        got_gain = load_gain_row(T["g_final_2"], last(dve, act))
        out_rows = out.rearrange("a (i p) d -> (a p) i d", p=P)
        stored = Loads(sem("stored"))
        ends = []

        def then_2(acc, n, i, m):
            square(1, i, n, x1[:, i, halves[n]], [m])
            if n == 1:
                r, m = rstd(1, i)
                for half in halves:
                    k = dve.do(nc.vector.scalar_tensor_tensor, acc[:, i, half], x1[:, i, half], r, gain_row[:, half],
                               ALU.mult, ALU.mult, after=[m, got_gain])
                    ends.append(stored.start(sp, out_rows[:, i, half], acc[:, i, half], [k]))

        scope = ffn("2", FFN2_GROUPS, relu2, 1, hs_free, x1, then_2)
        sp.wait(ends[-1])
        scope.close()
        assert state["used"] == len(chunks)

        block = outer.enter_context(nc.Block())

        @block.sync
        def _(e):
            sp.write()

        @block.tensor
        def _(e):
            pe.write()

        @block.scalar
        def _(e):
            act.write()

        @block.vector
        def _(e):
            dve.write()

        @block.gpsimd
        def _(e):
            pool.write()


def columns_of(v):
    return np.reshape(v, (-1, P)).T


def block_diagonal(w):
    out = np.zeros((NG * DH, w.shape[1], NG * DH), w.dtype)
    for g in range(NG):
        out[DH * g:DH * g + DH, :, DH * g:DH * g + DH] = w
    return out.reshape(NG * DH, -1)


def lay_out(inputs):
    parts = []
    for _, name, row0, nk, c in plan():
        w = inputs[name][0]
        if name == "w_proj_nsa":
            w = w[NSA_ROWS]
        w = w[row0:row0 + P * nk][:, c]
        parts.append(np.ascontiguousarray(w.reshape(nk, P, len(c)).transpose(1, 0, 2)).reshape(-1))
    return np.concatenate(parts)


_DIRECT = ["x", "gla_w_alpha2", "norm_mix_post",
           "norm_ffn_post", "g_final_2"]


def kernel(**inputs):
    import concourse.bacc as _bacc
    from concourse.bass_utils import run_bass_kernel_spmd as _run

    inputs = {k: np.asarray(v) for k, v in inputs.items()}
    nc = _bacc.Bacc("TRN2", target_bir_lowering=False, num_devices=1)
    arrays = {}

    def give(name, a):
        a = np.ascontiguousarray(a)
        arrays[f"in_{name}"] = a
        return nc.dram_tensor(f"in_{name}", a.shape, mybir.dt.from_np(a.dtype), kind="ExternalInput").ap()

    T = {name: give(name, inputs[name]) for name in _DIRECT}
    for n in "kv":
        T[f"pe_{n}"] = give(f"pe_{n}", np.concatenate([inputs[f"nsa_cmp_pe_{n}"][0].T] * NG))
    for n in "ab":
        w = inputs[f"w_conv_{n}_2"][0]
        T[f"taps_{n}"] = give(f"taps_{n}", w.reshape(len(w), 2, P).transpose(2, 1, 0).reshape(P, -1))
    for n in "kv":
        w = inputs[f"nsa_cmp_w1_{n}"][0].reshape(CL, DH, DH).transpose(1, 0, 2)
        T[f"w1_{n}"] = give(f"w1_{n}", block_diagonal(w))
        T[f"w2_{n}"] = give(f"w2_{n}", block_diagonal(inputs[f"nsa_cmp_w2_{n}"][0][:, None, :]))
    wstream = give("wstream", lay_out(inputs))
    vectors = give("vectors", np.concatenate([columns_of(inputs[n]) for n, _ in _vec], axis=1))
    consts = give("constants", constants())
    out = nc.dram_tensor("out", (1, S, D), F32, kind="ExternalOutput").ap()
    program(nc, T, wstream, vectors, consts, out)
    r = _run(nc, [arrays], core_ids=[0])
    return r.results[0]["out"]
```
